# Optimizing a Trainium2 kernel written in Bass

```python
import math
import jax, jax.numpy as jnp
from jax import lax
import numpy as np

D_MODEL = 1024
BATCH = 1
SEQ = 256
DEPTH = 2

N_A_LAYERS = DEPTH // 2
N_B_LAYERS = DEPTH - N_A_LAYERS
MIX_W = D_MODEL
MEM_LEN = 256
MEM_HEADS = 4
MEM_HEAD_DIM = 64
MEM_W = MEM_HEADS * MEM_HEAD_DIM
SEQ_MIX_W = MIX_W - MEM_W
HGRN_EXPAND = 128
HGRN_HEADS = SEQ_MIX_W // HGRN_EXPAND
HGRN_DK = HGRN_EXPAND
HGRN_DV = SEQ_MIX_W // HGRN_HEADS
HGRN_CHUNK = 64
SB_HEAD_DIM = 64
SB_HEADS = SEQ_MIX_W // SB_HEAD_DIM
SB_BLOCK = 128
A_IN_W = 4 * SEQ_MIX_W + MEM_W
B_IN_W = SEQ_MIX_W + MEM_W
N_GROUPS = 4
EXPERTS_PER_GROUP = 4
N_EXPERTS = N_GROUPS * EXPERTS_PER_GROUP
TOP_K_IN_GROUP = 2
D_EXPERT = 256
DEEPNORM_ALPHA = (2 * DEPTH) ** 0.25
DEEPNORM_BETA = (8 * DEPTH) ** -0.25
LN_EPS = 1e-5
RMS_EPS = 1e-6


def layer_norm(x, g, b):
    xf = x.astype(jnp.float32)
    mu = jnp.mean(xf, axis=-1, keepdims=True)
    var = jnp.mean(jnp.square(xf - mu), axis=-1, keepdims=True)
    y = (xf - mu) * lax.rsqrt(var + LN_EPS) * g.astype(jnp.float32) + b.astype(jnp.float32)
    return y.astype(x.dtype)

def post_norm(x, y, g, b):
    return layer_norm(DEEPNORM_ALPHA * x + y.astype(x.dtype), g, b)

def gla_chunkwise(q, k, v, logf):
    B, S, H, dk = q.shape
    dv = v.shape[-1]
    nc = S // HGRN_CHUNK

    def to_chunks(t):
        return t.reshape(B, nc, HGRN_CHUNK, H, t.shape[-1]).transpose(1, 0, 3, 2, 4)

    qc, kc, vc = to_chunks(q), to_chunks(k), to_chunks(v)
    G = jnp.cumsum(to_chunks(logf), axis=3)
    incl = jnp.tril(jnp.ones((HGRN_CHUNK, HGRN_CHUNK), dtype=bool))

    def step(state, inp):
        q_, k_, v_, G_ = inp
        diff = G_[:, :, :, None, :] - G_[:, :, None, :, :]
        decay = jnp.exp(jnp.where(incl[:, :, None], diff, -jnp.inf))
        scores = jnp.einsum('bhtd,bhsd,bhtsd->bhts', q_, k_, decay)
        out = (jnp.einsum('bhts,bhse->bhte', scores, v_)
               + jnp.einsum('bhtd,bhde->bhte', q_ * jnp.exp(G_), state))
        g_last = G_[:, :, -1]
        state = (jnp.exp(g_last)[..., None] * state
                 + jnp.einsum('bhsd,bhse->bhde', k_ * jnp.exp(g_last[:, :, None] - G_), v_))
        return state, out

    s0 = jnp.zeros((B, H, dk, dv), jnp.float32)
    _, out = lax.scan(step, s0, (qc, kc, vc, G))
    return out.transpose(1, 0, 3, 2, 4).reshape(B, S, H, dv)

def hgrn2_mix(q, f_raw, i_in, g, lb, gnorm):
    B, S, _ = q.shape
    qh = (jax.nn.silu(q.astype(jnp.float32)) * HGRN_DK ** -0.5).reshape(B, S, HGRN_HEADS, HGRN_DK)
    lbf = lb.astype(jnp.float32)
    logf = jnp.logaddexp(jnp.log(lbf), jnp.log1p(-lbf) + jax.nn.log_sigmoid(f_raw.astype(jnp.float32)))
    logf = logf.reshape(B, S, HGRN_HEADS, HGRN_DK)
    kh = -jnp.expm1(logf)
    vh = i_in.astype(jnp.float32).reshape(B, S, HGRN_HEADS, HGRN_DV)
    o = gla_chunkwise(qh, kh, vh, logf)
    o = o * lax.rsqrt(jnp.mean(jnp.square(o), axis=-1, keepdims=True) + RMS_EPS)
    o = o * gnorm.astype(jnp.float32).reshape(HGRN_HEADS, HGRN_DV)
    o = o.reshape(B, S, SEQ_MIX_W) * jax.nn.silu(g.astype(jnp.float32))
    return o

def stick_breaking_attention(q, k, v):
    B, S, _ = q.shape
    qh = q.astype(jnp.float32).reshape(B, S, SB_HEADS, SB_HEAD_DIM).transpose(0, 2, 1, 3)
    scale = 1.0 / math.sqrt(SB_HEAD_DIM)
    outs = []
    for blk in range(S // SB_BLOCK):
        start, end = blk * SB_BLOCK, (blk + 1) * SB_BLOCK
        qb = qh[:, :, start:end]
        kb, vb = k[:, :, :end], v[:, :, :end]
        z = jnp.einsum('bhtd,bhsd->bhts', qb, kb) * scale
        t_pos = start + jnp.arange(SB_BLOCK)
        s_pos = jnp.arange(end)
        mask = s_pos[None, :] < t_pos[:, None]
        neg_log_1m_beta = jnp.where(mask, jax.nn.softplus(z), 0.0)
        rest = lax.cumsum(neg_log_1m_beta, axis=3, reverse=True) - neg_log_1m_beta
        log_a = jax.nn.log_sigmoid(z) - rest
        a = jnp.where(mask, jnp.exp(log_a), 0.0)
        outs.append(jnp.einsum('bhts,bhsd->bhtd', a, vb))
    o = jnp.concatenate(outs, axis=2)
    return o.transpose(0, 2, 1, 3).reshape(B, S, SEQ_MIX_W)

def memory_attention(qm, mem_k, mem_v):
    B, S, _ = qm.shape
    qh = qm.astype(jnp.float32).reshape(B, S, MEM_HEADS, MEM_HEAD_DIM)
    scores = jnp.einsum('bthd,bmhd->bhtm', qh, mem_k.astype(jnp.float32)) / math.sqrt(MEM_HEAD_DIM)
    p = jax.nn.softmax(scores, axis=-1)
    o = jnp.einsum('bhtm,bmhd->bthd', p, mem_v.astype(jnp.float32))
    return o.reshape(B, S, MEM_W)

def hier_moe(x, w_group, b_group, w_router, b_router, w_gate, w_up, w_down):
    B, S, D = x.shape
    xf = x.reshape(B * S, D)
    T = xf.shape[0]
    probs_g = jax.nn.softmax((xf @ w_group + b_group).astype(jnp.float32), axis=-1)
    p_top, g_idx = lax.top_k(probs_g, 1)
    logits_e = (xf @ w_router + b_router).astype(jnp.float32).reshape(T, N_GROUPS, EXPERTS_PER_GROUP)
    in_group = jnp.take_along_axis(logits_e, g_idx[:, :, None], axis=1)[:, 0]
    probs_in = jax.nn.softmax(in_group, axis=-1)
    w_top, e_local = lax.top_k(probs_in, TOP_K_IN_GROUP)
    w_top = w_top / jnp.sum(w_top, axis=-1, keepdims=True)
    ids = g_idx * EXPERTS_PER_GROUP + e_local
    gates = jnp.einsum('tk,tke->te', p_top * w_top, jax.nn.one_hot(ids, N_EXPERTS, dtype=jnp.float32))
    h = jax.nn.silu(jnp.einsum('td,edf->tef', xf, w_gate)) * jnp.einsum('td,edf->tef', xf, w_up)
    y = jnp.einsum('tef,efd->td', h * gates[:, :, None].astype(h.dtype), w_down)
    return y.reshape(B, S, D)

def first_inputs(seed: int = 0) -> dict:
    key = jax.random.key(seed)
    ks = iter(jax.random.split(key, 40))

    def nrm(shape, scale):
        return jax.random.normal(next(ks), shape, jnp.float32) * scale

    d_s = D_MODEL ** -0.5
    x = nrm((BATCH, SEQ, D_MODEL), 1.0)
    mem = nrm((BATCH, MEM_LEN, D_MODEL), 1.0)
    a_w_in = jnp.concatenate([
        nrm((N_A_LAYERS, D_MODEL, SEQ_MIX_W), d_s),
        nrm((N_A_LAYERS, D_MODEL, SEQ_MIX_W), d_s),
        nrm((N_A_LAYERS, D_MODEL, SEQ_MIX_W), d_s * DEEPNORM_BETA),
        nrm((N_A_LAYERS, D_MODEL, SEQ_MIX_W), d_s),
        nrm((N_A_LAYERS, D_MODEL, MEM_W), d_s),
    ], axis=-1)
    a_lower_bounds = nrm((N_A_LAYERS, SEQ_MIX_W), 0.1)
    a_gnorm = 1.0 + nrm((N_A_LAYERS, SEQ_MIX_W), 0.02)
    b_w_in = nrm((N_B_LAYERS, D_MODEL, B_IN_W), d_s)
    w_kv_shared = jnp.concatenate([nrm((D_MODEL, SEQ_MIX_W), d_s),
                                   nrm((D_MODEL, SEQ_MIX_W), d_s * DEEPNORM_BETA)], axis=-1)
    w_mem_kv = jnp.concatenate([nrm((DEPTH, D_MODEL, MEM_W), d_s),
                                nrm((DEPTH, D_MODEL, MEM_W), d_s * DEEPNORM_BETA)], axis=-1)
    w_o = nrm((DEPTH, MIX_W, D_MODEL), MIX_W ** -0.5 * DEEPNORM_BETA)
    ln_mix_g = 1.0 + nrm((DEPTH, D_MODEL), 0.02)
    ln_mix_b = nrm((DEPTH, D_MODEL), 0.02)
    ln_ffn_g = 1.0 + nrm((DEPTH, D_MODEL), 0.02)
    ln_ffn_b = nrm((DEPTH, D_MODEL), 0.02)
    w_group = nrm((DEPTH, D_MODEL, N_GROUPS), d_s)
    b_group = nrm((DEPTH, N_GROUPS), 0.01)
    w_router = nrm((DEPTH, D_MODEL, N_EXPERTS), d_s)
    b_router = nrm((DEPTH, N_EXPERTS), 0.01)
    w_gate = nrm((DEPTH, N_EXPERTS, D_MODEL, D_EXPERT), d_s)
    w_up = nrm((DEPTH, N_EXPERTS, D_MODEL, D_EXPERT), d_s)
    w_down = nrm((DEPTH, N_EXPERTS, D_EXPERT, D_MODEL), D_EXPERT ** -0.5 * DEEPNORM_BETA)
    return {"x": x, "mem": mem, "a_w_in": a_w_in, "a_lower_bounds": a_lower_bounds,
            "a_gnorm": a_gnorm, "b_w_in": b_w_in, "w_kv_shared": w_kv_shared,
            "w_mem_kv": w_mem_kv, "w_o": w_o, "ln_mix_g": ln_mix_g, "ln_mix_b": ln_mix_b,
            "ln_ffn_g": ln_ffn_g, "ln_ffn_b": ln_ffn_b, "w_group": w_group, "b_group": b_group,
            "w_router": w_router, "b_router": b_router, "w_gate": w_gate, "w_up": w_up,
            "w_down": w_down}

def first_block(x, mem, a_w_in, a_lower_bounds, a_gnorm, b_w_in, w_kv_shared, w_mem_kv, w_o,
              ln_mix_g, ln_mix_b, ln_ffn_g, ln_ffn_b, w_group, b_group, w_router, b_router,
              w_gate, w_up, w_down):
    B, S, _ = x.shape
    lb_all = jnp.cumsum(jax.nn.softmax(a_lower_bounds.astype(jnp.float32), axis=0), axis=0)
    lb_all = lb_all - lb_all[0]
    shared_k = None
    shared_v = None
    for layer in range(DEPTH):
        mem_kv = mem @ w_mem_kv[layer]
        mem_k = mem_kv[..., :MEM_W].reshape(B, MEM_LEN, MEM_HEADS, MEM_HEAD_DIM)
        mem_v = mem_kv[..., MEM_W:].reshape(B, MEM_LEN, MEM_HEADS, MEM_HEAD_DIM)
        if layer < N_A_LAYERS:
            h = x @ a_w_in[layer]
            q, f_raw, i_in, g, qm = jnp.split(
                h, [SEQ_MIX_W, 2 * SEQ_MIX_W, 3 * SEQ_MIX_W, 4 * SEQ_MIX_W], axis=-1)
            seq_out = hgrn2_mix(q, f_raw, i_in, g, lb_all[layer], a_gnorm[layer])
        else:
            if layer == N_A_LAYERS:
                kv = x @ w_kv_shared
                shared_k = kv[..., :SEQ_MIX_W].astype(jnp.float32).reshape(
                    B, S, SB_HEADS, SB_HEAD_DIM).transpose(0, 2, 1, 3)
                shared_v = kv[..., SEQ_MIX_W:].astype(jnp.float32).reshape(
                    B, S, SB_HEADS, SB_HEAD_DIM).transpose(0, 2, 1, 3)
            h = x @ b_w_in[layer - N_A_LAYERS]
            q, qm = jnp.split(h, [SEQ_MIX_W], axis=-1)
            seq_out = stick_breaking_attention(q, shared_k, shared_v)
        mem_out = memory_attention(qm, mem_k, mem_v)
        mixed = jnp.concatenate([seq_out.astype(x.dtype), mem_out.astype(x.dtype)], axis=-1)
        x = post_norm(x, mixed @ w_o[layer], ln_mix_g[layer], ln_mix_b[layer])
        moe_out = hier_moe(x, w_group[layer], b_group[layer], w_router[layer], b_router[layer],
                           w_gate[layer], w_up[layer], w_down[layer])
        x = post_norm(x, moe_out, ln_ffn_g[layer], ln_ffn_b[layer])
    return x


DEPTH_2 = 1

N_MIXERS = 2
N_ATTN_LAYERS = (DEPTH_2 + N_MIXERS - 1) // N_MIXERS
N_SSM_LAYERS = DEPTH_2 // N_MIXERS

ATTN_HEAD_DIM = 64
ATTN_HEADS = D_MODEL // ATTN_HEAD_DIM
Q_BLOCK = 128
SSM_EXPAND = 2
SSM_D_INNER = SSM_EXPAND * D_MODEL
SSM_HEAD_DIM = 64
SSM_HEADS = SSM_D_INNER // SSM_HEAD_DIM
SSM_GROUPS = 8
SSM_STATE = 128
SSM_CONV = 4
SSM_CHUNK = 128
SSM_XBC = SSM_D_INNER + 2 * SSM_GROUPS * SSM_STATE
FFN_DIM = 2816
FFN_CONV = 3
PLE_DIM = 256

RMS_EPS_2 = 1e-5
DEEPNORM_ALPHA_2 = (2 * DEPTH_2) ** 0.25
DEEPNORM_BETA_2 = (8 * DEPTH_2) ** -0.25


def layer_norm_2(x, g, b):
    xf = x.astype(jnp.float32)
    mu = jnp.mean(xf, axis=-1, keepdims=True)
    var = jnp.mean(jnp.square(xf - mu), axis=-1, keepdims=True)
    return ((xf - mu) * lax.rsqrt(var + LN_EPS) * g + b).astype(x.dtype)

def causal_dwconv(u, w, b):
    K = w.shape[0]
    S = u.shape[1]
    up = jnp.pad(u, ((0, 0), (K - 1, 0), (0, 0)))
    out = b
    for k in range(K):
        out = out + up[:, k:k + S] * w[k]
    return out

def fox_mixer(x, w_in, b_f, w_out):
    Bsz, S, _ = x.shape
    H, Dh = ATTN_HEADS, ATTN_HEAD_DIM
    proj = x @ w_in
    q, k, v, f_logit = jnp.split(proj, [D_MODEL, 2 * D_MODEL, 3 * D_MODEL], axis=-1)
    q = q.reshape(Bsz, S, H, Dh).transpose(0, 2, 1, 3)
    k = k.reshape(Bsz, S, H, Dh).transpose(0, 2, 1, 3)
    v = v.reshape(Bsz, S, H, Dh).transpose(0, 2, 1, 3)
    log_f = jax.nn.log_sigmoid(f_logit.astype(jnp.float32) + b_f)
    c = jnp.cumsum(log_f, axis=1).transpose(0, 2, 1)
    nb = S // Q_BLOCK
    qb = q.reshape(Bsz, H, nb, Q_BLOCK, Dh).transpose(2, 0, 1, 3, 4)
    cqb = c.reshape(Bsz, H, nb, Q_BLOCK).transpose(2, 0, 1, 3)
    kpos = jnp.arange(S)
    scale = 1.0 / math.sqrt(Dh)

    def block(args):
        qi, cqi, bi = args
        s = jnp.einsum('bhqd,bhkd->bhqk', qi, k).astype(jnp.float32) * scale
        s = s + cqi[..., None] - c[:, :, None, :]
        qpos = bi * Q_BLOCK + jnp.arange(Q_BLOCK)
        s = jnp.where(kpos[None, :] <= qpos[:, None], s, -jnp.inf)
        pr = jax.nn.softmax(s, axis=-1)
        return jnp.einsum('bhqk,bhkd->bhqd', pr.astype(v.dtype), v)

    o = lax.map(block, (qb, cqb, jnp.arange(nb)))
    o = o.transpose(1, 0, 3, 2, 4).reshape(Bsz, S, D_MODEL)
    return o @ w_out

def ssd_scan(xh, dt, A, Bm, Cm):
    Bsz, S = xh.shape[0], xh.shape[1]
    G, R, P, N, Q = SSM_GROUPS, SSM_HEADS // SSM_GROUPS, SSM_HEAD_DIM, SSM_STATE, SSM_CHUNK
    nc = S // Q

    def to_chunks(t):
        return jnp.moveaxis(t.reshape((Bsz, nc, Q) + t.shape[2:]), 1, 0)

    xc = to_chunks(xh.reshape(Bsz, S, G, R, P))
    dtc = to_chunks(dt.reshape(Bsz, S, G, R))
    Bc = to_chunks(Bm)
    Cc = to_chunks(Cm)
    A_g = A.reshape(G, R)
    tri = jnp.tril(jnp.ones((Q, Q), dtype=bool))[None, :, :, None, None]

    def step(state, inp):
        x_, dt_, B_, C_ = inp
        acum = jnp.cumsum(dt_ * A_g, axis=1)
        seg = acum[:, :, None] - acum[:, None, :]
        L = jnp.exp(jnp.where(tri, seg, -jnp.inf))
        CB = jnp.einsum('btgn,bsgn->btsg', C_, B_)
        y_intra = jnp.einsum('btsg,btsgr,bsgr,bsgrp->btgrp', CB, L, dt_, x_)
        y_inter = jnp.einsum('btgn,bgrpn,btgr->btgrp', C_, state, jnp.exp(acum))
        w_end = jnp.exp(acum[:, -1:] - acum) * dt_
        new_state = state * jnp.exp(acum[:, -1])[..., None, None] + \
            jnp.einsum('bsgn,bsgr,bsgrp->bgrpn', B_, w_end, x_)
        return new_state, (y_intra + y_inter).astype(jnp.float32)

    state0 = jnp.zeros((Bsz, G, R, P, N), jnp.float32)
    _, y = lax.scan(step, state0, (xc, dtc, Bc, Cc))
    return jnp.moveaxis(y, 0, 1).reshape(Bsz, S, SSM_HEADS, P)

def ssd_mixer(x, w_in, conv_w, conv_b, dt_bias, A_log, D_skip, norm_w, w_out):
    Bsz, S, _ = x.shape
    GN = SSM_GROUPS * SSM_STATE
    proj = x @ w_in
    z, xBC, dt_raw = jnp.split(proj, [SSM_D_INNER, SSM_D_INNER + SSM_XBC], axis=-1)
    xBC = jax.nn.silu(causal_dwconv(xBC, conv_w, conv_b))
    xs, Bm, Cm = jnp.split(xBC, [SSM_D_INNER, SSM_D_INNER + GN], axis=-1)
    dt = jax.nn.softplus(dt_raw.astype(jnp.float32) + dt_bias)
    A = -jnp.exp(A_log.astype(jnp.float32))
    xh = xs.reshape(Bsz, S, SSM_HEADS, SSM_HEAD_DIM)
    y = ssd_scan(xh, dt, A,
                 Bm.reshape(Bsz, S, SSM_GROUPS, SSM_STATE),
                 Cm.reshape(Bsz, S, SSM_GROUPS, SSM_STATE))
    y = y + D_skip[:, None] * xh
    y = y.reshape(Bsz, S, SSM_D_INNER) * jax.nn.silu(z.astype(jnp.float32))
    yg = y.reshape(Bsz, S, SSM_GROUPS, SSM_D_INNER // SSM_GROUPS)
    yg = yg * lax.rsqrt(jnp.mean(jnp.square(yg), axis=-1, keepdims=True) + RMS_EPS_2)
    y = yg.reshape(Bsz, S, SSM_D_INNER) * norm_w
    return y.astype(x.dtype) @ w_out

def conv_ffn(x, w_up, conv_w, conv_b, w_down):
    u, g = jnp.split(x @ w_up, [FFN_DIM], axis=-1)
    g = causal_dwconv(g, conv_w, conv_b)
    return (jax.nn.gelu(g, approximate=False) * u) @ w_down

def second_inputs(seed: int = 0) -> dict:
    key = jax.random.key(seed)
    ks = iter(jax.random.split(key, 40))

    def nrm(shape, scale):
        return jax.random.normal(next(ks), shape, jnp.float32) * scale

    D, H = D_MODEL, ATTN_HEADS
    NA, NB = N_ATTN_LAYERS, N_SSM_LAYERS
    beta = DEEPNORM_BETA_2
    x = nrm((BATCH, SEQ, D), 1.0)
    p = nrm((DEPTH_2, BATCH, SEQ, PLE_DIM), 1.0)
    attn_w_in = nrm((NA, D, 3 * D + H), D ** -0.5)
    attn_w_in = attn_w_in.at[:, :, 2 * D:3 * D].multiply(beta)
    attn_b_f = jax.random.uniform(next(ks), (NA, H), jnp.float32, 1.0, 6.0)
    attn_w_out = nrm((NA, D, D), beta * D ** -0.5)
    ssm_in_dim = 2 * SSM_D_INNER + 2 * SSM_GROUPS * SSM_STATE + SSM_HEADS
    ssm_w_in = nrm((NB, D, ssm_in_dim), D ** -0.5)
    ssm_conv_w = nrm((NB, SSM_CONV, SSM_XBC), SSM_CONV ** -0.5)
    ssm_conv_b = nrm((NB, SSM_XBC), 0.02)
    dt0 = jnp.exp(jax.random.uniform(next(ks), (NB, SSM_HEADS), jnp.float32,
                                     math.log(1e-3), math.log(1e-1)))
    ssm_dt_bias = dt0 + jnp.log(-jnp.expm1(-dt0))
    ssm_A_log = jnp.log(jax.random.uniform(next(ks), (NB, SSM_HEADS), jnp.float32, 1.0, 16.0))
    ssm_D = 1.0 + nrm((NB, SSM_HEADS), 0.1)
    ssm_norm_w = 1.0 + nrm((NB, SSM_D_INNER), 0.05)
    ssm_w_out = nrm((NB, SSM_D_INNER, D), beta * SSM_D_INNER ** -0.5)
    ln_mix_g = 1.0 + nrm((DEPTH_2, D), 0.05)
    ln_mix_b = nrm((DEPTH_2, D), 0.02)
    ffn_w_up = nrm((DEPTH_2, D, 2 * FFN_DIM), D ** -0.5)
    ffn_conv_w = nrm((DEPTH_2, FFN_CONV, FFN_DIM), FFN_CONV ** -0.5)
    ffn_conv_b = nrm((DEPTH_2, FFN_DIM), 0.02)
    ffn_w_down = nrm((DEPTH_2, FFN_DIM, D), beta * FFN_DIM ** -0.5)
    ln_ffn_g = 1.0 + nrm((DEPTH_2, D), 0.05)
    ln_ffn_b = nrm((DEPTH_2, D), 0.02)
    ple_w_proj = nrm((DEPTH_2, PLE_DIM, D), beta * PLE_DIM ** -0.5)
    ple_w_gate = nrm((DEPTH_2, D, D), D ** -0.5)
    ple_b_gate = nrm((DEPTH_2, D), 0.02)
    return {"x": x, "p": p,
            "attn_w_in": attn_w_in, "attn_b_f": attn_b_f, "attn_w_out": attn_w_out,
            "ssm_w_in": ssm_w_in, "ssm_conv_w": ssm_conv_w, "ssm_conv_b": ssm_conv_b,
            "ssm_dt_bias": ssm_dt_bias, "ssm_A_log": ssm_A_log, "ssm_D": ssm_D,
            "ssm_norm_w": ssm_norm_w, "ssm_w_out": ssm_w_out,
            "ln_mix_g": ln_mix_g, "ln_mix_b": ln_mix_b,
            "ffn_w_up": ffn_w_up, "ffn_conv_w": ffn_conv_w, "ffn_conv_b": ffn_conv_b,
            "ffn_w_down": ffn_w_down, "ln_ffn_g": ln_ffn_g, "ln_ffn_b": ln_ffn_b,
            "ple_w_proj": ple_w_proj, "ple_w_gate": ple_w_gate, "ple_b_gate": ple_b_gate}

def second_block(x, p, attn_w_in, attn_b_f, attn_w_out, ssm_w_in, ssm_conv_w, ssm_conv_b,
              ssm_dt_bias, ssm_A_log, ssm_D, ssm_norm_w, ssm_w_out, ln_mix_g, ln_mix_b,
              ffn_w_up, ffn_conv_w, ffn_conv_b, ffn_w_down, ln_ffn_g, ln_ffn_b,
              ple_w_proj, ple_w_gate, ple_b_gate):
    for i in range(DEPTH_2):
        j = i // N_MIXERS
        if i % N_MIXERS == 0:
            mix = fox_mixer(x, attn_w_in[j], attn_b_f[j], attn_w_out[j])
        else:
            mix = ssd_mixer(x, ssm_w_in[j], ssm_conv_w[j], ssm_conv_b[j], ssm_dt_bias[j],
                            ssm_A_log[j], ssm_D[j], ssm_norm_w[j], ssm_w_out[j])
        x = layer_norm_2(DEEPNORM_ALPHA_2 * x + mix, ln_mix_g[i], ln_mix_b[i])
        ffn = conv_ffn(x, ffn_w_up[i], ffn_conv_w[i], ffn_conv_b[i], ffn_w_down[i])
        x = layer_norm_2(DEEPNORM_ALPHA_2 * x + ffn, ln_ffn_g[i], ln_ffn_b[i])
        gate = jax.nn.sigmoid(x @ ple_w_gate[i] + ple_b_gate[i])
        x = x + gate * (p[i] @ ple_w_proj[i])
    return x


def setup_inputs(seed=0):
    out = dict(first_inputs(seed))
    for name, value in second_inputs(seed + 1).items():
        if name != "x":
            out[name + "_2"] = value
    return out


def reference(
    x, mem, a_w_in, a_lower_bounds, a_gnorm, b_w_in, w_kv_shared, w_mem_kv, w_o, ln_mix_g,
    ln_mix_b, ln_ffn_g, ln_ffn_b, w_group, b_group, w_router, b_router, w_gate, w_up, w_down,
    p_2, attn_w_in_2, attn_b_f_2, attn_w_out_2, ssm_w_in_2, ssm_conv_w_2, ssm_conv_b_2,
    ssm_dt_bias_2, ssm_A_log_2, ssm_D_2, ssm_norm_w_2, ssm_w_out_2, ln_mix_g_2, ln_mix_b_2,
    ffn_w_up_2, ffn_conv_w_2, ffn_conv_b_2, ffn_w_down_2, ln_ffn_g_2, ln_ffn_b_2, ple_w_proj_2,
    ple_w_gate_2, ple_b_gate_2,
):
    x = first_block(
        x, mem, a_w_in, a_lower_bounds, a_gnorm, b_w_in, w_kv_shared, w_mem_kv, w_o, ln_mix_g,
        ln_mix_b, ln_ffn_g, ln_ffn_b, w_group, b_group, w_router, b_router, w_gate, w_up,
        w_down,
    )
    return second_block(
        x, p_2, attn_w_in_2, attn_b_f_2, attn_w_out_2, ssm_w_in_2, ssm_conv_w_2, ssm_conv_b_2,
        ssm_dt_bias_2, ssm_A_log_2, ssm_D_2, ssm_norm_w_2, ssm_w_out_2, ln_mix_g_2, ln_mix_b_2,
        ffn_w_up_2, ffn_conv_w_2, ffn_conv_b_2, ffn_w_down_2, ln_ffn_g_2, ln_ffn_b_2,
        ple_w_proj_2, ple_w_gate_2, ple_b_gate_2,
    )


_drawn_inputs = setup_inputs


def setup_inputs(seed=0):
    import zlib

    import numpy as np

    out = dict(_drawn_inputs(seed))
    spreads = {}
    factors = {'mem': 3.185,
     'a_gnorm': 8.0,
     'w_mem_kv': 3.141,
     'b_group': 8.0,
     'b_router': 8.0,
     'ln_mix_b_2': 2.844,
     'ffn_conv_b_2': 8.0,
     'ln_ffn_b_2': 2.956,
     'ple_b_gate_2': 24.108}
    for name, (base, spread) in spreads.items():
        noise = np.random.default_rng([zlib.crc32(name.encode()), seed]).standard_normal(out[name].shape)
        drawn = base * np.exp(spread * noise) if base else spread * noise
        out[name] = __import__('jax').numpy.asarray(drawn.astype(out[name].dtype))
    for name, factor in factors.items():
        out[name] = (out[name] * factor).astype(out[name].dtype)
    return out
```

```python
from contextlib import ExitStack

import concourse.bass as bass
from concourse import mybir

F32 = mybir.dt.float32
F32R = mybir.dt.float32r
I32 = mybir.dt.int32
I8 = mybir.dt.int8
ALU = mybir.AluOpType
ACT = mybir.ActivationFunctionType
AX = mybir.AxisListType.X

P = 128
D = 1024
T = 256
TB = T // P
KC = D // P
SEQ_W = 768
MEM_W = 256
HG_HEADS = 6
SB_HEADS = 12
FOX_HEADS = 16
GROUPS = 4
PER_GROUP = 4
EXPERTS = GROUPS * PER_GROUP
FFN = 2816
FC = FFN // P
ALPHA = 4 ** 0.25
ALPHA_2 = 2 ** 0.25
LN_EPS = 1e-5
RMS_EPS = 1e-6
HG_SCALE = 128 ** -0.5
HD_SCALE = 0.125
NEG = -1e30
HALF = 2048
RING = 4
AHEAD = 3
LEVELS = (64, 32, 16, 8, 4, 2, 1)
STEPS = len(LEVELS) + 2

_sizes = [("A_F", 3), ("A_Q", 3), ("A_IG", 6), ("A_QM", 1), ("MK0", 1), ("MV0", 1), ("MK1", 1), ("MV1", 1),
          ("O0", 4), ("E0", 48), ("B_K", 3), ("B_V", 3), ("B_Q", 3), ("B_QM", 1), ("O1", 4), ("E1", 48),
          ("C_Q", 4), ("C_K", 4), ("C_V", 4), ("O2", 4), ("UP", 22), ("DN", 11), ("PP", 1), ("PG", 4)]
AT = {}
_n = 0
for _name, _k in _sizes:
    AT[_name] = _n
    _n += _k
HALVES = _n
GROUP_ORDER = [("G", 0, 0), ("G", 0, 1), ("G", 1, 0), ("G", 1, 1), ("G", 2, 0), ("G", 2, 1), ("D", 0, 0),
               ("G", 3, 0), ("G", 3, 1), ("D", 1, 0), ("D", 2, 0), ("D", 3, 0)]
G_AT = {0: 0, 1: 2, 2: 4, 3: 7}
D_AT = {0: 6, 1: 9, 2: 10, 3: 11}
PER_G = len(GROUP_ORDER)

UNITS = {}
_order = []


def _unit(name, h, n, banks, who):
    UNITS[name] = (h, n, banks, who)
    _order.append(name)


for _j in range(3):
    _unit(f"A_F{_j}", AT["A_F"] + _j, 1, [_j], "v")
for _j in range(3):
    _unit(f"A_Q{_j}", AT["A_Q"] + _j, 1, [(3 + _j) % 4], "a")
for _j, _w in enumerate(("v", "av", "a")):
    _unit(f"A_IG{_j}", AT["A_IG"] + 2 * _j, 2, [[2, 3], [0, 1], [2, 3]][_j], _w)
_unit("A_QM", AT["A_QM"], 1, [0], "a")
for _l in range(2):
    _unit(f"MK{_l}", AT[f"MK{_l}"], 1, [1 if _l == 0 else 3], "a")
    _unit(f"MV{_l}", AT[f"MV{_l}"], 1, [2 if _l == 0 else 0], "v")
_unit("O00", AT["O0"], 2, [0, 1], "v")
_unit("O01", AT["O0"] + 2, 2, [2, 3], "v")
for _j in range(3):
    _unit(f"B_K{_j}", AT["B_K"] + _j, 1, [_j], "ava"[_j])
_unit("B_V0", AT["B_V"], 2, [0, 1], "av")
_unit("B_V1", AT["B_V"] + 2, 1, [2], "v")
for _j in range(3):
    _unit(f"B_Q{_j}", AT["B_Q"] + _j, 1, [[3, 0, 1][_j]], "ava"[_j])
_unit("B_QM", AT["B_QM"], 1, [2], "v")
_unit("O10", AT["O1"], 2, [0, 1], "v")
_unit("O11", AT["O1"] + 2, 2, [2, 3], "v")
for _j in range(4):
    _unit(f"C_Q{_j}", AT["C_Q"] + _j, 1, [_j], "avav"[_j])
for _j in range(4):
    _unit(f"C_K{_j}", AT["C_K"] + _j, 1, [_j], "avav"[_j])
for _j in range(2):
    _unit(f"C_V{_j}", AT["C_V"] + 2 * _j, 2, [2 * _j, 2 * _j + 1], "av")
_unit("O20", AT["O2"], 2, [0, 1], "v")
_unit("O21", AT["O2"] + 2, 2, [2, 3], "v")


def drained_by(name, who):
    upto = _order[:_order.index(name) + 1]
    return sum(who in UNITS[u][3] for u in upto)


def free_waits(name):
    i = _order.index(name)
    last = {}
    for u in _order[:i]:
        for b in UNITS[u][2]:
            last[b] = u
    return sorted({last[b] for b in UNITS[name][2] if b in last}, key=_order.index)


class Tally:

    def __init__(self, eng, sem):
        self.eng, self.sem, self.n, self.dyn = eng, sem, 0, None

    def did(self, ins):
        ins.then_inc(self.sem, 1)
        self.n += 1
        return ins

    def settle(self):
        self.eng.wait_ge(self.sem, self.n if self.dyn is None else self.dyn + self.n)

    def link(self, ins):
        self.did(ins)
        self.settle()

    def enter(self, i, per):
        self.dyn, self.at, self.per = i * per, self.n, per

    def leave(self, count):
        assert self.n - self.at == self.per, (self.n - self.at, self.per)
        self.n, self.dyn = self.at + self.per * count, None


def build(nc, a, out, FAST_LIMIT=P):
    ctx = ExitStack()
    with ctx:
        def sb(name, shape, dt=F32):
            return ctx.enter_context(nc.sbuf_tensor(name, shape, dt))

        sems = {}

        def sem(name):
            if name not in sems:
                sems[name] = ctx.enter_context(nc.semaphore(name))
            return sems[name]

        raw = sb("raw", [P, RING, HALF])
        w_hi = sb("w_hi", [P, RING, HALF], F32R)
        w_lo = sb("w_lo", [P, RING, HALF], F32R)
        x_res = sb("x_res", [P, TB, D])
        xt_hi = sb("xt_hi", [P, KC, T], F32R)
        xt_lo = sb("xt_lo", [P, KC, T], F32R)
        mixed = sb("mixed", [P, TB, D])
        gain = sb("gain", [P, 2, D])
        mt_hi = sb("mt_hi", [P, KC, T], F32R)
        mt_lo = sb("mt_lo", [P, KC, T], F32R)
        perm = sb("perm", [P, TB, P], F32R)
        perm_t = sb("perm_t", [P, T], F32R)
        ht_hi = sb("ht_hi", [P, 2, 2, T], F32R)
        ht_lo = sb("ht_lo", [P, 2, 2, T], F32R)
        mem_k = sb("mem_k", [P, 2, 2, T])
        mem_v = sb("mem_v", [P, 2, TB, MEM_W])
        ident = sb("ident", [P, P])
        ident_r = sb("ident_r", [P, P], F32R)
        zeros_r = sb("zeros_r", [P, P], F32R)
        ones = sb("ones", [P, P])
        neg_ones = sb("neg_ones", [P, P])
        before = sb("before", [P, P])
        upto = sb("upto", [P, P])
        neg_from = sb("neg_from", [P, P])
        bias_sb_r = sb("bias_sb_r", [P, P], F32R)
        bias_fox_r = sb("bias_fox_r", [P, P], F32R)
        slot_no = sb("slot_no", [P, P])
        reset64 = sb("reset64", [P, 512])
        reset4 = sb("reset4", [P, 8])
        level_mask = sb("level_mask", [P, len(LEVELS) + 1, P], I8)
        neg_half = sb("neg_half", [P, 16])
        small_hi = sb("small_hi", [P, 3, 160], F32R)
        small_lo = sb("small_lo", [P, 3, 160], F32R)
        r_bias = sb("r_bias", [P, 2, 20])
        f_bias = sb("f_bias", [P, 16])
        conv = sb("conv", [P, 4, FC])
        stats = sb("stats", [P, TB, 2, 6])
        mv = sb("mv", [P, TB, 2])
        var_eps = sb("var_eps", [P, 16])
        rstd = sb("rstd", [P, 16])
        peak = sb("peak", [P, 64])
        total = sb("total", [P, 64])
        rt = sb("rt", [P, 320])
        load_max = sb("load_max", [P, 1], I32)
        slot_gate = sb("slot_gate", [P, 4])
        arena = sb("arena", [P, 9216])

        psum = ctx.enter_context(nc.psum_tensor("psum", [P, 8, 512], F32))

        def ar(at, *dims):
            n = 1
            for d in dims:
                n *= d
            v = arena[:, at:at + n]
            if len(dims) == 2:
                v = v.rearrange("p (a b) -> p a b", a=dims[0])
            elif len(dims) == 3:
                v = v.rearrange("p (a b c) -> p a b c", a=dims[0], b=dims[1])
            return v

        small_w = ar(0, 3, 160)
        bias_sb, bias_fox = ar(1536, P), ar(1664, P)

        raw_in = [sem(f"raw_in{i}") for i in range(RING)]
        x_in, mem_in, small_in, gain_in = sem("x_in"), sem("mem_in"), sem("small_in"), sem("gain_in")
        p_in, gnorm_in, c_moved, out_in = sem("p_in"), sem("gnorm_in"), sem("c_moved"), sem("out_in")
        consts = sem("consts")
        consts_r = sem("consts_r")
        hi_split = sem("hi_split")
        lo_split = sem("lo_split")
        half_used = sem("half_used")
        drained_a, drained_v = sem("drained_a"), sem("drained_v")
        tr_done, tr_hi, tr_lo = sem("tr_done"), sem("tr_hi"), sem("tr_lo")
        small_h, small_l = sem("small_h"), sem("small_l")
        ln_done = sem("ln_done")
        var_ready, rstd_ready = sem("var_ready"), sem("rstd_ready")

        def w_half(h, part):
            return part[:, h % RING, :]

        block = ctx.enter_context(nc.Block())

        @block.sync
        def _(sp):
            def load(h, pieces, lo_count=None):
                if not isinstance(h, int) or h >= RING:
                    sp.wait_ge(lo_split, (h if lo_count is None else lo_count) - RING + 1)
                return pieces

            def send(slot, dst_src):
                for dst, src in dst_src:
                    sp.dma_start(dst, src).then_inc(raw_in[slot], 16)

            def fm(w, col):
                v = w.rearrange("(k p) n -> p k n", p=P)[:, :, col:col + 256]
                return lambda r: [(r.rearrange("p (k n) -> p k n", k=8)[:, 4 * i:4 * i + 4, :],
                                   v[:, 4 * i:4 * i + 4, :]) for i in range(2)]

            def tm(w, col, half):
                v = w.rearrange("(k p) n -> p k n", p=P)[:, 4 * half:4 * half + 4, col:col + 512]
                return lambda r: [(r.rearrange("p (k n) -> p k n", k=4)[:, 2 * i:2 * i + 2, :],
                                   v[:, 2 * i:2 * i + 2, :]) for i in range(2)]

            def rows(w, chunk):
                v = w.rearrange("(k p) n -> p k n", p=P)[:, chunk:chunk + 2, :]
                return lambda r: [(r.rearrange("p (k n) -> p k n", k=2)[:, i, :], v[:, i, :]) for i in range(2)]

            h = 0

            def put(make):
                nonlocal h
                load(h, None)
                send(h % RING, make(raw[:, h % RING, :]))
                h += 1

            def experts(layer):
                nonlocal h
                assert h == AT[f"E{layer}"]
                wg = a["w_gate"][layer].rearrange("(g j) (k p) f -> g j p k f", j=PER_GROUP, p=P)
                wu = a["w_up"][layer].rearrange("(g j) (k p) f -> g j p k f", j=PER_GROUP, p=P)
                wd = a["w_down"][layer].rearrange("(g j) (k p) n -> g j p k n", j=PER_GROUP, p=P)
                with sp.Fori(0, GROUPS) as g:
                    for n, (kind, j, half) in enumerate(GROUP_ORDER):
                        sp.wait_ge(lo_split, g * PER_G + (h + n - RING + 1))
                        slot = (h + n) % RING
                        r = raw[:, slot, :]
                        if kind == "G":
                            v = r.rearrange("p (k n) -> p k n", k=4)
                            send(slot, [(v[:, :, 0:256], wg[g, j, :, 4 * half:4 * half + 4, :]),
                                        (v[:, :, 256:512], wu[g, j, :, 4 * half:4 * half + 4, :])])
                        else:
                            v = r.rearrange("p (k n) -> p k n", k=2)
                            send(slot, [(v[:, i, :], wd[g, j, :, i, :]) for i in range(2)])
                h += GROUPS * PER_G

            def gains(g, b, n):
                if n:
                    sp.wait_ge(ln_done, 2 * n)
                for i, v in enumerate((g, b)):
                    sp.dma_start(gain[:, i, :], v.rearrange("(o d) -> o d", o=1).to_broadcast([P, D]))\
                        .then_inc(gain_in, 16)

            sp.dma_start(x_res[:], a["x"][0].rearrange("(b p) d -> p b d", p=P)).then_inc(x_in, 16)
            wa = a["a_w_in"][0]
            for j in range(3):
                put(fm(wa, SEQ_W + 256 * j))
            sp.dma_start(mixed[:], a["mem"][0].rearrange("(b p) d -> p b d", p=P)).then_inc(mem_in, 16)
            for j in range(3):
                put(fm(wa, 256 * j))
            for j in range(3):
                for half in range(2):
                    put(tm(wa, 2 * SEQ_W + 512 * j, half))
            put(fm(wa, 4 * SEQ_W))
            for layer in range(2):
                put(fm(a["w_mem_kv"][layer], 0))
                put(fm(a["w_mem_kv"][layer], MEM_W))
            for layer in range(2):
                if layer:
                    for j in range(3):
                        put(fm(a["w_kv_shared"], 256 * j))
                    for half in range(2):
                        put(tm(a["w_kv_shared"], SEQ_W, half))
                    put(fm(a["w_kv_shared"], SEQ_W + 512))
                    for j in range(3):
                        put(fm(a["b_w_in"][0], 256 * j))
                    put(fm(a["b_w_in"][0], SEQ_W))
                for j in range(2):
                    for half in range(2):
                        put(tm(a["w_o"][layer], 512 * j, half))
                if layer == 0:
                    sp.wait_ge(sem("mixed_ready"), 2)
                gains(a["ln_mix_g"][layer], a["ln_mix_b"][layer], 2 * layer)
                experts(layer)
                gains(a["ln_ffn_g"][layer], a["ln_ffn_b"][layer], 2 * layer + 1)
            wc = a["attn_w_in_2"][0]
            for j in range(8):
                put(fm(wc, 256 * j))
            for j in range(2):
                for half in range(2):
                    put(tm(wc, 2 * D + 512 * j, half))
            for j in range(2):
                for half in range(2):
                    put(tm(a["attn_w_out_2"][0], 512 * j, half))
            gains(a["ln_mix_g_2"][0], a["ln_mix_b_2"][0], 4)
            wu2 = a["ffn_w_up_2"][0]
            for j in range(FC // 2):
                put(fm(wu2, FFN + 256 * j))
                put(fm(wu2, 256 * j))
            for j in range(FC // 2):
                put(rows(a["ffn_w_down_2"][0], 2 * j))
            gains(a["ln_ffn_g_2"][0], a["ln_ffn_b_2"][0], 5)
            sp.wait_ge(tr_done, 18)
            sp.dma_start(mixed[:, :, 0:256], a["p_2"][0, 0].rearrange("(b p) d -> p b d", p=P)).then_inc(p_in, 16)
            put(rows(a["ple_w_proj_2"][0], 0))
            for j in range(2):
                for half in range(2):
                    put(tm(a["ple_w_gate_2"][0], 512 * j, half))
            assert h == HALVES
            sp.wait_ge(ln_done, 12)
            sp.dma_start(gain[:, 0, :], a["ple_b_gate_2"][0].rearrange("(o d) -> o d", o=1).to_broadcast([P, D]))\
                .then_inc(gain_in, 16)
            out_v = out[0].rearrange("(b p) d -> p b d", p=P)
            for b in range(TB):
                sp.wait_ge(sem("result"), b + 1)
                sp.dma_start(out_v[:, b, :], x_res[:, b, :]).then_inc(out_in, 16)
            sp.wait_ge(out_in, 16 * TB)

        @block.gpsimd
        def _(pool):
            own = Tally(pool, sem("pool_own"))
            pool.memset(zeros_r[:].bitcast(F32), 0.0)
            pool.memset(ident[:], 0.0)
            pool.memset(ones[:], 1.0)
            pool.memset(neg_ones[:], -1.0)
            pool.memset(before[:], 1.0)
            pool.memset(upto[:], 1.0)
            pool.memset(neg_from[:], -1.0)
            pool.memset(bias_sb[:], 0.0)
            pool.memset(bias_fox[:], 0.0)
            pool.memset(reset64[:], 1.0)
            pool.memset(reset4[:], 1.0)
            pool.memset(neg_half[:], -0.5)
            own.link(pool.memset(level_mask[:], 0))

            def keep(tile, op, fill, base, step, mult, n=P):
                own.did(pool.affine_select(out=tile, in_=tile, compare_op=op, fill=fill, base=base,
                                           pattern=[[step, n]], channel_multiplier=mult))

            keep(ident[:], ALU.not_equal, 1.0, 0, -1, 1)
            keep(before[:], ALU.is_gt, 0.0, 0, 1, -1)
            keep(upto[:], ALU.is_ge, 0.0, 0, 1, -1)
            keep(neg_from[:], ALU.is_ge, 0.0, 0, -1, 1)
            keep(bias_sb[:], ALU.is_gt, NEG, 0, 1, -1)
            keep(bias_fox[:], ALU.is_ge, NEG, 0, -1, 1)
            own.did(pool.memset(reset64[:].rearrange("p (c t) -> p c t", t=64)[:, :, 0:1], 0.0))
            own.did(pool.memset(reset4[:].rearrange("p (c t) -> p c t", t=4)[:, :, 0:1], 0.0))
            own.did(pool.iota(slot_no[:], pattern=[[1, P]], base=0, channel_multiplier=0,
                              allow_small_or_imprecise_dtypes=True))
            own.settle()
            pool.nop().then_inc(consts, 1)
            for i, L in enumerate(LEVELS):
                up = level_mask[:, i, :].rearrange("p (b u t) -> p b u t", u=2, t=L)[:, :, 1, :]
                nb = P // (2 * L)
                own.link(pool.memset(up, 1))
                own.link(pool.affine_select(out=up, in_=up, compare_op=ALU.is_ge, fill=0.0, base=0,
                                            pattern=[[-2 * L, nb], [0, L]], channel_multiplier=1))
                own.link(pool.affine_select(out=up, in_=up, compare_op=ALU.is_ge, fill=0.0, base=L - 1,
                                            pattern=[[2 * L, nb], [0, L]], channel_multiplier=-1))
            dg = level_mask[:, len(LEVELS), :]
            own.link(pool.memset(dg, 1))
            own.link(pool.affine_select(out=dg, in_=dg, compare_op=ALU.is_equal, fill=0.0, base=0,
                                        pattern=[[-1, P]], channel_multiplier=1))
            own.link(pool.memset(ar(6144, 1536), 0.0))
            pool.nop().then_inc(consts, 1)

            def power(n, cols):
                pool.wait_ge(var_ready, n)
                pool.tensor_tensor(rstd[:, cols], var_eps[:, cols], neg_half[:, cols], ALU.pow)\
                    .then_inc(rstd_ready, 1)

            n = 0
            for b in range(3):
                n += 1
                power(n, slice(4 * b, 4 * b + 4))
            for _ in range(6):
                for b in range(TB):
                    n += 1
                    power(n, slice(b, b + 1))

        hq = ar(0, HG_HEADS, T)
        hG = ar(1536, HG_HEADS, T)
        hk = ar(3072, HG_HEADS, T)
        hX = ar(4608, 3, 512)
        hS = ar(6144, 2 * HG_HEADS, P)
        hg = ar(7680, TB, SEQ_W)
        spare = gain[:].rearrange("p g d -> p (g d)")
        hSx = spare[:, 768:1536].rearrange("p (h t) -> p h t", t=P)
        a_qm = spare[:, 1536:2048].rearrange("p (c t) -> p c t", t=T)
        sq = ar(4608, 3, 512)

        b_q = ar(0, 6, T)
        b_k = ar(1536, 6, T)
        b_qm = ar(3072, 2, T)
        b_l = ar(3584, 2, 2, 384)
        b_s = ar(5120, 2, 2, 384)
        b_a = ar(6656, 2, 2, 384)

        c_q = ar(0, 8, T)
        c_k = ar(2048, 8, T)
        c_f = ar(4096, TB, FOX_HEADS)
        c_c = ar(4128, TB, FOX_HEADS)
        c_p = ar(4608, 2, 2, 384)
        c_pt = ar(6144, 2, 2, 384)
        c_t = ar(4160, T)

        ff_t = ar(0, 2, 512)
        ff_g = ar(1024, 2, 512)
        ff_a = ar(2048, FC, T)
        pl_s = ar(0, 2, 512)

        ex_s = ar(0, 2, 2, 256)
        ex_h = ar(1024, 2, 2, 256)

        A_HALVES = list(range(AT["A_IG"], AT["O0"]))
        N_STEPS = 3 * STEPS

        def decayed(st):
            p, i = divmod(st, STEPS)
            return (STEPS - 1) * p + min(i + 1, STEPS - 1)

        ends = {UNITS[u][0] + UNITS[u][1] - 1: u for u in _order}
        mem_tmp = {0: (0, 1024), 1: (3584, 5120)}

        r_log = rt[:, 0:40].rearrange("p (b e) -> p b e", b=2)
        r_g = rt[:, 40:48].rearrange("p (b e) -> p b e", b=2)
        r_eq = rt[:, 48:56]
        r_cum = rt[:, 56:64]
        r_og = rt[:, 64:72].rearrange("p (b e) -> p b e", b=2)
        r_t16 = rt[:, 72:104].rearrange("p (b g e) -> p b g e", b=2, g=4)
        r_e = rt[:, 104:112].rearrange("p (b e) -> p b e", b=2)
        r_o1 = rt[:, 112:120].rearrange("p (b e) -> p b e", b=2)
        r_o2 = rt[:, 120:128].rearrange("p (b e) -> p b e", b=2)
        r_m = rt[:, 128:144].rearrange("p (n b) -> p n b", b=2)
        r_g4 = rt[:, 144:152].rearrange("p (b e) -> p b e", b=2)
        r_gate = rt[:, 160:192].rearrange("p (b g e) -> p b g e", b=2, g=4)
        r_pos = rt[:, 192:204].rearrange("p (n g) -> p n g", g=4)
        r_i4 = rt[:, 208:216].rearrange("p (b e) -> p b e", b=2)
        r_e2 = rt[:, 216:224].rearrange("p (b e) -> p b e", b=2)
        r_mx = rt[:, 224:225]

        @block.tensor
        def _(pe):
            def mm(o, l, r, start, stop, skip=False):
                return pe.matmul(o, l, r, start=start, stop=stop, skip_group_check=skip)

            def free(name):
                for u in free_waits(name):
                    for who, s in (("a", drained_a), ("v", drained_v)):
                        if who in UNITS[u][3]:
                            pe.wait_ge(s, drained_by(u, who))

            def passes(hi, lo, whi, wlo):
                return ((hi, whi), (hi, wlo), (lo, whi))

            def fm_half(name, xh, xl):
                h, _, banks, _ = UNITS[name]
                free(name)
                pe.wait_ge(lo_split, h + 1)
                fm_products(h, banks[0], xh, xl)

            def fm_products(h, bank, xh, xl, used=None):
                wh, wl = (w_half(h, w).rearrange("p (k n) -> p k n", k=8) for w in (w_hi, w_lo))
                for c in range(2):
                    for k in range(KC):
                        ws = slice(P * c, P * c + P)
                        for i, (x, w) in enumerate(passes(xh[:, k, :], xl[:, k, :], wh[:, k, ws], wl[:, k, ws])):
                            last = mm(psum[:, bank, T * c:T * c + T], w, x, c == 0 and k == 0 and i == 0,
                                      c == 1 and k == KC - 1 and i == 2, skip=True)
                last.then_inc(half_used, 1)

            def tm256(name, xh, xl):
                h, _, banks, _ = UNITS[name]
                free(name)
                pe.wait_ge(lo_split, h + 1)
                wh, wl = (w_half(h, w).rearrange("p (k n) -> p k n", k=8) for w in (w_hi, w_lo))
                for b in range(TB):
                    for k in range(KC):
                        ts = slice(P * b, P * b + P)
                        for i, (x, w) in enumerate(passes(xh[:, k, ts], xl[:, k, ts], wh[:, k, :], wl[:, k, :])):
                            last = mm(psum[:, banks[0], 256 * b:256 * b + 256], x, w,
                                      b == 0 and k == 0 and i == 0, b == 1 and k == KC - 1 and i == 2, skip=True)
                last.then_inc(half_used, 1)

            def tm_half(h, half, banks, xh, xl):
                pe.wait_ge(lo_split, h + 1)
                wh, wl = (w_half(h, w).rearrange("p (k n) -> p k n", k=4) for w in (w_hi, w_lo))
                for b in range(TB):
                    for kk in range(4):
                        k = 4 * half + kk
                        ts = slice(P * b, P * b + P)
                        for i, (x, w) in enumerate(passes(xh[:, k, ts], xl[:, k, ts], wh[:, kk, :], wl[:, kk, :])):
                            last = mm(psum[:, banks[b], :], x, w, k == 0 and i == 0, k == KC - 1 and i == 2)
                last.then_inc(half_used, 1)

            def tm_tile(name, xh, xl):
                h, _, banks, _ = UNITS[name]
                free(name)
                for half in range(2):
                    tm_half(h + half, half, banks, xh, xl)

            def turn(s, src, chunk0, n=4):
                if s >= 2:
                    pe.wait_ge(tr_lo, s - 1)
                bank = 4 + 2 * (s % 2)
                for c in range(n):
                    for b in range(TB):
                        k = chunk0 + c
                        last = pe.transpose(psum[:, bank + c // 2, T * (c % 2) + P * b:T * (c % 2) + P * b + P],
                                            src[:, b, P * k:P * k + P], ident[:])
                last.then_inc(tr_done, 1)

            def turn_both(s, src, ready, value):
                pe.wait_ge(ready, value)
                turn(s, src, 0)
                turn(s + 1, src, 4)

            def split_ready(s):
                pe.wait_ge(tr_lo, s + 1)

            pe.wait_ge(consts, 1)
            pe.wait_ge(x_in, 16)
            turn(0, x_res, 0)
            turn(1, x_res, 4)
            split_ready(1)
            for j in range(3):
                fm_half(f"A_F{j}", xt_hi, xt_lo)
            pe.wait_ge(mem_in, 16)
            turn(2, mixed, 0)
            turn(3, mixed, 4)
            for j in range(3):
                fm_half(f"A_Q{j}", xt_hi, xt_lo)
            pe.wait_ge(tr_lo, 4)

            def a_step(st):
                p, i = divmod(st, STEPS)
                if i <= len(LEVELS):
                    pe.wait_ge(sem("x_ready"), decayed(st))
                else:
                    pe.wait_ge(sem("q_scaled"), p + 1)
                    pe.wait_ge(sem("k_ready"), p + 1)
                if st >= 4:
                    pe.wait_ge(sem("merged"), st - 3)
                bank = psum[:, 4 + st % 4, :]
                x = hX[:, st % 3, :].rearrange("p (h t) -> p h t", h=2)
                for hh in range(2):
                    if i == len(LEVELS):
                        last = mm(bank[:, P * hh:P * hh + P], x[:, hh, 0:P], x[:, hh, P:T], True, True)
                        continue
                    for b in range(TB):
                        o = bank[:, (2 * hh + b) * P:(2 * hh + b) * P + P]
                        if i < len(LEVELS):
                            v = x[:, hh, P * b:P * b + P]
                            last = mm(o, v, v, True, True)
                        else:
                            last = mm(o, hk[:, 2 * p + hh, P * b:P * b + P], hq[:, 2 * p + hh, P * b:P * b + P],
                                      True, True)
                last.then_inc(sem("level_done"), 1)

            for n, h in enumerate(A_HALVES):
                name = next(u for u in _order if UNITS[u][0] <= h < UNITS[u][0] + UNITS[u][1])
                if name.startswith("A_IG"):
                    if h == UNITS[name][0]:
                        free(name)
                    tm_half(h, h - UNITS[name][0], UNITS[name][2], xt_hi, xt_lo)
                elif name == "A_QM":
                    fm_half(name, xt_hi, xt_lo)
                elif name.startswith("MK"):
                    fm_half(name, mt_hi, mt_lo)
                else:
                    tm256(name, mt_hi, mt_lo)
                for st in range(3 * n, min(3 * n + 3, N_STEPS)):
                    a_step(st)
            pe.wait_ge(sem("merged"), N_STEPS)
            pe.wait_ge(drained_a, drained_by("MK1", "a"))
            pe.wait_ge(drained_v, drained_by("MV1", "v"))
            for p in range(3):
                for hh in range(2):
                    h = 2 * p + hh
                    cs = slice(P * h, P * h + P)
                    for b in range(TB):
                        o = psum[:, p, (2 * hh + b) * P:(2 * hh + b) * P + P]
                        last = mm(o, hS[:, 2 * h + b, :], mixed[:, b, cs], True, b == 0)
                        if b:
                            last = mm(o, hSx[:, h, :], mixed[:, 0, cs], False, True)
                last.then_inc(sem("hg_out"), 1)

            def memory_attention(layer, qm):
                tp, tt = mem_tmp[layer]
                pt = ar(tt, 2, 2, T)
                qk, ptr, pv = sem("mem_scores"), sem("mem_turned"), sem("mem_out")
                for h in range(4):
                    rows = slice(64 * (h % 2), 64 * (h % 2) + 64)
                    for b in range(TB):
                        last = mm(psum[:, 4 + h, T * b:T * b + T], qm[rows, h // 2, P * b:P * b + P],
                                  mem_k[rows, layer, h // 2, :], True, True)
                    last.then_inc(qk, 1)
                for h in range(4):
                    n = 4 * layer + h
                    pe.wait_ge(sem("mem_prob"), n + 1)
                    prob = ar(tp, 2, 2, T)[:, h % 2, :, :]
                    for m in range(2):
                        for b in range(TB):
                            last = pe.transpose(psum[:, 4 + h, T * m + P * b:T * m + P * b + P],
                                                prob[:, b, P * m:P * m + P], ident[:])
                    last.then_inc(ptr, 1)
                    pe.wait_ge(sem("mem_pt"), n + 1)
                    for b in range(TB):
                        for m in range(2):
                            last = mm(psum[:, 3, 256 * b + 64 * h:256 * b + 64 * h + 64],
                                      pt[:, h % 2, m, P * b:P * b + P], mem_v[:, layer, m, 64 * h:64 * h + 64],
                                      m == 0, m == 1)
                    last.then_inc(pv, 1)

            pe.wait_ge(drained_a, drained_by("MK1", "a"))
            memory_attention(0, a_qm)

            def project(layer, s):
                pe.wait_ge(sem("mixed_ready"), 2 * (layer + 1))
                turn(s, mixed, 0)
                turn(s + 1, mixed, 4)
                split_ready(s + 1)
                for j in range(2):
                    tm_tile(f"O{layer}{j}", xt_hi, xt_lo)

            def experts(layer):
                s = {n: sem(f"{n}{layer}") for n in ("perm_ready", "gathered", "xg_hi", "xg_lo", "y_hi", "y_lo")}
                base = AT[f"E{layer}"]
                zeros_row = zeros_r[:].rearrange("p (o n) -> p o n", o=1).to_broadcast([P, 4, P])
                for b in range(TB):
                    for k in range(KC):
                        ts = slice(P * b, P * b + P)
                        wh, wl = (w[:, layer, 20 * k:20 * k + 20] for w in (small_hi, small_lo))
                        for i, (x, w) in enumerate(passes(xt_hi[:, k, ts], xt_lo[:, k, ts], wh, wl)):
                            last = mm(psum[:, 0, 20 * b:20 * b + 20], x, w, b == 0 and k == 0 and i == 0,
                                      b == 1 and k == KC - 1 and i == 2, skip=True)
                last.then_inc(sem("logits"), 1)
                pe.wait_ge(sem("group_ready"), layer + 1)
                og = rt[:, 64:72]
                mm(psum[:, 1, 0:4], before[:], og[:, 0:4], True, True)
                mm(psum[:, 1, 4:8], ones[:], og[:, 0:4], True, False)
                mm(psum[:, 1, 4:8], before[:], og[:, 4:8], False, True)
                mm(psum[:, 1, 8:12], ones[:], og[:, 0:4], True, False)
                mm(psum[:, 1, 8:12], ones[:], og[:, 4:8], False, True).then_inc(sem("counted"), 1)
                pe.wait_ge(sem("routed"), layer + 1)
                for q in range(4):
                    mm(psum[:, q, :], zeros_r[:], zeros_row, True, False, skip=True)
                load = pe.value_load(load_max[0:1, 0:1], min_val=0, max_val=T)

                def group(g, dense):
                    nb = TB if dense else 1
                    if not dense:
                        pe.wait_ge(s["perm_ready"], g + 1)
                        for k in range(KC):
                            o = psum[:, 4 + k // 4, P * (k % 4):P * (k % 4) + P]
                            n = 0
                            for b in range(TB):
                                for x in (mt_hi, mt_lo):
                                    xv = x[:].rearrange("p k t -> p (k t)")
                                    mm(o, xv[:, D * b + P * k:D * b + P * k + P], perm[:, b, :], n == 0, n == 3)
                                    n += 1
                        for b in range(TB):
                            mm(psum[:, 7, 0:4], perm[:, b, :].bitcast(F32),
                               r_gate[:, b, bass.ds(g, 1), :].rearrange("p a e -> p (a e)"), b == 0, b == 1)
                        for b in range(TB):
                            last = pe.transpose(psum[:, 7, 128 + P * b:256 + P * b], perm[:, b, :].bitcast(F32),
                                                ident[:])
                        last.then_inc(s["gathered"], 1)
                        pe.wait_ge(s["xg_hi"], g + 1)
                        pe.wait_ge(s["xg_lo"], g + 1)

                    e0 = 16 * layer

                    def gu_bank(j, b):
                        return 4 + 2 * (j % 2) + b if dense else 6 + j % 2

                    def gate_up(j):
                        if j >= 2:
                            pe.wait_ge(sem("ht_hi_ready"), g * PER_GROUP + (e0 + j - 1))
                            pe.wait_ge(sem("ht_lo_ready"), g * PER_GROUP + (e0 + j - 1))
                        for half in range(2):
                            h = base + G_AT[j] + half
                            pe.wait_ge(lo_split, g * PER_G + (h + 1))
                            wh, wl = (w_half(h, w).rearrange("p (k n) -> p k n", k=4) for w in (w_hi, w_lo))
                            for b in range(nb):
                                for kk in range(4):
                                    k = 4 * half + kk
                                    ts = slice(P * b, P * b + P)
                                    for i, (x, w) in enumerate(passes(xt_hi[:, k, ts], xt_lo[:, k, ts],
                                                                      wh[:, kk, :], wl[:, kk, :])):
                                        last = mm(psum[:, gu_bank(j, b), :], x, w, k == 0 and i == 0,
                                                  k == KC - 1 and i == 2)
                            last.then_inc(half_used, 1)

                    def turn_h(j):
                        pe.wait_ge(sem("h_ready"), g * PER_GROUP + (e0 + j + 1))
                        for f in range(2):
                            for b in range(nb):
                                last = pe.transpose(
                                    psum[:, gu_bank(j, 0), P * nb * f + P * b:P * nb * f + P * b + P],
                                    ex_h[:, j % 2, b, P * f:P * f + P], ident[:])
                        last.then_inc(sem("h_turned"), 1)

                    def down(j):
                        pe.wait_ge(sem("ht_hi_ready"), g * PER_GROUP + (e0 + j + 1))
                        pe.wait_ge(sem("ht_lo_ready"), g * PER_GROUP + (e0 + j + 1))
                        h = base + D_AT[j]
                        pe.wait_ge(lo_split, g * PER_G + (h + 1))
                        wh, wl = (w_half(h, w).rearrange("p (k n) -> p k n", k=2) for w in (w_hi, w_lo))
                        for n in range(2):
                            for b in range(nb):
                                for f in range(2):
                                    ts = slice(P * b, P * b + P)
                                    for i, (x, w) in enumerate(passes(
                                            ht_hi[:, j % 2, f, ts], ht_lo[:, j % 2, f, ts],
                                            wh[:, f, 512 * n:512 * n + 512], wl[:, f, 512 * n:512 * n + 512])):
                                        if dense:
                                            last = mm(psum[:, 2 * n + b, :], x, w, False, False, skip=True)
                                        else:
                                            last = mm(psum[:, 4 + n, :], x, w, j == 0 and f == 0 and i == 0,
                                                      j == 3 and f == 1 and i == 2)
                        last.then_inc(half_used, 1)

                    gate_up(0)
                    gate_up(1)
                    turn_h(0)
                    gate_up(2)
                    turn_h(1)
                    down(0)
                    gate_up(3)
                    turn_h(2)
                    down(1)
                    turn_h(3)
                    down(2)
                    down(3)
                    if not dense:
                        pe.wait_ge(s["y_hi"], g + 1)
                        pe.wait_ge(s["y_lo"], g + 1)
                        for n in range(2):
                            for b in range(TB):
                                for y in (xt_hi, xt_lo):
                                    last = mm(psum[:, 2 * n + b, :], perm_t[:, P * b:P * b + P],
                                              y[:, 4 * n:4 * n + 4, P:T], False, False, skip=True)

                with pe.If(load < FAST_LIMIT + 1):
                    with pe.Fori(0, GROUPS) as g:
                        group(g, False)
                with pe.Else():
                    with pe.Fori(0, GROUPS) as g:
                        group(g, True)
                for q in range(4):
                    last = mm(psum[:, q, :], zeros_r[:], zeros_row, False, True, skip=True)
                last.then_inc(sem("moe_done"), 1)

            project(0, 4)
            pe.wait_ge(ln_done, 2)
            turn(6, x_res, 0)
            turn(7, x_res, 4)
            split_ready(7)
            pe.wait_ge(small_l, 1)
            experts(0)
            pe.wait_ge(ln_done, 4)
            turn(8, x_res, 0)
            turn(9, x_res, 4)
            split_ready(9)

            for j in range(3):
                fm_half(f"B_K{j}", xt_hi, xt_lo)
            tm_tile("B_V0", xt_hi, xt_lo)
            tm256("B_V1", xt_hi, xt_lo)
            for j in range(3):
                fm_half(f"B_Q{j}", xt_hi, xt_lo)
            fm_half("B_QM", xt_hi, xt_lo)
            pe.wait_ge(drained_a, drained_by("B_Q2", "a"))
            pe.wait_ge(drained_v, drained_by("B_QM", "v"))

            def sb_scores(o, p, hh, start, stop):
                rows = slice(64 * hh, 64 * hh + 64)
                mm(o[:, 0:T], b_k[rows, p, 0:P], b_q[rows, p, :], start, False, skip=True)
                mm(o[:, T:T + P], b_k[rows, p, P:T], b_q[rows, p, P:T], False, False, skip=True)
                mm(o[:, 0:P], ident_r[:], bias_sb_r[:], False, False, skip=True)
                return mm(o[:, T:T + P], ident_r[:], bias_sb_r[:], False, stop, skip=True)

            def sb_pair(p):
                zb, ab = 4 * (p % 2), 4 * (p % 2) + 2
                if p >= 2:
                    pe.wait_ge(sem("sb_o_out"), p - 1)
                for hh in range(2):
                    last = sb_scores(psum[:, zb + hh, :], p, hh, True, True)
                last.then_inc(sem("sb_z"), 1)
                for hh in range(2):
                    sb_scores(psum[:, ab + hh, :], p, hh, True, False)

            def sb_rest(p):
                ab = 4 * (p % 2) + 2
                pe.wait_ge(sem("sb_sp"), p + 1)
                for hh in range(2):
                    o, sp = psum[:, ab + hh, :], b_s[:, p % 2, hh, :]
                    mm(o[:, 0:384], neg_from[:], sp[:, 0:384], False, False, skip=True)
                    last = mm(o[:, P:T], neg_ones[:], sp[:, T:384], False, True, skip=True)
                last.then_inc(sem("sb_log"), 1)

            def sb_out(p):
                ab = 4 * (p % 2) + 2
                pe.wait_ge(sem("sb_a"), p + 1)
                for hh in range(2):
                    o = psum[:, ab + hh, 384:512]
                    w = b_a[:, p % 2, hh, :]
                    cs = slice(64 * (2 * p + hh), 64 * (2 * p + hh) + 64)
                    mm(o[:, 0:64], w[:, 0:P], mixed[:, 0, cs], True, True)
                    mm(o[:, 64:128], w[:, P:T], mixed[:, 0, cs], True, False)
                    last = mm(o[:, 64:128], w[:, T:384], mixed[:, 1, cs], False, True)
                last.then_inc(sem("sb_o"), 1)

            sb_pair(0)
            sb_pair(1)
            for p in range(6):
                sb_rest(p)
                if p:
                    sb_out(p - 1)
                    if p + 1 < 6:
                        sb_pair(p + 1)
            sb_out(5)
            pe.wait_ge(sem("sb_o_out"), 6)
            memory_attention(1, b_qm)
            project(1, 10)
            pe.wait_ge(ln_done, 6)
            turn(12, x_res, 0)
            turn(13, x_res, 4)
            split_ready(13)
            experts(1)
            pe.wait_ge(ln_done, 8)
            turn(14, x_res, 0)
            turn(15, x_res, 4)
            split_ready(15)

            for b in range(TB):
                for k in range(KC):
                    ts = slice(P * b, P * b + P)
                    wh, wl = (w[:, 2, 16 * k:16 * k + 16] for w in (small_hi, small_lo))
                    for i, (x, w) in enumerate(passes(xt_hi[:, k, ts], xt_lo[:, k, ts], wh, wl)):
                        last = mm(psum[:, 4, 16 * b:16 * b + 16], x, w, b == 0 and k == 0 and i == 0,
                                  b == 1 and k == KC - 1 and i == 2, skip=True)
            last.then_inc(sem("f_logits"), 1)
            for j in range(4):
                fm_half(f"C_Q{j}", xt_hi, xt_lo)
            pe.wait_ge(sem("f_log"), 1)
            mm(psum[:, 5, 0:16], upto[:], c_f[:, 0, :], True, True)
            mm(psum[:, 5, 16:32], ones[:], c_f[:, 0, :], True, False)
            mm(psum[:, 5, 16:32], upto[:], c_f[:, 1, :], False, True).then_inc(sem("c_sum"), 1)
            for j in range(2):
                fm_half(f"C_K{j}", xt_hi, xt_lo)
            pe.wait_ge(sem("c_out"), 1)
            for b in range(TB):
                last = pe.transpose(psum[0:16, 6, P * b:P * b + P], c_c[:, b, :], ident[:])
            last.then_inc(sem("c_turned"), 1)
            for j in range(2, 4):
                fm_half(f"C_K{j}", xt_hi, xt_lo)
            for j in range(2):
                tm_tile(f"C_V{j}", xt_hi, xt_lo)
            pe.wait_ge(drained_a, drained_by("C_V1", "a"))
            pe.wait_ge(drained_v, drained_by("C_V1", "v"))
            pe.wait_ge(sem("c_split"), 2)

            c_hi = perm_t[0:16, :]
            c_lo = perm[0:16, :, :].rearrange("p b t -> p (b t)")

            def fox_scores(p):
                if p >= 2:
                    pe.wait_ge(sem("fox_o_out"), p - 1)
                for hh in range(2):
                    h = 2 * p + hh
                    o = psum[:, 4 * (p % 2) + hh, :]
                    rows = slice(64 * hh, 64 * hh + 64)
                    pick = ident_r[0:16, h:h + 1].to_broadcast([16, P])
                    mm(o[:, 0:P], c_q[rows, p, 0:P], c_k[rows, p, 0:P], True, False, skip=True)
                    mm(o[:, P:384], c_q[rows, p, P:T], c_k[rows, p, :], False, False, skip=True)
                    for c in (c_hi, c_lo):
                        mm(o[:, 0:P], pick, c[:, 0:P], False, False, skip=True)
                        mm(o[:, P:384], pick, c[:, :], False, False, skip=True)
                    mm(o[:, 0:P], ident_r[:], bias_fox_r[:], False, False, skip=True)
                    last = mm(o[:, T:384], ident_r[:], bias_fox_r[:], False, True, skip=True)
                last.then_inc(sem("fox_s"), 1)

            def fox_turn(p):
                pe.wait_ge(sem("fox_p"), p + 1)
                for hh in range(2):
                    o = psum[:, 4 * (p % 2) + 2 + hh, :]
                    w = c_p[:, p % 2, hh, :]
                    for n in range(3):
                        last = pe.transpose(o[:, P * n:P * n + P], w[:, P * n:P * n + P], ident[:])
                last.then_inc(sem("fox_turned"), 1)

            def fox_out(p):
                pe.wait_ge(sem("fox_pt"), p + 1)
                for hh in range(2):
                    o = psum[:, 4 * (p % 2) + 2 + hh, 384:512]
                    w = c_pt[:, p % 2, hh, :]
                    cs = slice(64 * (2 * p + hh), 64 * (2 * p + hh) + 64)
                    mm(o[:, 0:64], w[:, 0:P], mixed[:, 0, cs], True, True)
                    mm(o[:, 64:128], w[:, P:T], mixed[:, 0, cs], True, False)
                    last = mm(o[:, 64:128], w[:, T:384], mixed[:, 1, cs], False, True)
                last.then_inc(sem("fox_o"), 1)

            fox_scores(0)
            fox_scores(1)
            for p in range(8):
                fox_turn(p)
                if p:
                    fox_out(p - 1)
                    if p + 1 < 8:
                        fox_scores(p + 1)
            fox_out(7)
            pe.wait_ge(sem("fox_o_out"), 8)
            project(2, 16)
            pe.wait_ge(ln_done, 10)
            turn(18, x_res, 0)
            turn(19, x_res, 4)
            split_ready(19)

            def up_pair(j, h, i=None):
                for q in range(2):
                    pe.wait_ge(lo_split, h + q + 1 if i is None else i * 4 + (h + q + 1))
                    fm_products(h + q, 2 * (j % 2) + q, xt_hi, xt_lo)

            with pe.Fori(0, FC // 4) as i:
                for j in range(2):
                    pe.wait_ge(sem("ff_free"), i * 2 + (j + 1))
                    up_pair(j, AT["UP"] + 2 * j, i)
            pe.wait_ge(sem("ff_free"), 11)
            up_pair(0, AT["UP"] + 20)

            def row_half(h, xh, xl, bank, first, last_one):
                pe.wait_ge(lo_split, h + 1)
                wh, wl = (w_half(h, w).rearrange("p (k n) -> p k n", k=2) for w in (w_hi, w_lo))
                for n in range(2):
                    for b in range(TB):
                        for f in range(2):
                            ts = slice(P * b, P * b + P)
                            for i, (x, w) in enumerate(passes(xh[:, f, ts], xl[:, f, ts],
                                                              wh[:, f, 512 * n:512 * n + 512],
                                                              wl[:, f, 512 * n:512 * n + 512])):
                                last = mm(psum[:, bank + 2 * n + b, :], x, w, first and f == 0 and i == 0,
                                          last_one and f == 1 and i == 2)
                last.then_inc(half_used, 1)

            pe.wait_ge(sem("ff_free"), FC // 2 + 2)
            for j in range(FC // 2):
                pe.wait_ge(sem("fa_lo"), j + 1)
                q = 2 * (j % 4)
                row_half(AT["DN"] + j, mt_hi[:, q:q + 2, :], mt_lo[:, q:q + 2, :], 0, j == 0, j == FC // 2 - 1)

            pe.wait_ge(p_in, 16)
            pe.wait_ge(tr_lo, 20)
            turn(20, mixed, 0, n=2)
            split_ready(20)
            row_half(AT["PP"], mt_hi[:, 6:8, :], mt_lo[:, 6:8, :], 4, True, True)
            pe.wait_ge(ln_done, 12)
            for r in range(4):
                if r >= 2:
                    pe.wait_ge(sem("last_lo"), r - 1)
                for c in range(2):
                    for b in range(TB):
                        k = 2 * r + c
                        last = pe.transpose(psum[:, r % 2, T * c + P * b:T * c + P * b + P],
                                            x_res[:, b, P * k:P * k + P], ident[:])
                last.then_inc(sem("last_turned"), 1)
            pe.wait_ge(sem("last_lo"), 4)
            for j in range(2):
                for half in range(2):
                    tm_half(AT["PG"] + 2 * j + half, half, [2 * j, 2 * j + 1], xt_hi, xt_lo)

        @block.scalar
        def _(act):
            own = Tally(act, sem("act_own"))
            done = [0]

            def fn(o, i, f, **kw):
                return act.activation(o, i, f, **kw)

            def round_to(upto):
                while done[0] < min(upto, HALVES):
                    h = done[0]
                    act.wait_ge(raw_in[h % RING], 32 * (h // RING + 1))
                    if h >= RING:
                        act.wait_ge(half_used, h - RING + 1)
                    fn(w_half(h, w_hi), w_half(h, raw), ACT.Copy).then_inc(hi_split, 1)
                    done[0] += 1

            def used(h):
                round_to(h + 1 + AHEAD)
                act.wait_ge(half_used, h + 1)

            def split_set(s, n=4):
                act.wait_ge(tr_done, s + 1)
                dst, c0 = (mt_hi, 4 * (s - 2)) if s in (2, 3) else (mt_hi, 6) if s == 20 else (xt_hi, 4 * (s % 2))
                fn(dst[:, c0:c0 + n, :].rearrange("p k t -> p (k t)"),
                   psum[:, 4 + 2 * (s % 2):4 + 2 * (s % 2) + n // 2, :].rearrange("p b n -> p (b n)"), ACT.Copy)\
                    .then_inc(tr_hi, 1)

            def copy_unit(name, dst, bank, scale=1.0, f=ACT.Copy):
                used(UNITS[name][0] + UNITS[name][1] - 1)
                fn(dst, psum[:, bank, 0:dst.free_size()], f, scale=scale).then_inc(drained_a, 1)

            act.dma_start(small_w[:, 0:2, :], a["r_weights"]).then_inc(small_in, 16)
            act.dma_start(small_w[:, 2, 0:128], a["f_weights"]).then_inc(small_in, 16)
            act.dma_start(r_bias[:], a["r_bias"].rearrange("(o l) e -> o l e", o=1).to_broadcast([P, 2, 20]))\
                .then_inc(small_in, 16)
            act.dma_start(f_bias[:], a["attn_b_f_2"].to_broadcast([P, 16])).then_inc(small_in, 16)
            act.dma_start(conv[:], a["conv"]).then_inc(small_in, 16)
            act.dma_start(gain[:, 0, 0:SEQ_W], a["a_gnorm"].to_broadcast([P, SEQ_W])).then_inc(gnorm_in, 16)

            act.wait_ge(small_in, 80)
            for i, n in enumerate((320, 128)):
                v = (small_hi[:, 0:2, :].rearrange("p l n -> p (l n)"), small_hi[:, 2, 0:128])[i]
                w = (small_w[:, 0:2, :].rearrange("p l n -> p (l n)"), small_w[:, 2, 0:128])[i]
                last = fn(v, w, ACT.Copy)
            last.then_inc(small_h, 1)
            split_set(0)
            split_set(1)

            def pair(v, p):
                return v[:, 2 * p:2 * p + 2, :].rearrange("p h t -> p (h t)")

            for j in range(3):
                used(AT["A_F"] + j)
                k = pair(hk, j)
                own.link(fn(k, psum[:, j, :], ACT.Abs))
                own.link(fn(k, k, ACT.Exp, scale=-1.0))
                fn(k, k, ACT.Ln, bias=1.0).then_inc(sem("f_soft"), 1)
                act.wait_ge(drained_v, j + 1)
                fn(k, k, ACT.Exp).then_inc(sem("k_ready"), 1)
                if j == 0:
                    split_set(2)
                    split_set(3)
            for j in range(3):
                act.wait_ge(sem("g_ready"), j + 1)
                copy_unit(f"A_Q{j}", pair(hq, j), UNITS[f"A_Q{j}"][2][0], f=ACT.Silu)

            def a_drain(name):
                if name == "A_IG1":
                    used(UNITS[name][0] + 1)
                    act.wait_ge(drained_v, drained_by(name, "v"))
                    for b in range(TB):
                        last = fn(hg[:, b, 0:256], psum[:, UNITS[name][2][b], 256:512], ACT.Silu)
                    last.then_inc(drained_a, 1)
                elif name == "A_IG2":
                    used(UNITS[name][0] + 1)
                    for b in range(TB):
                        last = fn(hg[:, b, 256:768], psum[:, UNITS[name][2][b], :], ACT.Silu)
                    last.then_inc(drained_a, 1)
                elif name == "A_QM":
                    copy_unit(name, a_qm[:].rearrange("p c t -> p (c t)"), UNITS[name][2][0], HD_SCALE)
                elif name.startswith("MK"):
                    l = int(name[2])
                    copy_unit(name, mem_k[:, l, :, :].rearrange("p c t -> p (c t)"), UNITS[name][2][0])

            def a_exp(st):
                if st % STEPS <= len(LEVELS):
                    act.wait_ge(sem("x_logs"), decayed(st))
                    fn(hX[:, st % 3, :], hX[:, st % 3, :], ACT.Exp).then_inc(sem("x_exp"), 1)

            for n, h in enumerate(A_HALVES):
                for st in range(3 * n, min(3 * n + 3, N_STEPS)):
                    a_exp(st)
                if h - 1 in ends and h > A_HALVES[0]:
                    a_drain(ends[h - 1])
                round_to(h + AHEAD)
            round_to(A_HALVES[-1] + 1 + AHEAD)
            for p in range(3):
                act.wait_ge(sem("hg_out"), p + 1)
                act.wait_ge(sem("level_done"), N_STEPS)
                fn(sq[:, p, :], psum[:, p, :], ACT.Square).then_inc(sem("squared"), 1)

            def memory_attention(layer):
                tp, tt = mem_tmp[layer]
                pt = ar(tt, 2, 2, T)
                for h in range(4):
                    n = 4 * layer + h
                    act.wait_ge(sem("mem_peak"), n + 1)
                    if h >= 2:
                        act.wait_ge(sem("mem_turned"), n - 1)
                    for b in range(TB):
                        c = 2 * h + b
                        last = fn(ar(tp, 2, 2, T)[:, h % 2, b, :], psum[:, 4 + h, T * b:T * b + T], ACT.Exp,
                                  bias=peak[:, c:c + 1], accum_out=total[:, c:c + 1])
                    last.then_inc(sem("mem_prob"), 1)
                    if h:
                        mem_pt(layer, h - 1)
                mem_pt(layer, 3)

            def mem_pt(layer, h):
                tp, tt = mem_tmp[layer]
                n = 4 * layer + h
                act.wait_ge(sem("mem_turned"), n + 1)
                if h >= 2:
                    act.wait_ge(sem("mem_out"), n - 1)
                fn(ar(tt, 2, 2, T)[:, h % 2, :, :].rearrange("p m t -> p (m t)"), psum[:, 4 + h, :], ACT.Copy)\
                    .then_inc(sem("mem_pt"), 1)

            memory_attention(0)

            def experts(layer):
                base, e0 = AT[f"E{layer}"], 16 * layer
                s = {n: sem(f"{n}{layer}") for n in ("gathered", "xg_hi", "y_hi")}
                act.wait_ge(ln_done, 4 * layer + 2)
                fn(mt_hi[:].rearrange("p k t -> p (k t)"), x_res[:].rearrange("p b d -> p (b d)"), ACT.Copy)\
                    .then_inc(sem("x_rounded"), 1)
                act.wait_ge(sem("group_log"), layer + 1)
                fn(rt[:, 40:48], rt[:, 40:48], ACT.Exp).then_inc(sem("group_exp"), 1)
                act.wait_ge(sem("expert_log"), layer + 1)
                fn(rt[:, 104:112], rt[:, 104:112], ACT.Exp).then_inc(sem("expert_exp"), 1)
                round_to(base + 3)
                act.wait_ge(sem("routed"), layer + 1)
                load = act.value_load(load_max[0:1, 0:1], min_val=0, max_val=T)

                def group(g, dense, own2):
                    nb = TB if dense else 1
                    mark = [3]

                    def rnd(upto):
                        while mark[0] < upto:
                            h = base + mark[0]
                            act.wait_ge(raw_in[h % RING], g * (32 * PER_G // RING) + 32 * (h // RING + 1))
                            act.wait_ge(half_used, g * PER_G + (h - RING + 1))
                            fn(w_half(h, w_hi), w_half(h, raw), ACT.Copy).then_inc(hi_split, 1)
                            mark[0] += 1

                    def used_g(n):
                        rnd(n + 1 + AHEAD)
                        act.wait_ge(half_used, g * PER_G + (base + n + 1))

                    if not dense:
                        act.wait_ge(s["gathered"], g + 1)
                        fn(xt_hi[:, :, 0:P], psum[:, 4:6, :].rearrange("p b (k t) -> p (b k) t", t=P), ACT.Copy)
                        fn(perm_t[:], psum[:, 7, 128:384], ACT.Copy)
                        fn(slot_gate[:], psum[:, 7, 0:4], ACT.Copy).then_inc(s["xg_hi"], 1)

                    def silu(j):
                        used_g(G_AT[j] + 1)
                        if j >= 2:
                            act.wait_ge(sem("h_ready"), g * PER_GROUP + (e0 + j - 1))
                        for b in range(nb):
                            bank = 4 + 2 * (j % 2) + b if dense else 6 + j % 2
                            last = fn(ex_s[:, j % 2, b, :], psum[:, bank, 0:256], ACT.Silu)
                        last.then_inc(sem("silu_ready"), 1)

                    def h_round(j):
                        act.wait_ge(sem("h_turned"), g * PER_GROUP + (e0 + j + 1))
                        if j >= 2:
                            act.wait_ge(half_used, g * PER_G + (base + D_AT[j - 2] + 1))
                        bank = 4 + 2 * (j % 2) if dense else 6 + j % 2
                        fn(ht_hi[:, j % 2, :, 0:P * nb],
                           psum[:, bank, 0:2 * P * nb].rearrange("p (f t) -> p f t", f=2), ACT.Copy)\
                            .then_inc(sem("ht_hi_ready"), 1)

                    silu(0)
                    silu(1)
                    h_round(0)
                    silu(2)
                    h_round(1)
                    silu(3)
                    h_round(2)
                    rnd(12)
                    h_round(3)
                    used_g(11)
                    assert mark[0] == PER_G + 3
                    if not dense:
                        fn(xt_hi[:, :, P:T], psum[:, 4:6, :].rearrange("p b (k t) -> p (b k) t", t=P), ACT.Copy)\
                            .then_inc(s["y_hi"], 1)

                with act.If(load < FAST_LIMIT + 1):
                    with act.Fori(0, GROUPS) as g:
                        group(g, False, None)
                with act.Else():
                    with act.Fori(0, GROUPS) as g:
                        group(g, True, None)
                done[0] += GROUPS * PER_G

            split_set(4)
            split_set(5)
            round_to(AT["E0"] + 3)
            split_set(6)
            split_set(7)
            experts(0)
            split_set(8)
            split_set(9)

            copy_unit("B_K0", pair(b_k, 0), 0)
            copy_unit("B_K2", pair(b_k, 2), 2)
            copy_unit("B_V0", mixed[:, 0, 0:512], 0)
            copy_unit("B_Q0", pair(b_q, 0), 3, HD_SCALE)
            copy_unit("B_Q2", pair(b_q, 2), 1, HD_SCALE)
            round_to(AT["B_QM"] + 1 + AHEAD)

            def sb_soft(p):
                act.wait_ge(sem("sb_z"), p + 1)
                if p >= 2:
                    act.wait_ge(sem("sb_sp"), p - 1)
                l = b_l[:, p % 2, :, :]
                own.link(fn(l, psum[:, 4 * (p % 2):4 * (p % 2) + 2, 0:384], ACT.Abs))
                own.link(fn(l, l, ACT.Exp, scale=-1.0))
                fn(l, l, ACT.Ln, bias=1.0).then_inc(sem("sb_soft"), 1)

            def sb_weights(p):
                act.wait_ge(sem("sb_log"), p + 1)
                if p >= 2:
                    act.wait_ge(sem("sb_o"), p - 1)
                ab = 4 * (p % 2) + 2
                fn(b_a[:, p % 2, :, :], psum[:, ab:ab + 2, 0:384], ACT.Exp).then_inc(sem("sb_a"), 1)

            sb_soft(0)
            sb_soft(1)
            for p in range(6):
                sb_weights(p)
                if p + 2 < 6:
                    sb_soft(p + 2)
            memory_attention(1)
            split_set(10)
            split_set(11)
            round_to(AT["E1"] + 3)
            split_set(12)
            split_set(13)
            experts(1)
            split_set(14)
            split_set(15)

            act.wait_ge(sem("f_abs"), 1)
            f2 = ar(4320, 32)
            own.link(fn(f2, f2, ACT.Exp, scale=-1.0))
            fn(f2, f2, ACT.Ln, bias=1.0).then_inc(sem("f_soft2"), 1)
            copy_unit("C_Q0", pair(c_q, 0), 0, HD_SCALE)
            copy_unit("C_Q2", pair(c_q, 2), 2, HD_SCALE)
            copy_unit("C_K0", pair(c_k, 0), 0)
            copy_unit("C_K2", pair(c_k, 2), 2)
            act.wait_ge(sem("c_neg"), 1)
            fn(perm_t[0:16, :], c_t[0:16, :], ACT.Copy).then_inc(sem("c_split"), 1)
            copy_unit("C_V0", mixed[:, 0, 0:512], 0)
            copy_unit("C_V1", mixed[:, 0, 512:1024], 2)

            def fox_probs(p):
                act.wait_ge(sem("fox_peak"), p + 1)
                if p >= 2:
                    act.wait_ge(sem("fox_turned"), p - 1)
                for hh in range(2):
                    for b in range(TB):
                        c = 4 * (p % 2) + 2 * hh + b
                        cols = slice(0, P) if b == 0 else slice(P, 384)
                        last = fn(c_p[:, p % 2, hh, cols], psum[:, 4 * (p % 2) + hh, cols], ACT.Exp,
                                  bias=peak[:, c:c + 1], accum_out=total[:, c:c + 1])
                last.then_inc(sem("fox_p"), 1)

            def fox_pt(p):
                act.wait_ge(sem("fox_turned"), p + 1)
                if p >= 2:
                    act.wait_ge(sem("fox_o"), p - 1)
                ab = 4 * (p % 2) + 2
                fn(c_pt[:, p % 2, :, :], psum[:, ab:ab + 2, 0:384], ACT.Copy).then_inc(sem("fox_pt"), 1)

            fox_probs(0)
            fox_probs(1)
            for p in range(8):
                fox_pt(p)
                if p + 2 < 8:
                    fox_probs(p + 2)
            split_set(16)
            split_set(17)
            round_to(AT["UP"] + 3)
            split_set(18)
            split_set(19)

            def ff_pair(j, i=None):
                h = AT["UP"] + 2 * j

                def at(n, per):
                    return n if i is None else i * per + n

                if i is None:
                    used(h)
                else:
                    for hh in (h + 3, ):
                        act.wait_ge(raw_in[hh % RING], at(32 * (hh // RING + 1), 32))
                        act.wait_ge(half_used, at(hh - RING + 1, 4))
                        fn(w_half(hh, w_hi), w_half(hh, raw), ACT.Copy).then_inc(hi_split, 1)
                    act.wait_ge(half_used, at(h + 1, 4))
                for c in range(2):
                    k = 2 * j + c
                    w2, bb = ((conv[:, t, k:k + 1] if i is None else conv[:, t, bass.ds(i * 4 + k, 1)])
                              for t in (2, 3))
                    last = fn(ff_t[:, j % 2, T * c:T * c + T], psum[:, 2 * (j % 2), T * c:T * c + T],
                              ACT.Identity, bias=bb, scale=w2)
                last.then_inc(sem("ff_mid"), 1)
                if i is None:
                    used(h + 1)
                else:
                    hh = h + 4
                    act.wait_ge(raw_in[hh % RING], at(32 * (hh // RING + 1), 32))
                    act.wait_ge(half_used, at(hh - RING + 1, 4))
                    fn(w_half(hh, w_hi), w_half(hh, raw), ACT.Copy).then_inc(hi_split, 1)
                act.wait_ge(sem("ff_conv"), at(j + 1, 2))
                fn(ff_g[:, j % 2, :], ff_t[:, j % 2, :], ACT.Gelu).then_inc(sem("ff_gelu"), 1)

            with act.Fori(0, FC // 4) as i:
                for j in range(2):
                    act.wait_ge(sem("ff_free"), i * 2 + (j + 1))
                    ff_pair(j, i)
            done[0] += 20
            act.wait_ge(sem("ff_free"), 11)
            ff_pair(10)

            def row_round(j):
                if j >= 4:
                    act.wait_ge(half_used, AT["DN"] + j - 3)
                q = 2 * (j % 4)
                fn(mt_hi[:, q:q + 2, :].rearrange("p k t -> p (k t)"), ff_a[:, 2 * j:2 * j + 2, :]
                   .rearrange("p k t -> p (k t)"), ACT.Copy).then_inc(sem("fa_hi"), 1)

            act.wait_ge(sem("ff_free"), FC // 2 + 2)
            for j in range(4):
                row_round(j)
            for j in range(FC // 2):
                round_to(AT["DN"] + j + 4)
                if j + 4 < FC // 2:
                    row_round(j + 4)
            act.wait_ge(half_used, AT["PP"])
            split_set(20, n=2)
            for r in range(4):
                act.wait_ge(sem("last_turned"), r + 1)
                fn(xt_hi[:, 2 * r:2 * r + 2, :].rearrange("p k t -> p (k t)"), psum[:, r % 2, :], ACT.Copy)\
                    .then_inc(sem("last_hi"), 1)
            for j in range(2):
                for b in range(TB):
                    n = 2 * j + b
                    if b == 0:
                        round_to(AT["PG"] + 2 * j + 2 + AHEAD)
                    act.wait_ge(sem("pl_sum"), n + 1)
                    fn(pl_s[:, n % 2, :], pl_s[:, n % 2, :], ACT.Sigmoid).then_inc(sem("pl_gate"), 1)

        @block.vector
        def _(dve):
            own = Tally(dve, sem("dve_own"))
            done = [0]

            def split_half(h, up):
                dve.wait_ge(hi_split, up)
                return dve.tensor_tensor(w_half(h, w_lo), w_half(h, raw), w_half(h, w_hi).bitcast(F32),
                                         ALU.subtract).then_inc(lo_split, 1)

            def split_to(upto):
                while done[0] < min(upto, HALVES):
                    h = done[0]
                    if h >= RING:
                        dve.wait_ge(half_used, h - RING + 1)
                    split_half(h, h + 1)
                    done[0] += 1

            def used(h):
                split_to(h + 1 + AHEAD)
                dve.wait_ge(half_used, h + 1)

            def rest(o, whole, hi):
                return dve.tensor_tensor(o, whole, hi.bitcast(F32), ALU.subtract)

            def split_set(s, n=4):
                dve.wait_ge(tr_hi, s + 1)
                if s in (2, 3):
                    hi, lo, c0 = mt_hi, mt_lo, 4 * (s - 2)
                elif s == 20:
                    hi, lo, c0 = mt_hi, mt_lo, 6
                else:
                    hi, lo, c0 = xt_hi, xt_lo, 4 * (s % 2)
                flat = "p k t -> p (k t)"
                rest(lo[:, c0:c0 + n, :].rearrange(flat),
                     psum[:, 4 + 2 * (s % 2):4 + 2 * (s % 2) + n // 2, :].rearrange("p b n -> p (b n)"),
                     hi[:, c0:c0 + n, :].rearrange(flat)).then_inc(tr_lo, 1)

            def copy_unit(name, dst, bank, scale=None):
                used(UNITS[name][0] + UNITS[name][1] - 1)
                src = psum[:, bank, 0:dst.free_size()]
                if scale is None:
                    ins = dve.tensor_copy(dst, src)
                else:
                    ins = dve.tensor_scalar(dst, src, scale, None, ALU.mult)
                ins.then_inc(drained_v, 1)

            def pair(v, p):
                return v[:, 2 * p:2 * p + 2, :].rearrange("p h t -> p (h t)")

            dve.wait_ge(consts, 1)
            dve.tensor_copy(ident_r[:], ident[:])
            dve.tensor_copy(bias_sb_r[:], bias_sb[:])
            dve.tensor_copy(bias_fox_r[:], bias_fox[:]).then_inc(consts_r, 1)
            dve.wait_ge(small_h, 1)
            rest(small_lo[:, 0:2, :].rearrange("p l n -> p (l n)"), small_w[:, 0:2, :].rearrange("p l n -> p (l n)"),
                 small_hi[:, 0:2, :].rearrange("p l n -> p (l n)"))
            rest(small_lo[:, 2, 0:128], small_w[:, 2, 0:128], small_hi[:, 2, 0:128]).then_inc(small_l, 1)
            split_set(0)
            split_set(1)

            for j in range(3):
                used(AT["A_F"] + j)
                dve.wait_ge(sem("f_soft"), j + 1)
                lf = pair(hq, j)
                own.link(dve.scalar_tensor_tensor(lf, psum[:, j, :], 0.0, pair(hk, j), ALU.min, ALU.subtract))
                dve.tensor_tensor(pair(hk, j), lf, psum[:, j, :], ALU.subtract).then_inc(drained_v, 1)
                dve.tensor_tensor_scan(pair(hG, j), reset64[:], lf, 0.0, ALU.mult, ALU.add)\
                    .then_inc(sem("g_ready"), 1)
                if j == 0:
                    split_set(2)
                    split_set(3)
            for j in range(3):
                split_to(AT["A_Q"] + j + 1 + AHEAD)
                dve.wait_ge(drained_a, drained_by(f"A_Q{j}", "a"))
                dve.tensor_scalar(pair(hq, j), pair(hq, j), HG_SCALE, None, ALU.mult).then_inc(sem("q_scaled"), 1)

            def chunks(p):
                return hG[:, 2 * p:2 * p + 2, :].rearrange("p h (c t) -> p h c t", t=64)

            def a_logs(st):
                p, i = divmod(st, STEPS)
                if st >= 3:
                    dve.wait_ge(sem("level_done"), st - 2)
                if i > len(LEVELS):
                    return
                x = hX[:, st % 3, :]
                if i == len(LEVELS):
                    xc = x.rearrange("p (h c t) -> p h c t", h=2, t=64)
                    G = chunks(p)
                    end = [G[:, :, c, 63:64].to_broadcast([P, 2, 64]) for c in range(4)]
                    own.did(dve.tensor_tensor(xc[:, :, 0, :], end[0], G[:, :, 0, :], ALU.subtract))
                    own.did(dve.tensor_tensor(xc[:, :, 1, :], end[1], G[:, :, 1, :], ALU.subtract))
                    own.did(dve.tensor_copy(xc[:, :, 2, :], G[:, :, 2, :]))
                    own.did(dve.tensor_tensor(xc[:, :, 3, :], G[:, :, 3, :], end[2], ALU.add))
                    own.settle()
                    dve.tensor_tensor(xc[:, :, 0, :], xc[:, :, 0, :], end[1], ALU.add).then_inc(sem("x_logs"), 1)
                    return
                L = LEVELS[i]
                n = 512 // (2 * L)
                xv = x.rearrange("p (n u t) -> p n u t", u=2, t=L)
                G = pair(hG, p).rearrange("p (n u t) -> p n u t", u=2, t=L)
                anchor = G[:, :, 0, L - 1:L].to_broadcast([P, n, L])
                if L == 64:
                    dve.tensor_copy(xv[:, :, 1, :], G[:, :, 1, :])
                else:
                    dve.tensor_tensor(xv[:, :, 1, :], G[:, :, 1, :], anchor, ALU.subtract)
                dve.tensor_tensor(xv[:, :, 0, :], anchor, G[:, :, 0, :], ALU.subtract).then_inc(sem("x_logs"), 1)

            def a_scale(st):
                p, i = divmod(st, STEPS)
                if i > len(LEVELS):
                    return
                dve.wait_ge(sem("x_exp"), decayed(st))
                dve.wait_ge(sem("k_ready"), p + 1)
                x, q, k = hX[:, st % 3, :], hq[:, 2 * p:2 * p + 2, :], hk[:, 2 * p:2 * p + 2, :]
                if i == len(LEVELS):
                    x3 = x.rearrange("p (h t) -> p h t", h=2)
                    lo, up = slice(0, P), slice(P, T)
                    dve.tensor_tensor(x3[:, :, up], x3[:, :, up], q[:, :, up], ALU.mult)
                    dve.tensor_tensor(x3[:, :, lo], x3[:, :, lo], k[:, :, lo], ALU.mult).then_inc(sem("x_ready"), 1)
                    return
                L = LEVELS[i]
                v = [w.rearrange("p (n u t) -> p n u t", u=2, t=L) for w in (x, pair(hq, p), pair(hk, p))]
                dve.tensor_tensor(v[0][:, :, 1, :], v[0][:, :, 1, :], v[1][:, :, 1, :], ALU.mult)
                dve.tensor_tensor(v[0][:, :, 0, :], v[0][:, :, 0, :], v[2][:, :, 0, :], ALU.mult)\
                    .then_inc(sem("x_ready"), 1)

            def a_merge(st):
                p, i = divmod(st, STEPS)
                dve.wait_ge(sem("level_done"), st + 1)
                bank = psum[:, 4 + st % 4, :]
                if i == len(LEVELS):
                    dve.tensor_copy(pair(hSx, p), bank[:, 0:256]).then_inc(sem("merged"), 1)
                    return
                m = level_mask[:, i if i < len(LEVELS) else len(LEVELS), :]
                dst = hS[:, 4 * p:4 * p + 4, :]
                if st >= 1:
                    dve.wait_ge(sem("merged"), st)
                dve.copy_predicated(dst, m.rearrange("p (o t) -> p o t", o=1).to_broadcast([P, 4, P]),
                                    bank.rearrange("p (c t) -> p c t", c=4)).then_inc(sem("merged"), 1)

            def a_drain(name):
                h, n, banks, who = UNITS[name]
                if "v" not in who:
                    return
                used(h + n - 1)
                if name == "A_IG0":
                    for b in range(TB):
                        last = dve.tensor_copy(mixed[:, b, 0:512], psum[:, banks[b], :])
                elif name == "A_IG1":
                    for b in range(TB):
                        last = dve.tensor_copy(mixed[:, b, 512:768], psum[:, banks[b], 0:256])
                else:
                    last = dve.tensor_copy(mem_v[:, int(name[2]), :, :].rearrange("p m c -> p (m c)"),
                                           psum[:, banks[0], :])
                last.then_inc(drained_v, 1)

            dve.wait_ge(sem("q_scaled"), 3)
            dve.wait_ge(sem("g_ready"), 3)
            dve.wait_ge(consts, 2)
            for n, h in enumerate(A_HALVES):
                for st in range(3 * n, min(3 * n + 3, N_STEPS)):
                    if st == 0:
                        a_logs(0)
                    if st + 1 < N_STEPS:
                        a_logs(st + 1)
                    a_scale(st)
                    if st:
                        a_merge(st - 1)
                if 3 * n < N_STEPS <= 3 * n + 3:
                    a_merge(N_STEPS - 1)
                if h - 1 in ends and h > A_HALVES[0]:
                    a_drain(ends[h - 1])
                split_to(h + AHEAD)
            a_drain(ends[A_HALVES[-1]])
            dve.wait_ge(drained_a, drained_by("A_IG2", "a"))
            dve.wait_ge(gnorm_in, 16)
            dve.tensor_tensor(hg[:], hg[:], gain[:, 0, 0:SEQ_W].rearrange("p (o n) -> p o n", o=1)
                              .to_broadcast([P, TB, SEQ_W]), ALU.mult).then_inc(sem("gate_ready"), 1)
            for p in range(3):
                dve.wait_ge(sem("squared"), p + 1)
                c = slice(4 * p, 4 * p + 4)
                own.link(dve.tensor_reduce(peak[:, 32 + 4 * p:36 + 4 * p],
                                           sq[:, p, :].rearrange("p (c t) -> p c t", c=4), AX, ALU.add))
                dve.tensor_scalar(var_eps[:, c], peak[:, 32 + 4 * p:36 + 4 * p], 1.0 / P, RMS_EPS, ALU.mult, ALU.add)\
                    .then_inc(var_ready, 1)
            dve.wait_ge(sem("gate_ready"), 1)
            dve.wait_ge(sem("hg_out"), 3)
            for p in range(3):
                dve.wait_ge(rstd_ready, p + 1)
                for hh in range(2):
                    h = 2 * p + hh
                    for b in range(TB):
                        c = 2 * hh + b
                        last = dve.scalar_tensor_tensor(mixed[:, b, P * h:P * h + P], psum[:, p, P * c:P * c + P],
                                                        rstd[:, 4 * p + c:4 * p + c + 1], hg[:, b, P * h:P * h + P],
                                                        ALU.mult, ALU.mult)
            last.then_inc(sem("mixed_ready"), 1)

            def memory_attention(layer):
                for h in range(4):
                    n = 4 * layer + h
                    dve.wait_ge(sem("mem_scores"), n + 1)
                    c = slice(2 * h, 2 * h + 2)
                    own.link(dve.tensor_reduce(peak[:, c], psum[:, 4 + h, :].rearrange("p (b m) -> p b m", b=2),
                                               AX, ALU.max))
                    dve.tensor_scalar(peak[:, c], peak[:, c], -1.0, None, ALU.mult).then_inc(sem("mem_peak"), 1)
                dve.wait_ge(sem("mem_prob"), 4 * layer + 4)
                own.link(dve.reciprocal(total[:, 0:8], total[:, 0:8]))
                dve.wait_ge(sem("mem_out"), 4 * layer + 4)
                inv = total[:, 0:8].rearrange("p (h b) -> p b h", b=2)
                for b in range(TB):
                    last = dve.tensor_tensor(
                        mixed[:, b, SEQ_W:D].rearrange("p (h d) -> p h d", h=4),
                        psum[:, 3, 256 * b:256 * b + 256].rearrange("p (h d) -> p h d", h=4),
                        inv[:, b, :].rearrange("p (h o) -> p h o", o=1).to_broadcast([P, 4, 64]), ALU.mult)
                last.then_inc(sem("mixed_ready"), 1)

            memory_attention(0)

            def norm(n, alpha, ready, value, drains):
                dve.wait_ge(ready, value)
                first = 3 + 2 * n
                for b in range(TB):
                    for c in range(2):
                        cs = slice(512 * c, 512 * c + 512)
                        own.did(dve.scalar_tensor_tensor(x_res[:, b, cs], x_res[:, b, cs], alpha, psum[:, 2 * c + b, :],
                                                         ALU.mult, ALU.add))
                    own.settle()
                    for c in range(2):
                        own.did(dve.bn_stats(stats[:, b, c, :], x_res[:, b, 512 * c:512 * c + 512]))
                    own.settle()
                    own.link(dve.bn_aggr(mv[:, b, :], stats[:, b, :, :].rearrange("p c s -> p (c s)")))
                    dve.tensor_scalar(var_eps[:, b:b + 1], mv[:, b, 1:2], LN_EPS, None, ALU.add)\
                        .then_inc(var_ready, 1)
                if drains:
                    for _ in range(drains):
                        dve.nop().then_inc(drained_v, 1)
                dve.wait_ge(gain_in, 32 * (n + 1))
                for b in range(TB):
                    dve.wait_ge(rstd_ready, first + b + 1)
                    x = x_res[:, b, :]
                    own.link(dve.tensor_scalar(x, x, mv[:, b, 0:1], rstd[:, b:b + 1], ALU.subtract, ALU.mult))
                    own.link(dve.tensor_tensor(x, x, gain[:, 0, :], ALU.mult))
                    dve.tensor_tensor(x, x, gain[:, 1, :], ALU.add).then_inc(ln_done, 1)

            def first_of(o, x, m):
                own.link(dve.tensor_tensor(r_eq.rearrange("p (b e) -> p b e", b=2), x,
                                           m.rearrange("p (b o) -> p b o", o=1).to_broadcast([P, 2, 4]), ALU.is_equal))
                own.link(dve.tensor_tensor_scan(r_cum, reset4[:], r_eq, 0.0, ALU.mult, ALU.add))
                own.link(dve.scalar_tensor_tensor(o.rearrange("p b e -> p (b e)"), r_cum, 1.0, r_eq,
                                                  ALU.is_equal, ALU.mult))

            def wide(v):
                return v.rearrange("p (b o) -> p b o", o=1).to_broadcast([P, 2, 4])

            def route(layer):
                dve.wait_ge(sem("x_rounded"), layer + 1)
                rest(mt_lo[:].rearrange("p k t -> p (k t)"), x_res[:].rearrange("p b d -> p (b d)"),
                     mt_hi[:].rearrange("p k t -> p (k t)")).then_inc(sem("x_rest"), 1)
                dve.wait_ge(sem("logits"), layer + 1)
                dve.wait_ge(small_in, 80)
                own.link(dve.tensor_tensor(r_log, psum[:, 0, 0:40].rearrange("p (b e) -> p b e", b=2),
                                           r_bias[:, layer, :].rearrange("p (o e) -> p o e", o=1)
                                           .to_broadcast([P, 2, 20]), ALU.add))
                own.link(dve.tensor_reduce(r_m[:, 0, :], r_log[:, :, 0:4], AX, ALU.max))
                dve.tensor_tensor(r_g, r_log[:, :, 0:4], wide(r_m[:, 0, :]), ALU.subtract)\
                    .then_inc(sem("group_log"), 1)
                dve.wait_ge(sem("group_exp"), layer + 1)
                own.did(dve.tensor_reduce(r_m[:, 1, :], r_g, AX, ALU.max))
                own.link(dve.tensor_reduce(r_m[:, 2, :], r_g, AX, ALU.add))
                own.link(dve.reciprocal(r_m[:, 2, :], r_m[:, 2, :]))
                own.did(dve.tensor_tensor(r_m[:, 3, :], r_m[:, 1, :], r_m[:, 2, :], ALU.mult))
                first_of(r_og, r_g, r_m[:, 1, :])
                dve.nop().then_inc(sem("group_ready"), 1)
                own.link(dve.tensor_tensor(
                    r_t16, r_log[:, :, 4:20].rearrange("p b (g e) -> p b g e", g=4),
                    r_og.rearrange("p b (g o) -> p b g o", o=1).to_broadcast([P, 2, 4, 4]), ALU.mult))
                own.link(dve.tensor_reduce(r_i4, r_t16.rearrange("p b g e -> p b e g"), AX, ALU.add))
                own.link(dve.tensor_reduce(r_m[:, 4, :], r_i4, AX, ALU.max))
                dve.tensor_tensor(r_e, r_i4, wide(r_m[:, 4, :]), ALU.subtract).then_inc(sem("expert_log"), 1)
                dve.wait_ge(sem("expert_exp"), layer + 1)
                own.link(dve.tensor_reduce(r_m[:, 5, :], r_e, AX, ALU.max))
                first_of(r_o1, r_e, r_m[:, 5, :])
                own.link(dve.scalar_tensor_tensor(r_e2, r_o1, -2.0, r_e, ALU.mult, ALU.add))
                own.link(dve.tensor_reduce(r_m[:, 6, :], r_e2, AX, ALU.max))
                first_of(r_o2, r_e2, r_m[:, 6, :])
                own.link(dve.tensor_tensor(r_m[:, 7, :], r_m[:, 5, :], r_m[:, 6, :], ALU.add))
                own.link(dve.reciprocal(r_m[:, 7, :], r_m[:, 7, :]))
                own.did(dve.tensor_tensor(r_m[:, 7, :], r_m[:, 7, :], r_m[:, 3, :], ALU.mult))
                own.link(dve.tensor_tensor(r_o1, r_o1, r_o2, ALU.add))
                own.link(dve.tensor_tensor(r_g4, r_e, r_o1, ALU.mult))
                own.link(dve.tensor_tensor(r_g4, r_g4, wide(r_m[:, 7, :]), ALU.mult))
                own.did(dve.tensor_tensor(
                    r_gate, r_g4.rearrange("p b (o e) -> p b o e", o=1).to_broadcast([P, 2, 4, 4]),
                    r_og.rearrange("p b (g o) -> p b g o", o=1).to_broadcast([P, 2, 4, 4]), ALU.mult))
                dve.wait_ge(sem("counted"), layer + 1)
                own.did(dve.tensor_copy(r_pos.rearrange("p n g -> p (n g)"), psum[:, 1, 0:12]))
                own.settle()
                own.link(dve.tensor_reduce(r_mx, r_pos[:, 2, :], AX, ALU.max))
                own.link(dve.tensor_copy(load_max[:], r_mx))
                dve.nop().then_inc(sem("routed"), 1)

            def experts(layer):
                base, e0 = AT[f"E{layer}"], 16 * layer
                s = {n: sem(f"{n}{layer}") for n in ("perm_ready", "gathered", "xg_hi", "xg_lo", "y_hi", "y_lo")}
                split_to(base + 3)
                load = dve.value_load(load_max[0:1, 0:1], min_val=0, max_val=T)

                def group(g, dense):
                    nb = TB if dense else 1
                    mark = [3]

                    def spl(upto):
                        while mark[0] < upto:
                            h = base + mark[0]
                            dve.wait_ge(half_used, g * PER_G + (h - RING + 1))
                            split_half(h, g * PER_G + (h + 1))
                            mark[0] += 1

                    def used_g(n):
                        spl(n + 1 + AHEAD)
                        dve.wait_ge(half_used, g * PER_G + (base + n + 1))

                    if not dense:
                        for b in range(TB):
                            last = dve.tensor_scalar(perm[:, b, :], slot_no[:],
                                                     r_pos[:, b, bass.ds(g, 1)], r_og[:, b, bass.ds(g, 1)],
                                                     ALU.is_equal, ALU.mult)
                        last.then_inc(s["perm_ready"], 1)
                        dve.wait_ge(s["xg_hi"], g + 1)
                        rest(xt_lo[:, :, 0:P], psum[:, 4:6, :].rearrange("p b (k t) -> p (b k) t", t=P),
                             xt_hi[:, :, 0:P]).then_inc(s["xg_lo"], 1)

                    def hidden(j):
                        used_g(G_AT[j] + 1)
                        dve.wait_ge(sem("silu_ready"), g * PER_GROUP + (e0 + j + 1))
                        if j >= 2:
                            dve.wait_ge(sem("h_turned"), g * PER_GROUP + (e0 + j - 1))
                        for b in range(nb):
                            bank = 4 + 2 * (j % 2) + b if dense else 6 + j % 2
                            gate = (r_gate[:, b, bass.ds(g, 1), j:j + 1].rearrange("p a e -> p (a e)") if dense
                                    else slot_gate[:, j:j + 1])
                            last = dve.scalar_tensor_tensor(ex_h[:, j % 2, b, :], psum[:, bank, 256:512], gate,
                                                            ex_s[:, j % 2, b, :], ALU.mult, ALU.mult)
                        last.then_inc(sem("h_ready"), 1)

                    def h_rest(j):
                        dve.wait_ge(sem("ht_hi_ready"), g * PER_GROUP + (e0 + j + 1))
                        bank = 4 + 2 * (j % 2) if dense else 6 + j % 2
                        rest(ht_lo[:, j % 2, :, 0:P * nb],
                             psum[:, bank, 0:2 * P * nb].rearrange("p (f t) -> p f t", f=2),
                             ht_hi[:, j % 2, :, 0:P * nb]).then_inc(sem("ht_lo_ready"), 1)

                    hidden(0)
                    hidden(1)
                    h_rest(0)
                    hidden(2)
                    h_rest(1)
                    hidden(3)
                    h_rest(2)
                    spl(12)
                    h_rest(3)
                    used_g(11)
                    assert mark[0] == PER_G + 3
                    if not dense:
                        dve.wait_ge(s["y_hi"], g + 1)
                        rest(xt_lo[:, :, P:T], psum[:, 4:6, :].rearrange("p b (k t) -> p (b k) t", t=P),
                             xt_hi[:, :, P:T]).then_inc(s["y_lo"], 1)

                with dve.If(load < FAST_LIMIT + 1):
                    with dve.Fori(0, GROUPS) as g:
                        group(g, False)
                with dve.Else():
                    with dve.Fori(0, GROUPS) as g:
                        group(g, True)
                done[0] += GROUPS * PER_G

            split_set(4)
            split_set(5)
            split_to(AT["O0"] + 4)
            norm(0, ALPHA, half_used, AT["O0"] + 4, 2)
            split_to(AT["E0"] + 3)
            split_set(6)
            split_set(7)
            route(0)
            experts(0)
            norm(1, ALPHA, sem("moe_done"), 1, 0)
            split_set(8)
            split_set(9)

            copy_unit("B_K1", pair(b_k, 1), 1)
            copy_unit("B_V0", mixed[:, 1, 0:512], 1)
            used(UNITS["B_V1"][0])
            dve.tensor_copy(mixed[:, :, 512:768], psum[:, 2, :].rearrange("p (b n) -> p b n", b=2))\
                .then_inc(drained_v, 1)
            copy_unit("B_Q1", pair(b_q, 1), 0, HD_SCALE)
            copy_unit("B_QM", b_qm[:].rearrange("p c t -> p (c t)"), 2, HD_SCALE)

            def sb_sp(p):
                dve.wait_ge(sem("sb_soft"), p + 1)
                if p >= 2:
                    dve.wait_ge(sem("sb_log"), p - 1)
                zb = 4 * (p % 2)
                dve.scalar_tensor_tensor(b_s[:, p % 2, :, :], psum[:, zb:zb + 2, 0:384], 0.0, b_l[:, p % 2, :, :],
                                         ALU.max, ALU.add).then_inc(sem("sb_sp"), 1)

            def sb_take(p):
                dve.wait_ge(sem("sb_o"), p + 1)
                ab = 4 * (p % 2) + 2
                dve.tensor_copy(mixed[:, :, P * p:P * p + P].rearrange("p b (h d) -> p h b d", h=2),
                                psum[:, ab:ab + 2, 384:512].rearrange("p h (b d) -> p h b d", b=2))\
                    .then_inc(sem("sb_o_out"), 1)

            for p in range(6):
                sb_sp(p)
                if p:
                    sb_take(p - 1)
            sb_take(5)
            dve.wait_ge(sem("sb_o_out"), 6)
            dve.nop().then_inc(sem("mixed_ready"), 1)
            memory_attention(1)
            split_set(10)
            split_set(11)
            split_to(AT["O1"] + 4)
            norm(2, ALPHA, half_used, AT["O1"] + 4, 2)
            split_to(AT["E1"] + 3)
            split_set(12)
            split_set(13)
            route(1)
            experts(1)
            norm(3, ALPHA, sem("moe_done"), 2, 0)
            split_set(14)
            split_set(15)

            f1, f2 = ar(4288, 32), ar(4320, 32)
            dve.wait_ge(sem("f_logits"), 1)
            own.link(dve.tensor_tensor(f1.rearrange("p (b h) -> p b h", b=2),
                                       psum[:, 4, 0:32].rearrange("p (b h) -> p b h", b=2),
                                       f_bias[:].rearrange("p (o h) -> p o h", o=1).to_broadcast([P, 2, 16]), ALU.add))
            dve.scalar_tensor_tensor(f2, f1, -1.0, f1, ALU.mult, ALU.max).then_inc(sem("f_abs"), 1)
            dve.wait_ge(sem("f_soft2"), 1)
            dve.scalar_tensor_tensor(c_f.rearrange("p b h -> p (b h)"), f1, 0.0, f2, ALU.min, ALU.subtract)\
                .then_inc(sem("f_log"), 1)
            copy_unit("C_Q1", pair(c_q, 1), 1, HD_SCALE)
            copy_unit("C_Q3", pair(c_q, 3), 3, HD_SCALE)
            dve.wait_ge(sem("c_sum"), 1)
            dve.tensor_copy(c_c.rearrange("p b h -> p (b h)"), psum[:, 5, 0:32]).then_inc(sem("c_out"), 1)
            copy_unit("C_K1", pair(c_k, 1), 1)
            dve.wait_ge(sem("c_turned"), 1)
            dve.tensor_scalar(c_t[0:16, :], psum[0:16, 6, 0:T], -1.0, None, ALU.mult).then_inc(sem("c_neg"), 1)
            copy_unit("C_K3", pair(c_k, 3), 3)
            dve.wait_ge(sem("c_split"), 1)
            rest(perm[0:16, :, :].rearrange("p b t -> p (b t)"), c_t[0:16, :], perm_t[0:16, :])\
                .then_inc(sem("c_split"), 1)
            copy_unit("C_V0", mixed[:, 1, 0:512], 1)
            copy_unit("C_V1", mixed[:, 1, 512:1024], 3)

            def fox_peak(p):
                dve.wait_ge(sem("fox_s"), p + 1)
                sc = psum[:, 4 * (p % 2):4 * (p % 2) + 2, :]
                c = 4 * (p % 2)
                pk = peak[:, c:c + 4].rearrange("p (h b) -> p h b", b=2)
                own.did(dve.tensor_reduce(pk[:, :, 0:1], sc[:, :, 0:P], AX, ALU.max))
                own.did(dve.tensor_reduce(pk[:, :, 1:2], sc[:, :, P:384], AX, ALU.max))
                own.settle()
                dve.tensor_scalar(peak[:, c:c + 4], peak[:, c:c + 4], -1.0, None, ALU.mult)\
                    .then_inc(sem("fox_peak"), 1)

            def fox_take(p):
                c = 4 * (p % 2)
                dve.wait_ge(sem("fox_o"), p + 1)
                own.link(dve.reciprocal(peak[:, 16 + c:20 + c], total[:, c:c + 4]))
                ab = 4 * (p % 2) + 2
                for hh in range(2):
                    inv = peak[:, 16 + c + 2 * hh:18 + c + 2 * hh]
                    h = 2 * p + hh
                    last = dve.tensor_tensor(mixed[:, :, 64 * h:64 * h + 64],
                                             psum[:, ab + hh, 384:512].rearrange("p (b d) -> p b d", b=2),
                                             inv.rearrange("p (b o) -> p b o", o=1).to_broadcast([P, 2, 64]),
                                             ALU.mult)
                last.then_inc(sem("fox_o_out"), 1)

            fox_peak(0)
            fox_peak(1)
            for p in range(1, 8):
                fox_take(p - 1)
                if p + 1 < 8:
                    fox_peak(p + 1)
            fox_take(7)
            dve.wait_ge(sem("fox_o_out"), 8)
            dve.nop().then_inc(sem("mixed_ready"), 2)
            split_set(16)
            split_set(17)
            split_to(AT["O2"] + 4)
            norm(4, ALPHA_2, half_used, AT["O2"] + 4, 2)
            split_to(AT["UP"] + 3)
            split_set(18)
            split_set(19)

            def ff_pair(j, i=None):
                h = AT["UP"] + 2 * j

                def at(n, per):
                    return n if i is None else i * per + n

                if i is None:
                    split_to(h + 1 + AHEAD)
                else:
                    hh = h + 3
                    dve.wait_ge(half_used, at(hh - RING + 1, 4))
                    split_half(hh, at(hh + 1, 4))
                dve.wait_ge(sem("ff_mid"), at(j + 1, 2))
                for lag, tap in ((1, 1), (2, 0)):
                    for c in range(2):
                        k = 2 * j + c
                        w = conv[:, tap, k:k + 1] if i is None else conv[:, tap, bass.ds(i * 4 + k, 1)]
                        o = ff_t[:, j % 2, T * c + lag:T * c + T]
                        last = dve.scalar_tensor_tensor(o, psum[:, 2 * (j % 2), T * c:T * c + T - lag], w, o,
                                                        ALU.mult, ALU.add)
                        if lag == 1:
                            loop_own.did(last)
                    if lag == 1:
                        loop_own.settle()
                last.then_inc(sem("ff_conv"), 1)
                if i is None:
                    split_to(h + 2 + AHEAD)
                    dve.wait_ge(half_used, h + 2)
                else:
                    hh = h + 4
                    dve.wait_ge(half_used, at(hh - RING + 1, 4))
                    split_half(hh, at(hh + 1, 4))
                    dve.wait_ge(half_used, at(h + 2, 4))
                dve.wait_ge(sem("ff_gelu"), at(j + 1, 2))
                fa = ff_a[:, 2 * j:2 * j + 2, :] if i is None else ff_a[:, bass.ds(i * 4 + 2 * j, 2), :]
                dve.tensor_tensor(fa.rearrange("p k t -> p (k t)"), ff_g[:, j % 2, :], psum[:, 2 * (j % 2) + 1, :],
                                  ALU.mult).then_inc(sem("ff_free"), 1)

            loop_own = Tally(dve, sem("conv_own"))
            dve.nop().then_inc(sem("ff_free"), 2)
            with dve.Fori(0, FC // 4) as i:
                loop_own.enter(i, 4)
                for j in range(2):
                    ff_pair(j, i)
            loop_own.leave(FC // 4)
            done[0] += 20
            ff_pair(10)
            dve.wait_ge(sem("ff_free"), FC // 2 + 2)

            def row_rest(j):
                dve.wait_ge(sem("fa_hi"), j + 1)
                q = 2 * (j % 4)
                rest(mt_lo[:, q:q + 2, :].rearrange("p k t -> p (k t)"),
                     ff_a[:, 2 * j:2 * j + 2, :].rearrange("p k t -> p (k t)"),
                     mt_hi[:, q:q + 2, :].rearrange("p k t -> p (k t)")).then_inc(sem("fa_lo"), 1)

            for j in range(4):
                row_rest(j)
            for j in range(FC // 2):
                split_to(AT["DN"] + j + 4)
                if j + 4 < FC // 2:
                    row_rest(j + 4)
            split_set(20, n=2)
            split_to(AT["PP"] + 1)
            norm(5, ALPHA_2, half_used, AT["DN"] + 11, 0)
            for r in range(4):
                dve.wait_ge(sem("last_hi"), r + 1)
                rest(xt_lo[:, 2 * r:2 * r + 2, :].rearrange("p k t -> p (k t)"), psum[:, r % 2, :],
                     xt_hi[:, 2 * r:2 * r + 2, :].rearrange("p k t -> p (k t)")).then_inc(sem("last_lo"), 1)
            dve.wait_ge(gain_in, 32 * 6 + 16)
            for j in range(2):
                used(AT["PG"] + 2 * j + 1)
                for b in range(TB):
                    n = 2 * j + b
                    cs = slice(512 * j, 512 * j + 512)
                    dve.tensor_tensor(pl_s[:, n % 2, :], psum[:, 2 * j + b, :], gain[:, 0, cs], ALU.add)\
                        .then_inc(sem("pl_sum"), 1)
                for b in range(TB):
                    n = 2 * j + b
                    cs = slice(512 * j, 512 * j + 512)
                    dve.wait_ge(sem("pl_gate"), n + 1)
                    own.link(dve.tensor_tensor(pl_s[:, n % 2, :], pl_s[:, n % 2, :], psum[:, 4 + 2 * j + b, :], ALU.mult))
                    own.link(dve.tensor_tensor(x_res[:, b, cs], x_res[:, b, cs], pl_s[:, n % 2, :], ALU.add))
            dve.nop().then_inc(sem("result"), TB)


_FULL = ["x", "mem", "a_w_in", "a_gnorm", "b_w_in", "w_kv_shared", "w_mem_kv", "w_o", "ln_mix_g", "ln_mix_b",
         "ln_ffn_g", "ln_ffn_b", "w_gate", "w_up", "w_down", "p_2", "attn_w_in_2", "attn_b_f_2", "attn_w_out_2",
         "ln_mix_g_2", "ln_mix_b_2", "ffn_w_up_2", "ffn_w_down_2", "ln_ffn_g_2", "ln_ffn_b_2", "ple_w_proj_2",
         "ple_w_gate_2", "ple_b_gate_2"]


def kernel(**inputs):
    import numpy as np
    import concourse.bacc as bacc
    from concourse import mybir as mb
    from concourse.bass_utils import run_bass_kernel_spmd

    arrays = {n: np.ascontiguousarray(inputs[n]) for n in _FULL}

    def by_row(w):
        n = w.shape[-1]
        return np.ascontiguousarray(np.asarray(w).reshape(8, 128, n).transpose(1, 0, 2).reshape(128, 8 * n))

    router = [np.concatenate([np.asarray(inputs["w_group"][l]), np.asarray(inputs["w_router"][l])], axis=1)
              for l in range(2)]
    arrays["r_weights"] = np.ascontiguousarray(np.stack([by_row(r) for r in router], axis=1))
    arrays["r_bias"] = np.concatenate([np.asarray(inputs["b_group"]), np.asarray(inputs["b_router"])], axis=1)
    arrays["f_weights"] = by_row(np.asarray(inputs["attn_w_in_2"])[0][:, 3 * 1024:])
    taps = np.concatenate([np.asarray(inputs["ffn_conv_w_2"])[0], np.asarray(inputs["ffn_conv_b_2"])], axis=0)
    arrays["conv"] = np.ascontiguousarray(taps.reshape(4, 22, 128).transpose(2, 0, 1))

    nc = bacc.Bacc("TRN2", target_bir_lowering=False, num_devices=1, dynamic_dma_scratch_size=1024)
    a, named = {}, {}
    for name, v in arrays.items():
        named[f"in_{name}"] = v
        a[name] = nc.dram_tensor(f"in_{name}", v.shape, mb.dt.from_np(v.dtype), kind="ExternalInput").ap()
    out = nc.dram_tensor("out_0", (1, 256, 1024), mb.dt.from_np(np.dtype("float32")), kind="ExternalOutput").ap()
    build(nc, a, out)
    r = run_bass_kernel_spmd(nc, [named], core_ids=[0])
    return r.results[0]["out_0"]
```

```python
from contextlib import ExitStack

import concourse.bass as bass
from concourse import mybir

F32 = mybir.dt.float32
F32R = mybir.dt.float32r
I32 = mybir.dt.int32
I8 = mybir.dt.int8
ALU = mybir.AluOpType
ACT = mybir.ActivationFunctionType
AX = mybir.AxisListType.X

P = 128
D = 1024
T = 256
TB = T // P
KC = D // P
SEQ_W = 768
MEM_W = 256
HG_HEADS = 6
SB_HEADS = 12
FOX_HEADS = 16
GROUPS = 4
PAIRS = GROUPS // 2
PER_GROUP = 4
EXPERTS = GROUPS * PER_GROUP
FFN = 2816
FC = FFN // P
ALPHA = 4 ** 0.25
ALPHA_2 = 2 ** 0.25
LN_EPS = 1e-5
RMS_EPS = 1e-6
HG_SCALE = 128 ** -0.5
HD_SCALE = 0.125
NEG = -1e30
HALF = 2048
RING = 4
AHEAD = 3
LEVELS = (64, 32, 16, 8, 4, 2, 1)
STEPS = len(LEVELS) + 2

_sizes = [("A_F", 3), ("A_Q", 3), ("A_IG", 6), ("A_QM", 1), ("MK0", 1), ("MV0", 1),
          ("O0", 4), ("MK1", 1), ("MV1", 1), ("E0", 48), ("B_K", 3), ("B_V", 3), ("B_Q", 3), ("B_QM", 1), ("O1", 4), ("E1", 48),
          ("C_Q", 4), ("C_K", 4), ("C_V", 4), ("O2", 4), ("UP", 22), ("DN", 11), ("PP", 1), ("PG", 4)]
AT = {}
_n = 0
for _name, _k in _sizes:
    AT[_name] = _n
    _n += _k
HALVES = _n
GROUP_ORDER = [("G", 0, 0), ("G", 0, 1), ("G", 1, 0), ("G", 1, 1), ("G", 2, 0), ("G", 2, 1), ("D", 0, 0),
               ("G", 3, 0), ("G", 3, 1), ("D", 1, 0), ("D", 2, 0), ("D", 3, 0)]
G_AT = {0: 0, 1: 2, 2: 4, 3: 7}
D_AT = {0: 6, 1: 9, 2: 10, 3: 11}
PER_G = len(GROUP_ORDER)

UNITS = {}
_order = []


def _unit(name, h, n, banks, who):
    UNITS[name] = (h, n, banks, who)
    _order.append(name)


for _j in range(3):
    _unit(f"A_F{_j}", AT["A_F"] + _j, 1, [_j], "v")
for _j in range(3):
    _unit(f"A_Q{_j}", AT["A_Q"] + _j, 1, [(3 + _j) % 4], "a")
for _j, _w in enumerate("aaa"):
    _unit(f"A_IG{_j}", AT["A_IG"] + 2 * _j, 2, [[2, 3], [0, 1], [2, 3]][_j], _w)
_unit("A_QM", AT["A_QM"], 1, [0], "a")
_unit("MK0", AT["MK0"], 1, [1], "a")
_unit("MV0", AT["MV0"], 1, [2], "a")
_unit("O00", AT["O0"], 2, [0, 1], "v")
_unit("O01", AT["O0"] + 2, 2, [2, 3], "v")
_unit("MK1", AT["MK1"], 1, [4], "a")
_unit("MV1", AT["MV1"], 1, [5], "a")
for _j in range(3):
    _unit(f"B_K{_j}", AT["B_K"] + _j, 1, [_j], "ava"[_j])
_unit("B_V0", AT["B_V"], 2, [0, 1], "av")
_unit("B_V1", AT["B_V"] + 2, 1, [2], "v")
for _j in range(3):
    _unit(f"B_Q{_j}", AT["B_Q"] + _j, 1, [[3, 0, 1][_j]], "ava"[_j])
_unit("B_QM", AT["B_QM"], 1, [2], "v")
_unit("O10", AT["O1"], 2, [0, 1], "v")
_unit("O11", AT["O1"] + 2, 2, [2, 3], "v")
for _j in range(4):
    _unit(f"C_Q{_j}", AT["C_Q"] + _j, 1, [_j], "avav"[_j])
for _j in range(4):
    _unit(f"C_K{_j}", AT["C_K"] + _j, 1, [_j], "avav"[_j])
for _j in range(2):
    _unit(f"C_V{_j}", AT["C_V"] + 2 * _j, 2, [2 * _j, 2 * _j + 1], "av")
_unit("O20", AT["O2"], 2, [0, 1], "v")
_unit("O21", AT["O2"] + 2, 2, [2, 3], "v")


def drained_by(name, who):
    upto = _order[:_order.index(name) + 1]
    return sum(who in UNITS[u][3] for u in upto)


def free_waits(name):
    i = _order.index(name)
    last = {}
    for u in _order[:i]:
        for b in UNITS[u][2]:
            last[b] = u
    return sorted({last[b] for b in UNITS[name][2] if b in last}, key=_order.index)


class Tally:

    def __init__(self, eng, sem):
        self.eng, self.sem, self.n, self.dyn = eng, sem, 0, None

    def did(self, ins):
        ins.then_inc(self.sem, 1)
        self.n += 1
        return ins

    def settle(self, but=0):
        n = self.n - but
        self.eng.wait_ge(self.sem, n if self.dyn is None else self.dyn + n)

    def link(self, ins):
        self.did(ins)
        self.settle()

    def enter(self, i, per):
        self.dyn, self.at, self.per = i * per, self.n, per

    def leave(self, count):
        assert self.n - self.at == self.per, (self.n - self.at, self.per)
        self.n, self.dyn = self.at + self.per * count, None


def build(nc, a, out, FAST_LIMIT=P):
    ctx = ExitStack()
    with ctx:
        def sb(name, shape, dt=F32):
            return ctx.enter_context(nc.sbuf_tensor(name, shape, dt))

        sems = {}

        def sem(name):
            if name not in sems:
                sems[name] = ctx.enter_context(nc.semaphore(name))
            return sems[name]

        raw = sb("raw", [P, RING, HALF])
        w_hi = sb("w_hi", [P, RING, HALF], F32R)
        w_lo = sb("w_lo", [P, RING, HALF], F32R)
        x_res = sb("x_res", [P, TB, D])
        xt_hi = sb("xt_hi", [P, KC, T], F32R)
        xt_lo = sb("xt_lo", [P, KC, T], F32R)
        mixed = sb("mixed", [P, TB, D])
        gain = sb("gain", [P, 2, D])
        mt_hi = sb("mt_hi", [P, KC, T], F32R)
        mt_lo = sb("mt_lo", [P, KC, T], F32R)
        perm = sb("perm", [P, TB, 2 * P], F32R)
        perm_t = sb("perm_t", [P, 2, T], F32R)
        ht_hi = sb("ht_hi", [P, 2, 2, T], F32R)
        ht_lo = sb("ht_lo", [P, 2, 2, T], F32R)
        mem_k = sb("mem_k", [P, 2, 2, T])
        mem_v = sb("mem_v", [P, 2, TB, MEM_W])
        ident = sb("ident", [P, P])
        ident_r = sb("ident_r", [P, P], F32R)
        zeros_r = sb("zeros_r", [P, P], F32R)
        ones = sb("ones", [P, P])
        neg_ones = sb("neg_ones", [P, P])
        before = sb("before", [P, P])
        upto = sb("upto", [P, P])
        neg_from = sb("neg_from", [P, P])
        bias_sb_r = sb("bias_sb_r", [P, P], F32R)
        bias_fox_r = sb("bias_fox_r", [P, P], F32R)
        slot_no = sb("slot_no", [P, P])
        reset64 = sb("reset64", [P, 512])
        reset4 = sb("reset4", [P, 8])
        level_mask = sb("level_mask", [P, len(LEVELS) + 1, P], I8)
        neg_half = sb("neg_half", [P, 16])
        r_w = sb("r_w", [P, 2, KC, 2, 20], F32R)
        f_w = sb("f_w", [P, KC, 2, 16], F32R)
        r_both = sb("r_both", [P, 20])
        f_both = sb("f_both", [P, 16])
        c_pick = sb("c_pick", [P, 16], F32R)
        r_bias = sb("r_bias", [P, 2, 20])
        f_bias = sb("f_bias", [P, 16])
        conv = sb("conv", [P, 4, FC])
        stats = sb("stats", [P, TB, 2, 6])
        mv = sb("mv", [P, TB, 2])
        var_eps = sb("var_eps", [P, 16])
        rstd = sb("rstd", [P, 16])
        peak = sb("peak", [P, 64])
        total = sb("total", [P, 16])
        rt = sb("rt", [P, 228])
        load_max = sb("load_max", [P, 1], I32)
        slot_gate = sb("slot_gate", [P, 2, 4])
        arena = sb("arena", [P, 9216])

        psum = ctx.enter_context(nc.psum_tensor("psum", [P, 8, 512], F32))

        def ar(at, *dims):
            n = 1
            for d in dims:
                n *= d
            v = arena[:, at:at + n]
            if len(dims) == 2:
                v = v.rearrange("p (a b) -> p a b", a=dims[0])
            elif len(dims) == 3:
                v = v.rearrange("p (a b c) -> p a b c", a=dims[0], b=dims[1])
            return v

        small_w = ar(0, 3, 160)
        bias_sb, bias_fox = ar(1536, P), ar(1664, P)
        logits_t = ar(8192, T)

        raw_in = [sem(f"raw_in{i}") for i in range(RING)]
        x_in, mem_in, small_in, gain_in = sem("x_in"), sem("mem_in"), sem("small_in"), sem("gain_in")
        p_in, gnorm_in, c_moved, out_in = sem("p_in"), sem("gnorm_in"), sem("c_moved"), sem("out_in")
        consts = sem("consts")
        consts_r = sem("consts_r")
        hi_split = sem("hi_split")
        lo_split = sem("lo_split")
        half_used = sem("half_used")
        drained_a, drained_v = sem("drained_a"), sem("drained_v")
        tr_done, tr_hi, tr_lo = sem("tr_done"), sem("tr_hi"), sem("tr_lo")
        small_h, small_l = sem("small_h"), sem("small_l")
        ln_done = sem("ln_done")
        var_ready, rstd_ready = sem("var_ready"), sem("rstd_ready")

        def w_half(h, part):
            return part[:, h % RING, :]

        block = ctx.enter_context(nc.Block())

        @block.sync
        def _(sp):
            def load(h, pieces, lo_count=None):
                if not isinstance(h, int) or h >= RING:
                    sp.wait_ge(lo_split, (h if lo_count is None else lo_count) - RING + 1)
                return pieces

            def send(slot, dst_src):
                for dst, src in dst_src:
                    sp.dma_start(dst, src).then_inc(raw_in[slot], 16)

            def fm(w, col):
                v = w.rearrange("(k p) n -> p k n", p=P)[:, :, col:col + 256]
                return lambda r: [(r.rearrange("p (k n) -> p k n", k=8)[:, 4 * i:4 * i + 4, :],
                                   v[:, 4 * i:4 * i + 4, :]) for i in range(2)]

            def tm(w, col, half):
                v = w.rearrange("(k p) n -> p k n", p=P)[:, 4 * half:4 * half + 4, col:col + 512]
                return lambda r: [(r.rearrange("p (k n) -> p k n", k=4)[:, 2 * i:2 * i + 2, :],
                                   v[:, 2 * i:2 * i + 2, :]) for i in range(2)]

            def rows(w, chunk):
                v = w.rearrange("(k p) n -> p k n", p=P)[:, chunk:chunk + 2, :]
                return lambda r: [(r.rearrange("p (k n) -> p k n", k=2)[:, i, :], v[:, i, :]) for i in range(2)]

            h = 0

            def put(make):
                nonlocal h
                load(h, None)
                send(h % RING, make(raw[:, h % RING, :]))
                h += 1

            def experts(layer):
                nonlocal h
                assert h == AT[f"E{layer}"]
                wg = a["w_gate"][layer].rearrange("(g j) (k p) f -> g j p k f", j=PER_GROUP, p=P)
                wu = a["w_up"][layer].rearrange("(g j) (k p) f -> g j p k f", j=PER_GROUP, p=P)
                wd = a["w_down"][layer].rearrange("(g j) (k p) n -> g j p k n", j=PER_GROUP, p=P)
                with sp.Fori(0, GROUPS) as g:
                    for n, (kind, j, half) in enumerate(GROUP_ORDER):
                        sp.wait_ge(lo_split, g * PER_G + (h + n - RING + 1))
                        slot = (h + n) % RING
                        r = raw[:, slot, :]
                        if kind == "G":
                            v = r.rearrange("p (k n) -> p k n", k=4)
                            send(slot, [(v[:, :, 0:256], wg[g, j, :, 4 * half:4 * half + 4, :]),
                                        (v[:, :, 256:512], wu[g, j, :, 4 * half:4 * half + 4, :])])
                        else:
                            v = r.rearrange("p (k n) -> p k n", k=2)
                            send(slot, [(v[:, i, :], wd[g, j, :, i, :]) for i in range(2)])
                h += GROUPS * PER_G

            def gains(g, b, n):
                if n:
                    sp.wait_ge(ln_done, 2 * n)
                for i, v in enumerate((g, b)):
                    sp.dma_start(gain[:, i, :], v.rearrange("(o d) -> o d", o=1).to_broadcast([P, D]))\
                        .then_inc(gain_in, 16)

            sp.dma_start(x_res[:], a["x"][0].rearrange("(b p) d -> p b d", p=P)).then_inc(x_in, 16)
            wa = a["a_w_in"][0]
            for j in range(3):
                put(fm(wa, SEQ_W + 256 * j))
            sp.dma_start(mixed[:], a["mem"][0].rearrange("(b p) d -> p b d", p=P)).then_inc(mem_in, 16)
            for j in range(3):
                put(fm(wa, 256 * j))
            for j in range(3):
                for half in range(2):
                    put(tm(wa, 2 * SEQ_W + 512 * j, half))
            put(fm(wa, 4 * SEQ_W))
            for half in range(2):
                put(fm(a["w_mem_kv"][0], MEM_W * half))
            for layer in range(2):
                if layer:
                    for j in range(3):
                        put(fm(a["w_kv_shared"], 256 * j))
                    for half in range(2):
                        put(tm(a["w_kv_shared"], SEQ_W, half))
                    put(fm(a["w_kv_shared"], SEQ_W + 512))
                    for j in range(3):
                        put(fm(a["b_w_in"][0], 256 * j))
                    put(fm(a["b_w_in"][0], SEQ_W))
                for j in range(2):
                    for half in range(2):
                        put(tm(a["w_o"][layer], 512 * j, half))
                if layer == 0:
                    for half in range(2):
                        put(fm(a["w_mem_kv"][1], MEM_W * half))
                    sp.wait_ge(sem("mixed_ready"), 2)
                gains(a["ln_mix_g"][layer], a["ln_mix_b"][layer], 2 * layer)
                experts(layer)
                gains(a["ln_ffn_g"][layer], a["ln_ffn_b"][layer], 2 * layer + 1)
            wc = a["attn_w_in_2"][0]
            for j in range(8):
                put(fm(wc, 256 * j))
            for j in range(2):
                for half in range(2):
                    put(tm(wc, 2 * D + 512 * j, half))
            for j in range(2):
                for half in range(2):
                    put(tm(a["attn_w_out_2"][0], 512 * j, half))
            gains(a["ln_mix_g_2"][0], a["ln_mix_b_2"][0], 4)
            wu2 = a["ffn_w_up_2"][0]
            for j in range(FC // 2):
                put(fm(wu2, FFN + 256 * j))
                put(fm(wu2, 256 * j))
            for j in range(FC // 2):
                put(rows(a["ffn_w_down_2"][0], 2 * j))
            gains(a["ln_ffn_g_2"][0], a["ln_ffn_b_2"][0], 5)
            sp.wait_ge(tr_done, 18)
            sp.dma_start(mixed[:, :, 0:256], a["p_2"][0, 0].rearrange("(b p) d -> p b d", p=P)).then_inc(p_in, 16)
            put(rows(a["ple_w_proj_2"][0], 0))
            for j in range(2):
                for half in range(2):
                    put(tm(a["ple_w_gate_2"][0], 512 * j, half))
            assert h == HALVES
            sp.wait_ge(ln_done, 12)
            sp.dma_start(gain[:, 0, :], a["ple_b_gate_2"][0].rearrange("(o d) -> o d", o=1).to_broadcast([P, D]))\
                .then_inc(gain_in, 16)
            out_v = out[0].rearrange("(b p) d -> p b d", p=P)
            for b in range(TB):
                sp.wait_ge(sem("result"), b + 1)
                sp.dma_start(out_v[:, b, :], x_res[:, b, :]).then_inc(out_in, 16)
            sp.wait_ge(out_in, 16 * TB)

        @block.gpsimd
        def _(pool):
            own = Tally(pool, sem("pool_own"))
            pool.memset(zeros_r[:].bitcast(F32), 0.0)
            pool.memset(ident[:], 0.0)
            pool.memset(ones[:], 1.0)
            pool.memset(neg_ones[:], -1.0)
            pool.memset(before[:], 1.0)
            pool.memset(upto[:], 1.0)
            pool.memset(neg_from[:], -1.0)
            pool.memset(bias_sb[:], 0.0)
            pool.memset(bias_fox[:], 0.0)
            pool.memset(reset64[:], 1.0)
            pool.memset(reset4[:], 1.0)
            pool.memset(neg_half[:], -0.5)
            own.link(pool.memset(level_mask[:], 0))

            def keep(tile, op, fill, base, step, mult, n=P):
                own.did(pool.affine_select(out=tile, in_=tile, compare_op=op, fill=fill, base=base,
                                           pattern=[[step, n]], channel_multiplier=mult))

            keep(ident[:], ALU.not_equal, 1.0, 0, -1, 1)
            keep(before[:], ALU.is_gt, 0.0, 0, 1, -1)
            keep(upto[:], ALU.is_ge, 0.0, 0, 1, -1)
            keep(neg_from[:], ALU.is_ge, 0.0, 0, -1, 1)
            keep(bias_sb[:], ALU.is_gt, NEG, 0, 1, -1)
            keep(bias_fox[:], ALU.is_ge, NEG, 0, -1, 1)
            own.did(pool.memset(reset64[:].rearrange("p (c t) -> p c t", t=64)[:, :, 0:1], 0.0))
            own.did(pool.memset(reset4[:].rearrange("p (c t) -> p c t", t=4)[:, :, 0:1], 0.0))
            own.did(pool.iota(slot_no[:], pattern=[[1, P]], base=0, channel_multiplier=0,
                              allow_small_or_imprecise_dtypes=True))
            own.settle()
            pool.nop().then_inc(consts, 1)
            for i, L in enumerate(LEVELS):
                up = level_mask[:, i, :].rearrange("p (b u t) -> p b u t", u=2, t=L)[:, :, 1, :]
                nb = P // (2 * L)
                own.link(pool.memset(up, 1))
                own.link(pool.affine_select(out=up, in_=up, compare_op=ALU.is_ge, fill=0.0, base=0,
                                            pattern=[[-2 * L, nb], [0, L]], channel_multiplier=1))
                own.link(pool.affine_select(out=up, in_=up, compare_op=ALU.is_ge, fill=0.0, base=L - 1,
                                            pattern=[[2 * L, nb], [0, L]], channel_multiplier=-1))
            dg = level_mask[:, len(LEVELS), :]
            own.link(pool.memset(dg, 1))
            own.link(pool.affine_select(out=dg, in_=dg, compare_op=ALU.is_equal, fill=0.0, base=0,
                                        pattern=[[-1, P]], channel_multiplier=1))
            own.link(pool.memset(ar(6144, 1536), 0.0))
            pool.nop().then_inc(consts, 1)

            def power(n, cols):
                pool.wait_ge(var_ready, n)
                pool.tensor_tensor(rstd[:, cols], var_eps[:, cols], neg_half[:, cols], ALU.pow)\
                    .then_inc(rstd_ready, 1)

            n = 0
            for b in range(3):
                n += 1
                power(n, slice(4 * b, 4 * b + 4))
            for _ in range(6):
                for b in range(TB):
                    n += 1
                    power(n, slice(b, b + 1))

        hq = ar(0, HG_HEADS, T)
        hG = ar(1536, HG_HEADS, T)
        hk = ar(3072, HG_HEADS, T)
        hX = ar(4608, 3, 512)
        hS = ar(6144, 2 * HG_HEADS, P)
        hg = ar(7680, TB, SEQ_W)
        spare = gain[:].rearrange("p g d -> p (g d)")
        hSx = spare[:, 768:1536].rearrange("p (h t) -> p h t", t=P)
        a_qm = spare[:, 1536:2048].rearrange("p (c t) -> p c t", t=T)
        sq = ar(4608, 3, 512)

        b_q = ar(0, 6, T)
        b_k = ar(1536, 6, T)
        b_qm = ar(3072, 2, T)
        b_s = ar(3584, 2, 2, 384)
        b_a = ar(5120, 2, 2, 384)

        c_q = ar(0, 8, T)
        c_k = ar(2048, 8, T)
        c_f = ar(4096, TB, FOX_HEADS)
        c_c = ar(4128, TB, P)
        c_p = ar(4608, 2, 2, 384)
        c_pt = ar(6144, 2, 2, 384)
        c_rows = perm[:].rearrange("p b t -> p (b t)")[:, 0:384]

        ff_t = ar(0, 2, 512)
        ff_g = ar(1024, 2, 512)
        ff_a = ar(2048, FC, T)
        pl_s = ar(0, 2, 512)

        ex_s = ar(0, 2, 2, 256)
        ex_h = ar(1024, 2, 2, 256)

        A_HALVES = list(range(AT["A_IG"], AT["O0"]))
        N_STEPS = 3 * STEPS

        def decayed(st):
            p, i = divmod(st, STEPS)
            return (STEPS - 1) * p + min(i + 1, STEPS - 1)

        ends = {UNITS[u][0] + UNITS[u][1] - 1: u for u in _order}

        def mem_work(layer, h):
            return (ar(0, 4, 2, T) if layer == 0 else ar(6656, 2, 2, T))[:, h % 4 if layer == 0 else h % 2, :, :]

        B_UNITS = [("S", 0), ("S", 1), ("M", 0), ("S", 2), ("S", 3), ("M", 1), ("S", 4), ("S", 5)]
        C_UNITS = [("F", p) for p in range(8)]
        SLOTS = 4

        def slot(u):
            return 2 * (u % SLOTS)

        r_log = rt[:, 0:40].rearrange("p (b e) -> p b e", b=2)
        r_g = rt[:, 40:48].rearrange("p (b e) -> p b e", b=2)
        r_eq = rt[:, 48:56]
        r_cum = rt[:, 56:64]
        r_og = rt[:, 64:72].rearrange("p (b e) -> p b e", b=2)
        r_t16 = rt[:, 72:104].rearrange("p (b g e) -> p b g e", b=2, g=4)
        r_e = rt[:, 104:112].rearrange("p (b e) -> p b e", b=2)
        r_o1 = rt[:, 112:120].rearrange("p (b e) -> p b e", b=2)
        r_o2 = rt[:, 120:128].rearrange("p (b e) -> p b e", b=2)
        r_m = rt[:, 128:144].rearrange("p (n b) -> p n b", b=2)
        r_g4 = rt[:, 144:152].rearrange("p (b e) -> p b e", b=2)
        r_gate = rt[:, 160:192].rearrange("p (b g e) -> p b g e", b=2, g=4)
        r_pos = rt[:, 192:204].rearrange("p (n g) -> p n g", g=4)
        r_i4 = rt[:, 208:216].rearrange("p (b e) -> p b e", b=2)
        r_e2 = rt[:, 216:224].rearrange("p (b e) -> p b e", b=2)
        r_mx = rt[:, 224:225]

        MOE_SEMS = ("perm_ready", "turned_perm", "perm_out", "gathered", "xg_hi", "xg_lo", "y_sum", "y_hi",
                    "y_lo")

        def of_group(i, q, n, per):
            return i * (2 * per) + (q * per + n)

        def y_tile(c):
            return psum[:, 6 + c, :].rearrange("p (k t) -> p k t", t=P)

        def slots_x(v):
            return v.rearrange("p b (k t) -> p (b k) t", t=2 * P)

        def small_parts(part):
            both = [(r_w[:, l, :, part, :], small_w[:, l, :].rearrange("p (k e) -> p k e", k=KC)) for l in range(2)]
            return both + [(f_w[:, :, part, :], small_w[:, 2, 0:128].rearrange("p (k e) -> p k e", k=KC))]

        @block.tensor
        def _(pe):
            def mm(o, l, r, start, stop, skip=False):
                return pe.matmul(o, l, r, start=start, stop=stop, skip_group_check=skip)

            def free(name):
                for u in free_waits(name):
                    for who, s in (("a", drained_a), ("v", drained_v)):
                        if who in UNITS[u][3]:
                            pe.wait_ge(s, drained_by(u, who))

            def passes(hi, lo, whi, wlo):
                return ((hi, whi), (hi, wlo), (lo, whi))

            def fm_half(name, xh, xl, s=None):
                h, _, banks, _ = UNITS[name]
                free(name)
                pe.wait_ge(lo_split, h + 1)
                fm_products(h, banks[0], xh, xl, s)

            def fm_products(h, bank, xh, xl, s=None):
                wh, wl = (w_half(h, w).rearrange("p (k n) -> p k n", k=8) for w in (w_hi, w_lo))
                for c in range(2):
                    for k in range(KC):
                        if s is not None and c == 0 and k % 4 == 0:
                            split_ready(s + k // 4)
                        ws = slice(P * c, P * c + P)
                        for i, (x, w) in enumerate(passes(xh[:, k, :], xl[:, k, :], wh[:, k, ws], wl[:, k, ws])):
                            last = mm(psum[:, bank, T * c:T * c + T], w, x, c == 0 and k == 0 and i == 0,
                                      c == 1 and k == KC - 1 and i == 2, skip=True)
                last.then_inc(half_used, 1)

            def tm256(name, xh, xl):
                h, _, banks, _ = UNITS[name]
                free(name)
                pe.wait_ge(lo_split, h + 1)
                wh, wl = (w_half(h, w).rearrange("p (k n) -> p k n", k=8) for w in (w_hi, w_lo))
                for b in range(TB):
                    for k in range(KC):
                        ts = slice(P * b, P * b + P)
                        for i, (x, w) in enumerate(passes(xh[:, k, ts], xl[:, k, ts], wh[:, k, :], wl[:, k, :])):
                            last = mm(psum[:, banks[0], 256 * b:256 * b + 256], x, w,
                                      b == 0 and k == 0 and i == 0, b == 1 and k == KC - 1 and i == 2, skip=True)
                last.then_inc(half_used, 1)

            def tm_half(h, half, banks, xh, xl):
                pe.wait_ge(lo_split, h + 1)
                wh, wl = (w_half(h, w).rearrange("p (k n) -> p k n", k=4) for w in (w_hi, w_lo))
                for b in range(TB):
                    for kk in range(4):
                        k = 4 * half + kk
                        ts = slice(P * b, P * b + P)
                        for i, (x, w) in enumerate(passes(xh[:, k, ts], xl[:, k, ts], wh[:, kk, :], wl[:, kk, :])):
                            last = mm(psum[:, banks[b], :], x, w, k == 0 and i == 0, k == KC - 1 and i == 2)
                last.then_inc(half_used, 1)

            def tm_tile(name, xh, xl, s=None):
                h, _, banks, _ = UNITS[name]
                free(name)
                for half in range(2):
                    if s is not None:
                        split_ready(s + half)
                    tm_half(h + half, half, banks, xh, xl)

            def turn(s, src, chunk0, n=4):
                if s >= 2:
                    pe.wait_ge(tr_lo, s - 1)
                bank = 4 + 2 * (s % 2)
                for c in range(n):
                    for b in range(TB):
                        k = chunk0 + c
                        last = pe.transpose(psum[:, bank + c // 2, T * (c % 2) + P * b:T * (c % 2) + P * b + P],
                                            src[:, b, P * k:P * k + P], ident[:])
                last.then_inc(tr_done, 1)

            def turn_normed(s, n):
                pe.wait_ge(tr_lo, s)
                for b in range(TB):
                    pe.wait_ge(ln_done, 2 * n + b + 1)
                    for k in range(KC):
                        bank = 4 + 2 * ((s + k // 4) % 2) + k % 4 // 2
                        at = T * (k % 2) + P * b
                        last = pe.transpose(psum[:, bank, at:at + P], x_res[:, b, P * k:P * k + P], ident[:])
                        if b and k % 4 == 3:
                            last.then_inc(tr_done, 1)

            def split_ready(s):
                pe.wait_ge(tr_lo, s + 1)

            pe.wait_ge(consts, 1)
            pe.wait_ge(x_in, 16)
            turn(0, x_res, 0)
            turn(1, x_res, 4)
            for j in range(3):
                fm_half(f"A_F{j}", xt_hi, xt_lo, 0)
            pe.wait_ge(mem_in, 16)
            turn(2, mixed, 0)
            turn(3, mixed, 4)
            for j in range(3):
                fm_half(f"A_Q{j}", xt_hi, xt_lo)
            pe.wait_ge(tr_lo, 4)

            def a_step(st):
                p, i = divmod(st, STEPS)
                if i <= len(LEVELS):
                    pe.wait_ge(sem("x_ready"), decayed(st))
                else:
                    pe.wait_ge(sem("q_scaled"), p + 1)
                    pe.wait_ge(sem("k_ready"), p + 1)
                if st >= 4:
                    pe.wait_ge(sem("merged"), st - 3)
                bank = psum[:, 4 + st % 4, :]
                x = hX[:, st % 3, :].rearrange("p (h t) -> p h t", h=2)
                for hh in range(2):
                    if i == len(LEVELS):
                        last = mm(bank[:, P * hh:P * hh + P], x[:, hh, 0:P], x[:, hh, P:T], True, True)
                        continue
                    for b in range(TB):
                        o = bank[:, (2 * hh + b) * P:(2 * hh + b) * P + P]
                        if i < len(LEVELS):
                            v = x[:, hh, P * b:P * b + P]
                            last = mm(o, v, v, True, True)
                        else:
                            last = mm(o, hk[:, 2 * p + hh, P * b:P * b + P], hq[:, 2 * p + hh, P * b:P * b + P],
                                      True, True)
                last.then_inc(sem("level_done"), 1)

            for n, h in enumerate(A_HALVES):
                name = next(u for u in _order if UNITS[u][0] <= h < UNITS[u][0] + UNITS[u][1])
                if name.startswith("A_IG"):
                    if h == UNITS[name][0]:
                        free(name)
                    tm_half(h, h - UNITS[name][0], UNITS[name][2], xt_hi, xt_lo)
                elif name == "A_QM":
                    fm_half(name, xt_hi, xt_lo)
                elif name == "MK0":
                    fm_half(name, mt_hi, mt_lo)
                else:
                    tm256(name, mt_hi, mt_lo)
                for st in range(3 * n, min(3 * n + 3, N_STEPS)):
                    a_step(st)
            def mem_scores(layer, qm, h, bank):
                rows = slice(64 * (h % 2), 64 * (h % 2) + 64)
                for b in range(TB):
                    last = mm(psum[:, bank, T * b:T * b + T], qm[rows, h // 2, P * b:P * b + P],
                              mem_k[rows, layer, h // 2, :], True, True)
                last.then_inc(sem("mem_scores"), 1)

            def mem_turn(layer, h, bank):
                pe.wait_ge(sem("mem_prob"), 4 * layer + h + 1)
                for m in range(2):
                    for b in range(TB):
                        last = pe.transpose(psum[:, bank, T * m + P * b:T * m + P * b + P],
                                            mem_work(layer, h)[:, b, P * m:P * m + P], ident[:])
                last.then_inc(sem("mem_turned"), 1)

            def mem_product(layer, h, bank):
                pe.wait_ge(sem("mem_pt"), 4 * layer + h + 1)
                for b in range(TB):
                    for m in range(2):
                        last = mm(psum[:, bank, 64 * b:64 * b + 64], mem_work(layer, h)[:, m, P * b:P * b + P],
                                  mem_v[:, layer, m, 64 * h:64 * h + 64], m == 0, m == 1)
                last.then_inc(sem("mem_out"), 1)

            pe.wait_ge(sem("merged"), N_STEPS)
            pe.wait_ge(drained_a, drained_by("MK0", "a"))
            for h in range(4):
                mem_scores(0, a_qm, h, 4 + h)
            pe.wait_ge(drained_a, drained_by("MV0", "a"))
            for p in range(3):
                for hh in range(2):
                    h = 2 * p + hh
                    cs = slice(P * h, P * h + P)
                    for b in range(TB):
                        o = psum[:, p, (2 * hh + b) * P:(2 * hh + b) * P + P]
                        last = mm(o, hS[:, 2 * h + b, :], mixed[:, b, cs], True, b == 0)
                        if b:
                            last = mm(o, hSx[:, h, :], mixed[:, 0, cs], False, True)
                last.then_inc(sem("hg_out"), 1)
            for h in range(4):
                mem_turn(0, h, 4 + h)
                if h:
                    mem_product(0, h - 1, 3 + h)
            mem_product(0, 3, 7)

            def project(layer, s):
                pe.wait_ge(sem("mixed_ready"), 2 * (layer + 1))
                turn(s, mixed, 0)
                turn(s + 1, mixed, 4)
                for j in range(2):
                    tm_tile(f"O{layer}{j}", xt_hi, xt_lo, s)

            n_logits = [0]

            def small_logits(w, n, both, s):
                for k in range(KC):
                    if k % 4 == 0:
                        split_ready(s + k // 4)
                    for i, x in enumerate((xt_hi, xt_lo)):
                        last = mm(psum[0:2 * n, 4, 0:T], w[:, k, :, :].rearrange("p a e -> p (a e)"), x[:, k, :],
                                  k == 0 and i == 0, k == KC - 1 and i == 1)
                last.then_inc(sem("logits_t"), 1)
                n_logits[0] += 1
                pe.wait_ge(sem("logits_copied"), n_logits[0])
                for b in range(TB):
                    last = mm(psum[:, 4, n * b:n * b + n], logits_t[0:2 * n, P * b:P * b + P], both[0:2 * n, :],
                              True, True)
                last.then_inc(sem("logits"), 1)

            def experts(layer):
                s = {n: sem(f"{n}{layer}") for n in MOE_SEMS}
                base = AT[f"E{layer}"]
                zeros_row = zeros_r[:].rearrange("p (o n) -> p o n", o=1).to_broadcast([P, 4, P])
                small_logits(r_w[:, layer, :, :, :], 20, r_both, 6 + 6 * layer)
                for q in range(4):
                    pe.wait_ge(drained_v, drained_by(f"O{layer}1", "v"))
                    mm(psum[:, q, :], zeros_r[:], zeros_row, True, False, skip=True)
                pe.wait_ge(sem("group_ready"), layer + 1)
                og = rt[:, 64:72]
                mm(psum[:, 5, 0:4], before[:], og[:, 0:4], True, True)
                mm(psum[:, 5, 4:8], ones[:], og[:, 0:4], True, False)
                mm(psum[:, 5, 4:8], before[:], og[:, 4:8], False, True)
                mm(psum[:, 5, 8:12], ones[:], og[:, 0:4], True, False)
                mm(psum[:, 5, 8:12], ones[:], og[:, 4:8], False, True).then_inc(sem("counted"), 1)
                pe.wait_ge(sem("placed"), layer + 1)
                load = pe.value_load(load_max[0:1, 0:1], min_val=0, max_val=T)

                def gather(i):
                    pe.wait_ge(s["perm_ready"], i + 1)
                    for q in range(2):
                        for b in range(TB):
                            last = pe.transpose(psum[:, 6, T * q + P * b:T * q + P * b + P],
                                                perm[:, b, P * q:P * q + P].bitcast(F32), ident[:])
                    for r in range(2):
                        if r:
                            pe.wait_ge(s["perm_out"], i + 1)
                        for k in range(4 * r, 4 * r + 4):
                            o = psum[:, 4 + k // 2, T * (k % 2):T * (k % 2) + T]
                            n = 0
                            for b in range(TB):
                                for x in (mt_hi, mt_lo):
                                    xv = x[:].rearrange("p k t -> p (k t)")
                                    last = mm(o, xv[:, D * b + P * k:D * b + P * k + P], perm[:, b, :],
                                              n == 0, n == 3)
                                    n += 1
                        last.then_inc(s["gathered"], 1)
                        if r:
                            continue
                        pe.wait_ge(sem("gated"), layer + 1)
                        for q in range(2):
                            for b in range(TB):
                                last = mm(psum[:, 7, 4 * q:4 * q + 4], perm[:, b, P * q:P * q + P].bitcast(F32),
                                          r_gate[:, b, bass.ds(i * 2 + q, 1), :].rearrange("p a e -> p (a e)"),
                                          b == 0, b == 1)
                        last.then_inc(s["turned_perm"], 1)

                def scatter(i, q):
                    for n in range(2):
                        pe.wait_ge(s["y_hi"], of_group(i, q, n + 1, 2))
                        pe.wait_ge(s["y_lo"], of_group(i, q, n + 1, 2))
                        for b in range(TB):
                            for y in (xt_hi, xt_lo):
                                mm(psum[:, 2 * n + b, :], perm_t[:, q, P * b:P * b + P],
                                   y[:, 4 * n:4 * n + 4, P * q:P * q + P], False, False, skip=True)

                def group(i, q, dense):
                    nb = TB if dense else 1
                    e0 = 16 * layer

                    def gu_bank(j, b):
                        return 4 + 2 * (j % 2) + b if dense else 4 + j % 2

                    def gate_up(j):
                        if j >= 2:
                            pe.wait_ge(sem("ht_hi_ready"), of_group(i, q, e0 + j - 1, PER_GROUP))
                            pe.wait_ge(sem("ht_lo_ready"), of_group(i, q, e0 + j - 1, PER_GROUP))
                        for half in range(2):
                            if j == 0 and q == 0 and not dense:
                                pe.wait_ge(s["xg_hi"], i * 2 + (half + 1))
                                pe.wait_ge(s["xg_lo"], i * 2 + (half + 1))
                            h = base + G_AT[j] + half
                            pe.wait_ge(lo_split, of_group(i, q, h + 1, PER_G))
                            wh, wl = (w_half(h, w).rearrange("p (k n) -> p k n", k=4) for w in (w_hi, w_lo))
                            for b in range(nb):
                                for kk in range(4):
                                    k = 4 * half + kk
                                    at = P * b if dense else P * q
                                    ts = slice(at, at + P)
                                    for n, (x, w) in enumerate(passes(xt_hi[:, k, ts], xt_lo[:, k, ts],
                                                                      wh[:, kk, :], wl[:, kk, :])):
                                        last = mm(psum[:, gu_bank(j, b), :], x, w, k == 0 and n == 0,
                                                  k == KC - 1 and n == 2)
                            last.then_inc(half_used, 1)

                    def turn_h(j):
                        pe.wait_ge(sem("h_ready"), of_group(i, q, e0 + j + 1, PER_GROUP))
                        for f in range(2):
                            for b in range(nb):
                                last = pe.transpose(
                                    psum[:, gu_bank(j, 0), P * nb * f + P * b:P * nb * f + P * b + P],
                                    ex_h[:, j % 2, b, P * f:P * f + P], ident[:])
                        last.then_inc(sem("h_turned"), 1)

                    def down(j):
                        pe.wait_ge(sem("ht_hi_ready"), of_group(i, q, e0 + j + 1, PER_GROUP))
                        pe.wait_ge(sem("ht_lo_ready"), of_group(i, q, e0 + j + 1, PER_GROUP))
                        h = base + D_AT[j]
                        pe.wait_ge(lo_split, of_group(i, q, h + 1, PER_G))
                        wh, wl = (w_half(h, w).rearrange("p (k n) -> p k n", k=2) for w in (w_hi, w_lo))
                        for c in range(2):
                            for b in range(nb):
                                for f in range(2):
                                    ts = slice(P * b, P * b + P)
                                    for n, (x, w) in enumerate(passes(
                                            ht_hi[:, j % 2, f, ts], ht_lo[:, j % 2, f, ts],
                                            wh[:, f, 512 * c:512 * c + 512], wl[:, f, 512 * c:512 * c + 512])):
                                        if dense:
                                            last = mm(psum[:, 2 * c + b, :], x, w, False, False, skip=True)
                                        else:
                                            last = mm(psum[:, 6 + c, :], x, w, j == 0 and f == 0 and n == 0,
                                                      j == 3 and f == 1 and n == 2)
                            if c == 0 and j == 3 and not dense:
                                last.then_inc(s["y_sum"], 1)
                        last.then_inc(half_used, 1)

                    gate_up(0)
                    if q and not dense:
                        scatter(i, 0)
                    gate_up(1)
                    turn_h(0)
                    gate_up(2)
                    turn_h(1)
                    down(0)
                    gate_up(3)
                    turn_h(2)
                    down(1)
                    turn_h(3)
                    down(2)
                    down(3)
                    if q and not dense:
                        scatter(i, 1)

                with pe.If(load < FAST_LIMIT + 1):
                    with pe.Fori(0, PAIRS) as i:
                        gather(i)
                        for q in range(2):
                            group(i, q, False)
                with pe.Else():
                    with pe.Fori(0, PAIRS) as i:
                        for q in range(2):
                            group(i, q, True)
                for q in range(4):
                    last = mm(psum[:, q, :], zeros_r[:], zeros_row, False, True, skip=True)
                last.then_inc(sem("moe_done"), 1)

            project(0, 4)
            fm_half("MK1", mt_hi, mt_lo)
            tm256("MV1", mt_hi, mt_lo)
            pe.wait_ge(drained_a, drained_by("MV1", "a"))
            turn_normed(6, 0)
            pe.wait_ge(small_l, 1)
            pe.wait_ge(sem("both_ready"), 1)
            experts(0)
            turn_normed(8, 1)

            for j in range(3):
                fm_half(f"B_K{j}", xt_hi, xt_lo, 8)
            tm_tile("B_V0", xt_hi, xt_lo)
            tm256("B_V1", xt_hi, xt_lo)
            for j in range(3):
                fm_half(f"B_Q{j}", xt_hi, xt_lo)
            fm_half("B_QM", xt_hi, xt_lo)
            pe.wait_ge(drained_a, drained_by("B_Q2", "a"))
            pe.wait_ge(drained_v, drained_by("B_QM", "v"))

            def scores(u):
                kind, p = B_UNITS[u]
                if u >= SLOTS:
                    pe.wait_ge(sem("b_taken"), u - SLOTS + 1)
                if kind == "M":
                    for hh in range(2):
                        mem_scores(1, b_qm, 2 * p + hh, slot(u) + hh)
                    return
                for hh in range(2):
                    o, rows = psum[:, slot(u) + hh, :], slice(64 * hh, 64 * hh + 64)
                    mm(o[:, 0:T], b_k[rows, p, 0:P], b_q[rows, p, :], True, False, skip=True)
                    mm(o[:, T:T + P], b_k[rows, p, P:T], b_q[rows, p, P:T], False, False, skip=True)
                    last = mm(two_blocks(o), ident_r[:], twice(bias_sb_r), False, True, skip=True)
                last.then_inc(sem("sb_z"), 1)

            def two_blocks(o):
                return o.rearrange("p (b t) -> p b t", b=2)[:, :, 0:P]

            def twice(v):
                return v[:].rearrange("p (o t) -> p o t", o=1).to_broadcast([P, 2, P])

            def middle(u):
                kind, p = B_UNITS[u]
                if kind == "M":
                    for hh in range(2):
                        mem_turn(1, 2 * p + hh, slot(u) + hh)
                    return
                pe.wait_ge(sem("sb_sp"), p + 1)
                for hh in range(2):
                    o, sp = psum[:, slot(u) + hh, :], b_s[:, p % 2, hh, :]
                    mm(o[:, 0:384], neg_from[:], sp[:, 0:384], False, False, skip=True)
                    last = mm(o[:, P:T], neg_ones[:], sp[:, T:384], False, True, skip=True)
                last.then_inc(sem("sb_log"), 1)

            def product(u):
                kind, p = B_UNITS[u]
                if kind == "M":
                    for hh in range(2):
                        mem_product(1, 2 * p + hh, slot(u) + hh)
                    return
                pe.wait_ge(sem("sb_a"), p + 1)
                for hh in range(2):
                    o = psum[:, slot(u) + hh, 384:512]
                    w = b_a[:, p % 2, hh, :]
                    cs = slice(64 * (2 * p + hh), 64 * (2 * p + hh) + 64)
                    mm(o[:, 0:64], w[:, 0:P], mixed[:, 0, cs], True, True)
                    mm(o[:, 64:128], w[:, P:T], mixed[:, 0, cs], True, False)
                    last = mm(o[:, 64:128], w[:, T:384], mixed[:, 1, cs], False, True)
                last.then_inc(sem("sb_o"), 1)

            def pipeline(n, scores, middle, product):
                for u in range(3):
                    scores(u)
                for u in range(n):
                    middle(u)
                    if u:
                        product(u - 1)
                        if u + 2 < n:
                            scores(u + 2)
                product(n - 1)

            pipeline(len(B_UNITS), scores, middle, product)
            project(1, 10)
            turn_normed(12, 2)
            experts(1)
            turn_normed(14, 3)

            small_logits(f_w[:], 16, f_both, 14)
            for j in range(4):
                fm_half(f"C_Q{j}", xt_hi, xt_lo)
            pe.wait_ge(sem("f_log"), 1)
            mm(psum[:, 5, 0:16], upto[:], c_f[:, 0, :], True, True)
            mm(psum[:, 5, 16:32], ones[:], c_f[:, 0, :], True, False)
            mm(psum[:, 5, 16:32], upto[:], c_f[:, 1, :], False, True).then_inc(sem("c_sum"), 1)
            for j in range(2):
                fm_half(f"C_K{j}", xt_hi, xt_lo)
            pe.wait_ge(sem("c_out"), 1)
            for b in range(TB):
                last = pe.transpose(psum[:, 6, P * b:P * b + P], c_c[:, b, :], ident[:])
            last.then_inc(sem("c_turned"), 1)
            for j in range(2, 4):
                fm_half(f"C_K{j}", xt_hi, xt_lo)
            for j in range(2):
                tm_tile(f"C_V{j}", xt_hi, xt_lo)
            pe.wait_ge(drained_a, drained_by("C_V1", "a"))
            pe.wait_ge(drained_v, drained_by("C_V1", "v"))
            pe.wait_ge(sem("c_split"), 2)
            pe.wait_ge(sem("pick_ready"), 1)

            def fox_scores(p):
                if p >= SLOTS:
                    pe.wait_ge(sem("fox_o_out"), p - SLOTS + 1)
                for hh in range(2):
                    h = 2 * p + hh
                    o, rows = psum[:, slot(p) + hh, :], slice(64 * hh, 64 * hh + 64)
                    mm(o[:, 0:P], c_q[rows, p, 0:P], c_k[rows, p, 0:P], True, False, skip=True)
                    mm(o[:, P:384], c_q[rows, p, P:T], c_k[rows, p, :], False, False, skip=True)
                    mm(o[:, 0:384], c_pick[:, h:h + 1].to_broadcast([P, P]), c_rows,
                       False, False, skip=True)
                    last = mm(two_blocks(o), ident_r[:], twice(bias_fox_r), False, True, skip=True)
                last.then_inc(sem("fox_s"), 1)

            def fox_turn(p):
                pe.wait_ge(sem("fox_p"), p + 1)
                for hh in range(2):
                    o, w = psum[:, slot(p) + hh, :], c_p[:, p % 2, hh, :]
                    for n in range(3):
                        last = pe.transpose(o[:, P * n:P * n + P], w[:, P * n:P * n + P], ident[:])
                last.then_inc(sem("fox_turned"), 1)

            def fox_out(p):
                pe.wait_ge(sem("fox_pt"), p + 1)
                for hh in range(2):
                    o = psum[:, slot(p) + hh, 384:512]
                    w = c_pt[:, p % 2, hh, :]
                    cs = slice(64 * (2 * p + hh), 64 * (2 * p + hh) + 64)
                    mm(o[:, 0:64], w[:, 0:P], mixed[:, 0, cs], True, True)
                    mm(o[:, 64:128], w[:, P:T], mixed[:, 0, cs], True, False)
                    last = mm(o[:, 64:128], w[:, T:384], mixed[:, 1, cs], False, True)
                last.then_inc(sem("fox_o"), 1)

            pipeline(len(C_UNITS), fox_scores, fox_turn, fox_out)
            pe.wait_ge(sem("fox_o_out"), 8)
            project(2, 16)
            turn_normed(18, 4)

            def up_pair(j, h, i=None):
                for q in range(2):
                    pe.wait_ge(lo_split, h + q + 1 if i is None else i * 4 + (h + q + 1))
                    fm_products(h + q, 2 * (j % 2) + q, xt_hi, xt_lo, 18)

            with pe.Fori(0, FC // 4) as i:
                for j in range(2):
                    pe.wait_ge(sem("ff_free"), i * 2 + (j + 1))
                    up_pair(j, AT["UP"] + 2 * j, i)
            pe.wait_ge(sem("ff_free"), 11)
            up_pair(0, AT["UP"] + 20)

            def row_half(h, xh, xl, bank, first, last_one):
                pe.wait_ge(lo_split, h + 1)
                wh, wl = (w_half(h, w).rearrange("p (k n) -> p k n", k=2) for w in (w_hi, w_lo))
                for n in range(2):
                    for b in range(TB):
                        for f in range(2):
                            ts = slice(P * b, P * b + P)
                            for i, (x, w) in enumerate(passes(xh[:, f, ts], xl[:, f, ts],
                                                              wh[:, f, 512 * n:512 * n + 512],
                                                              wl[:, f, 512 * n:512 * n + 512])):
                                last = mm(psum[:, bank + 2 * n + b, :], x, w, first and f == 0 and i == 0,
                                          last_one and f == 1 and i == 2)
                last.then_inc(half_used, 1)

            pe.wait_ge(sem("ff_free"), FC // 2 + 2)
            for j in range(FC // 2):
                pe.wait_ge(sem("fa_lo"), j + 1)
                q = 2 * (j % 4)
                row_half(AT["DN"] + j, mt_hi[:, q:q + 2, :], mt_lo[:, q:q + 2, :], 0, j == 0, j == FC // 2 - 1)

            pe.wait_ge(p_in, 16)
            pe.wait_ge(tr_lo, 20)
            turn(20, mixed, 0, n=2)
            split_ready(20)
            row_half(AT["PP"], mt_hi[:, 6:8, :], mt_lo[:, 6:8, :], 4, True, True)
            pe.wait_ge(ln_done, 12)
            for r in range(4):
                if r >= 2:
                    pe.wait_ge(sem("last_lo"), r - 1)
                for c in range(2):
                    for b in range(TB):
                        k = 2 * r + c
                        last = pe.transpose(psum[:, r % 2, T * c + P * b:T * c + P * b + P],
                                            x_res[:, b, P * k:P * k + P], ident[:])
                last.then_inc(sem("last_turned"), 1)
            pe.wait_ge(sem("last_lo"), 4)
            for j in range(2):
                for half in range(2):
                    tm_half(AT["PG"] + 2 * j + half, half, [2 * j, 2 * j + 1], xt_hi, xt_lo)

        @block.scalar
        def _(act):
            own = Tally(act, sem("act_own"))
            done = [0]

            def fn(o, i, f, **kw):
                return act.activation(o, i, f, **kw)

            def round_to(upto):
                while done[0] < min(upto, HALVES):
                    h = done[0]
                    act.wait_ge(raw_in[h % RING], 32 * (h // RING + 1))
                    if h >= RING:
                        act.wait_ge(half_used, h - RING + 1)
                    fn(w_half(h, w_hi), w_half(h, raw), ACT.Copy).then_inc(hi_split, 1)
                    done[0] += 1

            def used(h):
                round_to(h + 1 + AHEAD)
                act.wait_ge(half_used, h + 1)

            def split_set(s, n=4):
                act.wait_ge(tr_done, s + 1)
                dst, c0 = (mt_hi, 4 * (s - 2)) if s in (2, 3) else (mt_hi, 6) if s == 20 else (xt_hi, 4 * (s % 2))
                fn(dst[:, c0:c0 + n, :].rearrange("p k t -> p (k t)"),
                   psum[:, 4 + 2 * (s % 2):4 + 2 * (s % 2) + n // 2, :].rearrange("p b n -> p (b n)"), ACT.Copy)\
                    .then_inc(tr_hi, 1)

            def copy_unit(name, dst, bank, scale=1.0, f=ACT.Copy):
                used(UNITS[name][0] + UNITS[name][1] - 1)
                fn(dst, psum[:, bank, 0:dst.free_size()], f, scale=scale).then_inc(drained_a, 1)

            act.dma_start(small_w[:, 0:2, :], a["r_weights"]).then_inc(small_in, 16)
            act.dma_start(small_w[:, 2, 0:128], a["f_weights"]).then_inc(small_in, 16)
            act.dma_start(r_bias[:], a["r_bias"].rearrange("(o l) e -> o l e", o=1).to_broadcast([P, 2, 20]))\
                .then_inc(small_in, 16)
            act.dma_start(f_bias[:], a["attn_b_f_2"].to_broadcast([P, 16])).then_inc(small_in, 16)
            act.dma_start(conv[:], a["conv"]).then_inc(small_in, 16)
            act.dma_start(gain[:, 0, 0:SEQ_W], a["a_gnorm"].to_broadcast([P, SEQ_W])).then_inc(gnorm_in, 16)

            act.preload_act_table_set("natural_log_exp_and_others")
            split_set(0)
            split_set(1)
            round_to(3)
            act.wait_ge(small_in, 80)
            for v, w in small_parts(0):
                last = fn(v, w, ACT.Copy)
            last.then_inc(small_h, 1)

            def pair(v, p):
                return v[:, 2 * p:2 * p + 2, :].rearrange("p h t -> p (h t)")

            for j in range(3):
                used(AT["A_F"] + j)
                k = pair(hk, j)
                own.link(fn(k, psum[:, j, :], ACT.Abs))
                own.link(fn(k, k, ACT.Exp, scale=-1.0))
                fn(k, k, ACT.Ln, bias=1.0).then_inc(sem("f_soft"), 1)
                act.wait_ge(drained_v, j + 1)
                fn(k, k, ACT.Exp).then_inc(sem("k_ready"), 1)
                if j == 0:
                    split_set(2)
                    split_set(3)
            for j in range(3):
                act.wait_ge(sem("g_ready"), j + 1)
                copy_unit(f"A_Q{j}", pair(hq, j), UNITS[f"A_Q{j}"][2][0], f=ACT.Silu)

            def a_drain(name):
                if name == "A_IG0":
                    used(UNITS[name][0] + 1)
                    for b in range(TB):
                        last = fn(mixed[:, b, 0:512], psum[:, UNITS[name][2][b], :], ACT.Copy)
                    last.then_inc(drained_a, 1)
                elif name == "A_IG1":
                    used(UNITS[name][0] + 1)
                    for b in range(TB):
                        bank = psum[:, UNITS[name][2][b], :]
                        fn(mixed[:, b, 512:768], bank[:, 0:256], ACT.Copy)
                        last = fn(hg[:, b, 0:256], bank[:, 256:512], ACT.Silu)
                    last.then_inc(drained_a, 1)
                elif name == "A_IG2":
                    used(UNITS[name][0] + 1)
                    for b in range(TB):
                        last = fn(hg[:, b, 256:768], psum[:, UNITS[name][2][b], :], ACT.Silu)
                    last.then_inc(drained_a, 1)
                elif name == "A_QM":
                    copy_unit(name, a_qm[:].rearrange("p c t -> p (c t)"), UNITS[name][2][0], HD_SCALE)
                elif name.startswith("MK"):
                    copy_unit(name, mem_k[:, 0, :, :].rearrange("p c t -> p (c t)"), UNITS[name][2][0])
                else:
                    copy_unit(name, mem_v[:, 0, :, :].rearrange("p m c -> p (m c)"), UNITS[name][2][0])

            def a_exp(st):
                if st % STEPS <= len(LEVELS):
                    act.wait_ge(sem("x_logs"), decayed(st))
                    fn(hX[:, st % 3, :], hX[:, st % 3, :], ACT.Exp).then_inc(sem("x_exp"), 1)

            for n, h in enumerate(A_HALVES):
                for st in range(3 * n, min(3 * n + 3, N_STEPS)):
                    a_exp(st)
                if h - 1 in ends and h > A_HALVES[0]:
                    a_drain(ends[h - 1])
                round_to(h + AHEAD)
            a_drain("MV0")
            def mem_exp(layer, h, bank):
                n = 4 * layer + h
                act.wait_ge(sem("mem_peak"), n + 1)
                if layer and h >= 2:
                    act.wait_ge(sem("mem_out"), n - 1)
                for b in range(TB):
                    c = 2 * h + b
                    last = fn(mem_work(layer, h)[:, b, :], psum[:, bank, T * b:T * b + T], ACT.Exp,
                              bias=peak[:, c:c + 1], accum_out=total[:, c:c + 1])
                last.then_inc(sem("mem_prob"), 1)

            def mem_pt(layer, h, bank):
                act.wait_ge(sem("mem_turned"), 4 * layer + h + 1)
                fn(mem_work(layer, h).rearrange("p m t -> p (m t)"), psum[:, bank, :], ACT.Copy)\
                    .then_inc(sem("mem_pt"), 1)

            for h in range(4):
                mem_exp(0, h, 4 + h)
            for p in range(3):
                act.wait_ge(sem("hg_out"), p + 1)
                fn(sq[:, p, :], psum[:, p, :], ACT.Square).then_inc(sem("squared"), 1)
            for h in range(4):
                mem_pt(0, h, 4 + h)

            def experts(layer):
                base, e0 = AT[f"E{layer}"], 16 * layer
                s = {n: sem(f"{n}{layer}") for n in MOE_SEMS}
                act.wait_ge(ln_done, 4 * layer + 2)
                fn(mt_hi[:].rearrange("p k t -> p (k t)"), x_res[:].rearrange("p b d -> p (b d)"), ACT.Copy)\
                    .then_inc(sem("x_rounded"), 1)
                act.wait_ge(sem("logits_t"), layer + 1)
                fn(logits_t[0:40, :], psum[0:40, 4, 0:T], ACT.Copy).then_inc(sem("logits_copied"), 1)
                act.wait_ge(sem("group_log"), layer + 1)
                fn(rt[:, 40:48], rt[:, 40:48], ACT.Exp).then_inc(sem("group_exp"), 1)
                act.wait_ge(sem("expert_log"), layer + 1)
                fn(rt[:, 104:112], rt[:, 104:112], ACT.Exp).then_inc(sem("expert_exp"), 1)
                act.preload_act_table_set("silu_and_others")
                round_to(base + 3)
                act.wait_ge(sem("placed"), layer + 1)
                load = act.value_load(load_max[0:1, 0:1], min_val=0, max_val=T)

                def gather(i):
                    for r in range(2):
                        act.wait_ge(s["gathered"], i * 2 + (r + 1))
                        fn(xt_hi[:, 4 * r:4 * r + 4, :], slots_x(psum[:, 4 + 2 * r:6 + 2 * r, :]), ACT.Copy)\
                            .then_inc(s["xg_hi"], 1)
                        if r:
                            continue
                        act.wait_ge(s["turned_perm"], i + 1)
                        fn(slot_gate[:].rearrange("p q e -> p (q e)"), psum[:, 7, 0:8], ACT.Copy)
                        fn(perm_t[:].rearrange("p q t -> p (q t)"), psum[:, 6, :], ACT.Copy)\
                            .then_inc(s["perm_out"], 1)

                def group(i, q, dense):
                    nb = TB if dense else 1
                    mark = [3]

                    def rnd(upto):
                        while mark[0] < upto:
                            h = base + mark[0]
                            act.wait_ge(raw_in[h % RING],
                                        of_group(i, q, 32 * (h // RING + 1), 32 * PER_G // RING))
                            act.wait_ge(half_used, of_group(i, q, h - RING + 1, PER_G))
                            fn(w_half(h, w_hi), w_half(h, raw), ACT.Copy).then_inc(hi_split, 1)
                            mark[0] += 1

                    def used_g(n):
                        rnd(n + 1 + AHEAD)
                        act.wait_ge(half_used, of_group(i, q, base + n + 1, PER_G))

                    def gu_bank(j, b):
                        return 4 + 2 * (j % 2) + b if dense else 4 + j % 2

                    def silu(j):
                        used_g(G_AT[j] + 1)
                        if j >= 2:
                            act.wait_ge(sem("h_ready"), of_group(i, q, e0 + j - 1, PER_GROUP))
                        for b in range(nb):
                            last = fn(ex_s[:, j % 2, b, :], psum[:, gu_bank(j, b), 0:256], ACT.Silu)
                        last.then_inc(sem("silu_ready"), 1)

                    def h_round(j):
                        act.wait_ge(sem("h_turned"), of_group(i, q, e0 + j + 1, PER_GROUP))
                        if j >= 2:
                            act.wait_ge(half_used, of_group(i, q, base + D_AT[j - 2] + 1, PER_G))
                        fn(ht_hi[:, j % 2, :, 0:P * nb],
                           psum[:, gu_bank(j, 0), 0:2 * P * nb].rearrange("p (f t) -> p f t", f=2), ACT.Copy)\
                            .then_inc(sem("ht_hi_ready"), 1)

                    silu(0)
                    silu(1)
                    h_round(0)
                    silu(2)
                    h_round(1)
                    silu(3)
                    h_round(2)
                    rnd(12)
                    h_round(3)
                    rnd(PER_G + 2)
                    if not dense:
                        for c in range(2):
                            if c:
                                act.wait_ge(half_used, of_group(i, q, base + 12, PER_G))
                            else:
                                act.wait_ge(s["y_sum"], of_group(i, q, 1, 1))
                            fn(xt_hi[:, 4 * c:4 * c + 4, P * q:P * q + P], y_tile(c), ACT.Copy)\
                                .then_inc(s["y_hi"], 1)
                    rnd(PER_G + 3)

                with act.If(load < FAST_LIMIT + 1):
                    with act.Fori(0, PAIRS) as i:
                        gather(i)
                        for q in range(2):
                            group(i, q, False)
                with act.Else():
                    with act.Fori(0, PAIRS) as i:
                        for q in range(2):
                            group(i, q, True)
                done[0] += GROUPS * PER_G

            split_set(4)
            split_set(5)
            copy_unit("MK1", mem_k[:, 1, :, :].rearrange("p c t -> p (c t)"), 4)
            copy_unit("MV1", mem_v[:, 1, :, :].rearrange("p m c -> p (m c)"), 5)
            round_to(AT["E0"] + 3)
            split_set(6)
            split_set(7)
            experts(0)
            split_set(8)
            split_set(9)

            act.preload_act_table_set("natural_log_exp_and_others")
            copy_unit("B_K0", pair(b_k, 0), 0)
            copy_unit("B_K2", pair(b_k, 2), 2)
            copy_unit("B_V0", mixed[:, 0, 0:512], 0)
            copy_unit("B_Q0", pair(b_q, 0), 3, HD_SCALE)
            copy_unit("B_Q2", pair(b_q, 2), 1, HD_SCALE)
            round_to(AT["B_QM"] + 1 + AHEAD)

            def first(u):
                kind, p = B_UNITS[u]
                if kind == "M":
                    for hh in range(2):
                        mem_exp(1, 2 * p + hh, slot(u) + hh)
                    return
                act.wait_ge(sem("sb_z"), p + 1)
                if p >= 2:
                    act.wait_ge(sem("sb_log"), p - 1)
                v = b_s[:, p % 2, :, :]
                own.link(fn(v, psum[:, slot(u):slot(u) + 2, 0:384], ACT.Abs))
                own.link(fn(v, v, ACT.Exp, scale=-1.0))
                fn(v, v, ACT.Ln, bias=1.0).then_inc(sem("sb_soft"), 1)

            def second(u):
                kind, p = B_UNITS[u]
                if kind == "M":
                    for hh in range(2):
                        mem_pt(1, 2 * p + hh, slot(u) + hh)
                    return
                act.wait_ge(sem("sb_log"), p + 1)
                if p >= 2:
                    act.wait_ge(sem("sb_o"), p - 1)
                fn(b_a[:, p % 2, :, :], psum[:, slot(u):slot(u) + 2, 0:384], ACT.Exp).then_inc(sem("sb_a"), 1)

            def pipeline(n, first, second):
                for u in range(3):
                    first(u)
                for u in range(n):
                    second(u)
                    if u and u + 2 < n:
                        first(u + 2)

            pipeline(len(B_UNITS), first, second)
            split_set(10)
            split_set(11)
            round_to(AT["E1"] + 3)
            split_set(12)
            split_set(13)
            experts(1)
            split_set(14)
            split_set(15)

            act.preload_act_table_set("natural_log_exp_and_others")
            act.wait_ge(sem("f_abs"), 1)
            f2 = ar(4432, 32)
            own.link(fn(f2, f2, ACT.Exp, scale=-1.0))
            fn(f2, f2, ACT.Ln, bias=1.0).then_inc(sem("f_soft2"), 1)
            copy_unit("C_Q0", pair(c_q, 0), 0, HD_SCALE)
            copy_unit("C_Q2", pair(c_q, 2), 2, HD_SCALE)
            copy_unit("C_K0", pair(c_k, 0), 0)
            copy_unit("C_K2", pair(c_k, 2), 2)
            act.wait_ge(sem("c_turned"), 1)
            fn(c_rows[:, 0:P], psum[:, 6, 0:P], ACT.Copy)
            fn(c_rows[:, P:384], psum[:, 6, 0:T], ACT.Copy).then_inc(sem("c_split"), 1)
            copy_unit("C_V0", mixed[:, 0, 0:512], 0)
            copy_unit("C_V1", mixed[:, 0, 512:1024], 2)

            def fox_probs(p):
                act.wait_ge(sem("fox_peak"), p + 1)
                if p >= 2:
                    act.wait_ge(sem("fox_turned"), p - 1)
                for hh in range(2):
                    for b in range(TB):
                        c = 4 * (p % SLOTS) + 2 * hh + b
                        cols = slice(0, P) if b == 0 else slice(P, 384)
                        last = fn(c_p[:, p % 2, hh, cols], psum[:, slot(p) + hh, cols], ACT.Exp,
                                  bias=peak[:, c:c + 1], accum_out=total[:, c:c + 1])
                last.then_inc(sem("fox_p"), 1)

            def fox_pt(p):
                act.wait_ge(sem("fox_turned"), p + 1)
                if p >= 2:
                    act.wait_ge(sem("fox_o"), p - 1)
                fn(c_pt[:, p % 2, :, :], psum[:, slot(p):slot(p) + 2, 0:384], ACT.Copy).then_inc(sem("fox_pt"), 1)

            pipeline(len(C_UNITS), fox_probs, fox_pt)
            split_set(16)
            split_set(17)
            round_to(AT["UP"] + 3)
            split_set(18)
            split_set(19)

            def ff_pair(j, i=None):
                h = AT["UP"] + 2 * j

                def at(n, per):
                    return n if i is None else i * per + n

                if i is None:
                    used(h)
                else:
                    for hh in (h + 3, ):
                        act.wait_ge(raw_in[hh % RING], at(32 * (hh // RING + 1), 32))
                        act.wait_ge(half_used, at(hh - RING + 1, 4))
                        fn(w_half(hh, w_hi), w_half(hh, raw), ACT.Copy).then_inc(hi_split, 1)
                    act.wait_ge(half_used, at(h + 1, 4))
                for c in range(2):
                    k = 2 * j + c
                    w2, bb = ((conv[:, t, k:k + 1] if i is None else conv[:, t, bass.ds(i * 4 + k, 1)])
                              for t in (2, 3))
                    last = fn(ff_t[:, j % 2, T * c:T * c + T], psum[:, 2 * (j % 2), T * c:T * c + T],
                              ACT.Identity, bias=bb, scale=w2)
                last.then_inc(sem("ff_mid"), 1)
                if i is None:
                    used(h + 1)
                else:
                    hh = h + 4
                    act.wait_ge(raw_in[hh % RING], at(32 * (hh // RING + 1), 32))
                    act.wait_ge(half_used, at(hh - RING + 1, 4))
                    fn(w_half(hh, w_hi), w_half(hh, raw), ACT.Copy).then_inc(hi_split, 1)
                act.wait_ge(sem("ff_conv"), at(j + 1, 2))
                fn(ff_g[:, j % 2, :], ff_t[:, j % 2, :], ACT.Gelu).then_inc(sem("ff_gelu"), 1)

            act.preload_act_table_set("gelu_and_others")
            with act.Fori(0, FC // 4) as i:
                for j in range(2):
                    act.wait_ge(sem("ff_free"), i * 2 + (j + 1))
                    ff_pair(j, i)
            done[0] += 20
            act.wait_ge(sem("ff_free"), 11)
            ff_pair(10)

            def row_round(j):
                if j >= 4:
                    act.wait_ge(half_used, AT["DN"] + j - 3)
                q = 2 * (j % 4)
                fn(mt_hi[:, q:q + 2, :].rearrange("p k t -> p (k t)"), ff_a[:, 2 * j:2 * j + 2, :]
                   .rearrange("p k t -> p (k t)"), ACT.Copy).then_inc(sem("fa_hi"), 1)

            act.wait_ge(sem("ff_free"), FC // 2 + 2)
            for j in range(4):
                row_round(j)
            for j in range(FC // 2):
                round_to(AT["DN"] + j + 4)
                if j + 4 < FC // 2:
                    row_round(j + 4)
            act.wait_ge(half_used, AT["PP"])
            split_set(20, n=2)
            for r in range(4):
                act.wait_ge(sem("last_turned"), r + 1)
                fn(xt_hi[:, 2 * r:2 * r + 2, :].rearrange("p k t -> p (k t)"), psum[:, r % 2, :], ACT.Copy)\
                    .then_inc(sem("last_hi"), 1)
            for j in range(2):
                for b in range(TB):
                    n = 2 * j + b
                    if b == 0:
                        round_to(AT["PG"] + 2 * j + 2 + AHEAD)
                    act.wait_ge(sem("pl_sum"), n + 1)
                    fn(pl_s[:, n % 2, :], pl_s[:, n % 2, :], ACT.Sigmoid).then_inc(sem("pl_gate"), 1)

        @block.vector
        def _(dve):
            own = Tally(dve, sem("dve_own"))
            done = [0]

            def split_half(h, up):
                dve.wait_ge(hi_split, up)
                return dve.tensor_tensor(w_half(h, w_lo), w_half(h, raw), w_half(h, w_hi).bitcast(F32),
                                         ALU.subtract).then_inc(lo_split, 1)

            def split_to(upto):
                while done[0] < min(upto, HALVES):
                    h = done[0]
                    if h >= RING:
                        dve.wait_ge(half_used, h - RING + 1)
                    split_half(h, h + 1)
                    done[0] += 1

            def used(h):
                split_to(h + 1 + AHEAD)
                dve.wait_ge(half_used, h + 1)

            def rest(o, whole, hi):
                return dve.tensor_tensor(o, whole, hi.bitcast(F32), ALU.subtract)

            def split_set(s, n=4):
                dve.wait_ge(tr_hi, s + 1)
                if s in (2, 3):
                    hi, lo, c0 = mt_hi, mt_lo, 4 * (s - 2)
                elif s == 20:
                    hi, lo, c0 = mt_hi, mt_lo, 6
                else:
                    hi, lo, c0 = xt_hi, xt_lo, 4 * (s % 2)
                flat = "p k t -> p (k t)"
                rest(lo[:, c0:c0 + n, :].rearrange(flat),
                     psum[:, 4 + 2 * (s % 2):4 + 2 * (s % 2) + n // 2, :].rearrange("p b n -> p (b n)"),
                     hi[:, c0:c0 + n, :].rearrange(flat)).then_inc(tr_lo, 1)

            def copy_unit(name, dst, bank, scale=None):
                used(UNITS[name][0] + UNITS[name][1] - 1)
                src = psum[:, bank, 0:dst.free_size()]
                if scale is None:
                    ins = dve.tensor_copy(dst, src)
                else:
                    ins = dve.tensor_scalar(dst, src, scale, None, ALU.mult)
                ins.then_inc(drained_v, 1)

            def pair(v, p):
                return v[:, 2 * p:2 * p + 2, :].rearrange("p h t -> p (h t)")

            dve.wait_ge(consts, 1)
            dve.tensor_copy(ident_r[:], ident[:])
            dve.tensor_copy(bias_sb_r[:], bias_sb[:])
            dve.tensor_copy(bias_fox_r[:], bias_fox[:]).then_inc(consts_r, 1)
            split_set(0)
            split_set(1)
            split_to(3)
            dve.wait_ge(small_h, 1)
            for n, ((lo, whole), (hi, _)) in enumerate(zip(small_parts(1), small_parts(0))):
                last = rest(lo, whole, hi)
            last.then_inc(small_l, 1)
            dve.tensor_tensor(r_both[0:40, :], ident[0:40, 0:20], ident[0:40, 20:40], ALU.add)
            dve.tensor_tensor(f_both[0:32, :], ident[0:32, 0:16], ident[0:32, 16:32], ALU.add)\
                .then_inc(sem("both_ready"), 1)
            own.link(dve.tensor_tensor(c_pick[:], ident[:, 0:16], ident[:, 32:48], ALU.add))
            dve.tensor_scalar(c_pick[:], c_pick[:].bitcast(F32), -1.0, None, ALU.mult)\
                .then_inc(sem("pick_ready"), 1)

            for j in range(3):
                used(AT["A_F"] + j)
                dve.wait_ge(sem("f_soft"), j + 1)
                lf = pair(hq, j)
                own.link(dve.scalar_tensor_tensor(lf, psum[:, j, :], 0.0, pair(hk, j), ALU.min, ALU.subtract))
                dve.tensor_tensor(pair(hk, j), lf, psum[:, j, :], ALU.subtract).then_inc(drained_v, 1)
                dve.tensor_tensor_scan(pair(hG, j), reset64[:], lf, 0.0, ALU.mult, ALU.add)\
                    .then_inc(sem("g_ready"), 1)
                if j == 0:
                    split_set(2)
                    split_set(3)
            for j in range(3):
                split_to(AT["A_Q"] + j + 1 + AHEAD)
                dve.wait_ge(drained_a, drained_by(f"A_Q{j}", "a"))
                dve.tensor_scalar(pair(hq, j), pair(hq, j), HG_SCALE, None, ALU.mult).then_inc(sem("q_scaled"), 1)

            def chunks(p):
                return hG[:, 2 * p:2 * p + 2, :].rearrange("p h (c t) -> p h c t", t=64)

            def a_logs(st):
                p, i = divmod(st, STEPS)
                if st >= 3:
                    dve.wait_ge(sem("level_done"), st - 2)
                if i > len(LEVELS):
                    return
                x = hX[:, st % 3, :]
                if i == len(LEVELS):
                    xc = x.rearrange("p (h c t) -> p h c t", h=2, t=64)
                    G = chunks(p)
                    end = [G[:, :, c, 63:64].to_broadcast([P, 2, 64]) for c in range(4)]
                    own.did(dve.tensor_tensor(xc[:, :, 0, :], end[0], G[:, :, 0, :], ALU.subtract))
                    own.did(dve.tensor_tensor(xc[:, :, 1, :], end[1], G[:, :, 1, :], ALU.subtract))
                    own.did(dve.tensor_copy(xc[:, :, 2, :], G[:, :, 2, :]))
                    own.did(dve.tensor_tensor(xc[:, :, 3, :], G[:, :, 3, :], end[2], ALU.add))
                    own.settle()
                    dve.tensor_tensor(xc[:, :, 0, :], xc[:, :, 0, :], end[1], ALU.add).then_inc(sem("x_logs"), 1)
                    return
                L = LEVELS[i]
                n = 512 // (2 * L)
                xv = x.rearrange("p (n u t) -> p n u t", u=2, t=L)
                G = pair(hG, p).rearrange("p (n u t) -> p n u t", u=2, t=L)
                anchor = G[:, :, 0, L - 1:L].to_broadcast([P, n, L])
                if L == 64:
                    dve.tensor_copy(xv[:, :, 1, :], G[:, :, 1, :])
                else:
                    dve.tensor_tensor(xv[:, :, 1, :], G[:, :, 1, :], anchor, ALU.subtract)
                dve.tensor_tensor(xv[:, :, 0, :], anchor, G[:, :, 0, :], ALU.subtract).then_inc(sem("x_logs"), 1)

            def a_scale(st):
                p, i = divmod(st, STEPS)
                if i > len(LEVELS):
                    return
                dve.wait_ge(sem("x_exp"), decayed(st))
                dve.wait_ge(sem("k_ready"), p + 1)
                x, q, k = hX[:, st % 3, :], hq[:, 2 * p:2 * p + 2, :], hk[:, 2 * p:2 * p + 2, :]
                if i == len(LEVELS):
                    x3 = x.rearrange("p (h t) -> p h t", h=2)
                    lo, up = slice(0, P), slice(P, T)
                    dve.tensor_tensor(x3[:, :, up], x3[:, :, up], q[:, :, up], ALU.mult)
                    dve.tensor_tensor(x3[:, :, lo], x3[:, :, lo], k[:, :, lo], ALU.mult).then_inc(sem("x_ready"), 1)
                    return
                L = LEVELS[i]
                v = [w.rearrange("p (n u t) -> p n u t", u=2, t=L) for w in (x, pair(hq, p), pair(hk, p))]
                dve.tensor_tensor(v[0][:, :, 1, :], v[0][:, :, 1, :], v[1][:, :, 1, :], ALU.mult)
                dve.tensor_tensor(v[0][:, :, 0, :], v[0][:, :, 0, :], v[2][:, :, 0, :], ALU.mult)\
                    .then_inc(sem("x_ready"), 1)

            def a_merge(st):
                p, i = divmod(st, STEPS)
                dve.wait_ge(sem("level_done"), st + 1)
                bank = psum[:, 4 + st % 4, :]
                if i == len(LEVELS):
                    dve.tensor_copy(pair(hSx, p), bank[:, 0:256]).then_inc(sem("merged"), 1)
                    return
                m = level_mask[:, i if i < len(LEVELS) else len(LEVELS), :]
                dst = hS[:, 4 * p:4 * p + 4, :]
                if st >= 1:
                    dve.wait_ge(sem("merged"), st)
                dve.copy_predicated(dst, m.rearrange("p (o t) -> p o t", o=1).to_broadcast([P, 4, P]),
                                    bank.rearrange("p (c t) -> p c t", c=4)).then_inc(sem("merged"), 1)

            dve.wait_ge(sem("q_scaled"), 3)
            dve.wait_ge(sem("g_ready"), 3)
            dve.wait_ge(consts, 2)
            for n, h in enumerate(A_HALVES):
                for st in range(3 * n, min(3 * n + 3, N_STEPS)):
                    if st == 0:
                        a_logs(0)
                    if st + 1 < N_STEPS:
                        a_logs(st + 1)
                    a_scale(st)
                    if st:
                        a_merge(st - 1)
                if 3 * n < N_STEPS <= 3 * n + 3:
                    a_merge(N_STEPS - 1)
                if h < A_HALVES[-1]:
                    split_to(h + AHEAD)

            def mem_peak(layer, h, bank):
                n = 4 * layer + h
                dve.wait_ge(sem("mem_scores"), n + 1)
                c = slice(2 * h, 2 * h + 2)
                own.link(dve.tensor_reduce(peak[:, c], psum[:, bank, :].rearrange("p (b m) -> p b m", b=2),
                                           AX, ALU.max))
                dve.tensor_scalar(peak[:, c], peak[:, c], -1.0, None, ALU.mult).then_inc(sem("mem_peak"), 1)

            def mem_take(layer, h, bank):
                dve.wait_ge(sem("mem_out"), 4 * layer + h + 1)
                c = slice(2 * h, 2 * h + 2)
                own.link(dve.reciprocal(total[:, c], total[:, c]))
                at = SEQ_W + 64 * h
                return dve.tensor_tensor(mixed[:, :, at:at + 64],
                                         psum[:, bank, 0:128].rearrange("p (b d) -> p b d", b=2),
                                         total[:, c].rearrange("p (b o) -> p b o", o=1).to_broadcast([P, 2, 64]),
                                         ALU.mult)

            for h in range(4):
                mem_peak(0, h, 4 + h)
            split_to(AT["O0"] + AHEAD)
            dve.wait_ge(drained_a, drained_by("A_IG2", "a"))
            dve.wait_ge(gnorm_in, 16)
            dve.tensor_tensor(hg[:], hg[:], gain[:, 0, 0:SEQ_W].rearrange("p (o n) -> p o n", o=1)
                              .to_broadcast([P, TB, SEQ_W]), ALU.mult).then_inc(sem("gate_ready"), 1)
            for p in range(3):
                dve.wait_ge(sem("squared"), p + 1)
                c = slice(4 * p, 4 * p + 4)
                own.link(dve.tensor_reduce(peak[:, 32 + 4 * p:36 + 4 * p],
                                           sq[:, p, :].rearrange("p (c t) -> p c t", c=4), AX, ALU.add))
                dve.tensor_scalar(var_eps[:, c], peak[:, 32 + 4 * p:36 + 4 * p], 1.0 / P, RMS_EPS, ALU.mult, ALU.add)\
                    .then_inc(var_ready, 1)
            dve.wait_ge(sem("gate_ready"), 1)
            dve.wait_ge(sem("hg_out"), 3)
            for p in range(3):
                dve.wait_ge(rstd_ready, p + 1)
                for hh in range(2):
                    h = 2 * p + hh
                    for b in range(TB):
                        c = 2 * hh + b
                        last = dve.scalar_tensor_tensor(mixed[:, b, P * h:P * h + P], psum[:, p, P * c:P * c + P],
                                                        rstd[:, 4 * p + c:4 * p + c + 1], hg[:, b, P * h:P * h + P],
                                                        ALU.mult, ALU.mult)
            last.then_inc(sem("mixed_ready"), 1)

            for h in range(4):
                last = mem_take(0, h, 4 + h)
            last.then_inc(sem("mixed_ready"), 1)

            def norm(n, alpha, ready):
                first = 3 + 2 * n

                def add(b, c):
                    cs = slice(512 * c, 512 * c + 512)
                    own.did(dve.scalar_tensor_tensor(x_res[:, b, cs], x_res[:, b, cs], alpha, psum[:, 2 * c + b, :],
                                                     ALU.mult, ALU.add))

                def measure(b, c):
                    own.did(dve.bn_stats(stats[:, b, c, :], x_res[:, b, 512 * c:512 * c + 512]))

                def gather_stats(b):
                    own.link(dve.bn_aggr(mv[:, b, :], stats[:, b, :, :].rearrange("p c s -> p (c s)")))
                    dve.tensor_scalar(var_eps[:, b:b + 1], mv[:, b, 1:2], LN_EPS, None, ALU.add)\
                        .then_inc(var_ready, 1)

                ready(0)
                add(0, 0)
                add(1, 0)
                own.settle(1)
                measure(0, 0)
                own.settle(1)
                measure(1, 0)
                if n % 2 == 0:
                    dve.nop().then_inc(drained_v, 1)
                ready(1)
                add(0, 1)
                own.settle()
                measure(0, 1)
                add(1, 1)
                own.settle(1)
                gather_stats(0)
                measure(1, 1)
                own.settle()
                if n % 2 == 0:
                    dve.nop().then_inc(drained_v, 1)
                gather_stats(1)
                dve.wait_ge(gain_in, 32 * (n + 1))
                for b in range(TB):
                    x = x_res[:, b, :]
                    own.link(dve.scalar_tensor_tensor(x, x, mv[:, b, 0:1], gain[:, 0, :], ALU.subtract, ALU.mult))
                    dve.wait_ge(rstd_ready, first + b + 1)
                    dve.scalar_tensor_tensor(x, x, rstd[:, b:b + 1], gain[:, 1, :], ALU.mult, ALU.add)\
                        .then_inc(ln_done, 1)

            def projected(layer):
                return lambda c: used(AT[f"O{layer}"] + 2 * c + 1)

            def summed(ready, value):
                return lambda c: dve.wait_ge(ready, value)

            def first_of(o, x, m):
                own.link(dve.tensor_tensor(r_eq.rearrange("p (b e) -> p b e", b=2), x,
                                           m.rearrange("p (b o) -> p b o", o=1).to_broadcast([P, 2, 4]), ALU.is_equal))
                own.link(dve.tensor_tensor_scan(r_cum, reset4[:], r_eq, 0.0, ALU.mult, ALU.add))
                own.link(dve.scalar_tensor_tensor(o.rearrange("p b e -> p (b e)"), r_cum, 1.0, r_eq,
                                                  ALU.is_equal, ALU.mult))

            def wide(v):
                return v.rearrange("p (b o) -> p b o", o=1).to_broadcast([P, 2, 4])

            def place(layer, pair):
                for b in range(TB):
                    for q in range(2):
                        g = bass.ds(pair * 2 + q, 1) if not isinstance(pair, int) else slice(2 * pair + q, 2 * pair + q + 1)
                        last = dve.tensor_scalar(perm[:, b, P * q:P * q + P], slot_no[:], r_pos[:, b, g], r_og[:, b, g],
                                                 ALU.is_equal, ALU.mult)
                last.then_inc(sem(f"perm_ready{layer}"), 1)

            def route(layer):
                dve.wait_ge(sem("x_rounded"), layer + 1)
                rest(mt_lo[:].rearrange("p k t -> p (k t)"), x_res[:].rearrange("p b d -> p (b d)"),
                     mt_hi[:].rearrange("p k t -> p (k t)")).then_inc(sem("x_rest"), 1)
                dve.wait_ge(sem("logits"), layer + 1)
                dve.wait_ge(small_in, 80)
                own.link(dve.tensor_tensor(r_log, psum[:, 4, 0:40].rearrange("p (b e) -> p b e", b=2),
                                           r_bias[:, layer, :].rearrange("p (o e) -> p o e", o=1)
                                           .to_broadcast([P, 2, 20]), ALU.add))
                own.link(dve.tensor_reduce(r_m[:, 0, :], r_log[:, :, 0:4], AX, ALU.max))
                dve.tensor_tensor(r_g, r_log[:, :, 0:4], wide(r_m[:, 0, :]), ALU.subtract)\
                    .then_inc(sem("group_log"), 1)
                dve.wait_ge(sem("group_exp"), layer + 1)
                own.did(dve.tensor_reduce(r_m[:, 1, :], r_g, AX, ALU.max))
                own.link(dve.tensor_reduce(r_m[:, 2, :], r_g, AX, ALU.add))
                own.link(dve.reciprocal(r_m[:, 2, :], r_m[:, 2, :]))
                own.did(dve.tensor_tensor(r_m[:, 3, :], r_m[:, 1, :], r_m[:, 2, :], ALU.mult))
                first_of(r_og, r_g, r_m[:, 1, :])
                dve.nop().then_inc(sem("group_ready"), 1)
                dve.wait_ge(sem("counted"), layer + 1)
                own.link(dve.tensor_copy(r_pos.rearrange("p n g -> p (n g)"), psum[:, 5, 0:12]))
                own.link(dve.tensor_reduce(r_mx, r_pos[:, 2, :], AX, ALU.max))
                own.link(dve.tensor_copy(load_max[:], r_mx))
                dve.nop().then_inc(sem("placed"), 1)
                place(layer, 0)
                own.link(dve.tensor_tensor(
                    r_t16, r_log[:, :, 4:20].rearrange("p b (g e) -> p b g e", g=4),
                    r_og.rearrange("p b (g o) -> p b g o", o=1).to_broadcast([P, 2, 4, 4]), ALU.mult))
                own.link(dve.tensor_reduce(r_i4, r_t16.rearrange("p b g e -> p b e g"), AX, ALU.add))
                own.link(dve.tensor_reduce(r_m[:, 4, :], r_i4, AX, ALU.max))
                dve.tensor_tensor(r_e, r_i4, wide(r_m[:, 4, :]), ALU.subtract).then_inc(sem("expert_log"), 1)
                dve.wait_ge(sem("expert_exp"), layer + 1)
                own.link(dve.tensor_reduce(r_m[:, 5, :], r_e, AX, ALU.max))
                first_of(r_o1, r_e, r_m[:, 5, :])
                own.link(dve.scalar_tensor_tensor(r_e2, r_o1, -2.0, r_e, ALU.mult, ALU.add))
                own.link(dve.tensor_reduce(r_m[:, 6, :], r_e2, AX, ALU.max))
                first_of(r_o2, r_e2, r_m[:, 6, :])
                own.link(dve.tensor_tensor(r_m[:, 7, :], r_m[:, 5, :], r_m[:, 6, :], ALU.add))
                own.link(dve.reciprocal(r_m[:, 7, :], r_m[:, 7, :]))
                own.did(dve.tensor_tensor(r_m[:, 7, :], r_m[:, 7, :], r_m[:, 3, :], ALU.mult))
                own.link(dve.tensor_tensor(r_o1, r_o1, r_o2, ALU.add))
                own.link(dve.tensor_tensor(r_g4, r_e, r_o1, ALU.mult))
                own.link(dve.tensor_tensor(r_g4, r_g4, wide(r_m[:, 7, :]), ALU.mult))
                own.link(dve.tensor_tensor(
                    r_gate, r_g4.rearrange("p b (o e) -> p b o e", o=1).to_broadcast([P, 2, 4, 4]),
                    r_og.rearrange("p b (g o) -> p b g o", o=1).to_broadcast([P, 2, 4, 4]), ALU.mult))
                dve.nop().then_inc(sem("gated"), 1)

            def experts(layer):
                base, e0 = AT[f"E{layer}"], 16 * layer
                s = {n: sem(f"{n}{layer}") for n in MOE_SEMS}
                split_to(base + 3)
                load = dve.value_load(load_max[0:1, 0:1], min_val=0, max_val=T)

                def gather(i):
                    for r in range(2):
                        dve.wait_ge(s["xg_hi"], i * 2 + (r + 1))
                        rest(xt_lo[:, 4 * r:4 * r + 4, :], slots_x(psum[:, 4 + 2 * r:6 + 2 * r, :]),
                             xt_hi[:, 4 * r:4 * r + 4, :]).then_inc(s["xg_lo"], 1)

                def group(i, q, dense):
                    nb = TB if dense else 1
                    mark = [3]

                    def spl(upto):
                        while mark[0] < upto:
                            h = base + mark[0]
                            dve.wait_ge(half_used, of_group(i, q, h - RING + 1, PER_G))
                            split_half(h, of_group(i, q, h + 1, PER_G))
                            mark[0] += 1

                    def used_g(n):
                        spl(n + 1 + AHEAD)
                        dve.wait_ge(half_used, of_group(i, q, base + n + 1, PER_G))

                    def gu_bank(j, b):
                        return 4 + 2 * (j % 2) + b if dense else 4 + j % 2

                    def hidden(j):
                        used_g(G_AT[j] + 1)
                        dve.wait_ge(sem("silu_ready"), of_group(i, q, e0 + j + 1, PER_GROUP))
                        if j >= 2:
                            dve.wait_ge(sem("h_turned"), of_group(i, q, e0 + j - 1, PER_GROUP))
                        for b in range(nb):
                            gate = (r_gate[:, b, bass.ds(i * 2 + q, 1), j:j + 1].rearrange("p a e -> p (a e)")
                                    if dense else slot_gate[:, q, j:j + 1])
                            last = dve.scalar_tensor_tensor(ex_h[:, j % 2, b, :], psum[:, gu_bank(j, b), 256:512],
                                                            gate, ex_s[:, j % 2, b, :], ALU.mult, ALU.mult)
                        last.then_inc(sem("h_ready"), 1)

                    def h_rest(j):
                        dve.wait_ge(sem("ht_hi_ready"), of_group(i, q, e0 + j + 1, PER_GROUP))
                        rest(ht_lo[:, j % 2, :, 0:P * nb],
                             psum[:, gu_bank(j, 0), 0:2 * P * nb].rearrange("p (f t) -> p f t", f=2),
                             ht_hi[:, j % 2, :, 0:P * nb]).then_inc(sem("ht_lo_ready"), 1)

                    hidden(0)
                    hidden(1)
                    h_rest(0)
                    hidden(2)
                    h_rest(1)
                    hidden(3)
                    if q and not dense:
                        place(layer, PAIRS - 1 - i)
                    h_rest(2)
                    spl(12)
                    h_rest(3)
                    spl(PER_G + 2)
                    if not dense:
                        for c in range(2):
                            dve.wait_ge(s["y_hi"], of_group(i, q, c + 1, 2))
                            rest(xt_lo[:, 4 * c:4 * c + 4, P * q:P * q + P], y_tile(c),
                                 xt_hi[:, 4 * c:4 * c + 4, P * q:P * q + P]).then_inc(s["y_lo"], 1)
                    spl(PER_G + 3)

                with dve.If(load < FAST_LIMIT + 1):
                    with dve.Fori(0, PAIRS) as i:
                        gather(i)
                        for q in range(2):
                            group(i, q, False)
                with dve.Else():
                    with dve.Fori(0, PAIRS) as i:
                        for q in range(2):
                            group(i, q, True)
                done[0] += GROUPS * PER_G

            split_set(4)
            split_set(5)
            norm(0, ALPHA, projected(0))
            split_set(6)
            split_set(7)
            route(0)
            experts(0)
            norm(1, ALPHA, summed(sem("moe_done"), 1))
            split_set(8)
            split_set(9)

            copy_unit("B_K1", pair(b_k, 1), 1)
            copy_unit("B_V0", mixed[:, 1, 0:512], 1)
            used(UNITS["B_V1"][0])
            dve.tensor_copy(mixed[:, :, 512:768], psum[:, 2, :].rearrange("p (b n) -> p b n", b=2))\
                .then_inc(drained_v, 1)
            copy_unit("B_Q1", pair(b_q, 1), 0, HD_SCALE)
            copy_unit("B_QM", b_qm[:].rearrange("p c t -> p (c t)"), 2, HD_SCALE)

            def maxima(u):
                kind, p = B_UNITS[u]
                if kind == "M":
                    for hh in range(2):
                        mem_peak(1, 2 * p + hh, slot(u) + hh)

            def softplus(u):
                kind, p = B_UNITS[u]
                if kind == "M":
                    return
                dve.wait_ge(sem("sb_soft"), p + 1)
                dve.scalar_tensor_tensor(b_s[:, p % 2, :, :], psum[:, slot(u):slot(u) + 2, 0:384], 0.0,
                                         b_s[:, p % 2, :, :], ALU.max, ALU.add).then_inc(sem("sb_sp"), 1)

            def take(u):
                kind, p = B_UNITS[u]
                if kind == "M":
                    for hh in range(2):
                        last = mem_take(1, 2 * p + hh, slot(u) + hh)
                else:
                    dve.wait_ge(sem("sb_o"), p + 1)
                    last = dve.tensor_copy(mixed[:, :, P * p:P * p + P].rearrange("p b (h d) -> p h b d", h=2),
                                           psum[:, slot(u):slot(u) + 2, 384:512]
                                           .rearrange("p h (b d) -> p h b d", b=2))
                last.then_inc(sem("b_taken"), 1)

            for u in range(3):
                maxima(u)
            softplus(0)
            for u in range(len(B_UNITS)):
                if u + 1 < len(B_UNITS):
                    softplus(u + 1)
                if u:
                    take(u - 1)
                    if u + 2 < len(B_UNITS):
                        maxima(u + 2)
            take(len(B_UNITS) - 1)
            dve.wait_ge(sem("b_taken"), len(B_UNITS))
            dve.nop().then_inc(sem("mixed_ready"), 2)
            split_set(10)
            split_set(11)
            norm(2, ALPHA, projected(1))
            split_set(12)
            split_set(13)
            route(1)
            experts(1)
            norm(3, ALPHA, summed(sem("moe_done"), 2))
            split_set(14)
            split_set(15)

            f1, f2 = ar(4400, 32), ar(4432, 32)
            dve.wait_ge(sem("logits_t"), 3)
            dve.tensor_copy(logits_t[0:32, :], psum[0:32, 4, 0:T]).then_inc(sem("logits_copied"), 1)
            dve.wait_ge(sem("logits"), 3)
            own.link(dve.tensor_tensor(f1.rearrange("p (b h) -> p b h", b=2),
                                       psum[:, 4, 0:32].rearrange("p (b h) -> p b h", b=2),
                                       f_bias[:].rearrange("p (o h) -> p o h", o=1).to_broadcast([P, 2, 16]), ALU.add))
            dve.scalar_tensor_tensor(f2, f1, -1.0, f1, ALU.mult, ALU.max).then_inc(sem("f_abs"), 1)
            dve.wait_ge(sem("f_soft2"), 1)
            dve.scalar_tensor_tensor(c_f.rearrange("p b h -> p (b h)"), f1, 0.0, f2, ALU.min, ALU.subtract)\
                .then_inc(sem("f_log"), 1)
            copy_unit("C_Q1", pair(c_q, 1), 1, HD_SCALE)
            copy_unit("C_Q3", pair(c_q, 3), 3, HD_SCALE)
            dve.wait_ge(sem("c_sum"), 1)
            sums = psum[:, 5, 0:32].rearrange("p (b h) -> p b h", b=2)
            own.link(dve.memset(c_c, 0.0))
            dve.tensor_copy(c_c[:, :, 0:16], sums)
            dve.tensor_copy(c_c[:, :, 32:48], sums).then_inc(sem("c_out"), 1)
            copy_unit("C_K1", pair(c_k, 1), 1)
            copy_unit("C_K3", pair(c_k, 3), 3)
            dve.wait_ge(sem("c_split"), 1)
            rest(c_rows[32:48, 0:P], psum[32:48, 6, 0:P], c_rows[32:48, 0:P])
            rest(c_rows[32:48, P:384], psum[32:48, 6, 0:T], c_rows[32:48, P:384]).then_inc(sem("c_split"), 1)
            copy_unit("C_V0", mixed[:, 1, 0:512], 1)
            copy_unit("C_V1", mixed[:, 1, 512:1024], 3)

            def fox_peak(p):
                dve.wait_ge(sem("fox_s"), p + 1)
                sc = psum[:, slot(p):slot(p) + 2, :]
                c = 4 * (p % SLOTS)
                pk = peak[:, c:c + 4].rearrange("p (h b) -> p h b", b=2)
                own.did(dve.tensor_reduce(pk[:, :, 0:1], sc[:, :, 0:P], AX, ALU.max))
                own.did(dve.tensor_reduce(pk[:, :, 1:2], sc[:, :, P:384], AX, ALU.max))
                own.settle()
                dve.tensor_scalar(peak[:, c:c + 4], peak[:, c:c + 4], -1.0, None, ALU.mult)\
                    .then_inc(sem("fox_peak"), 1)

            def fox_take(p):
                c = 4 * (p % SLOTS)
                dve.wait_ge(sem("fox_o"), p + 1)
                own.link(dve.reciprocal(peak[:, 16 + c:20 + c], total[:, c:c + 4]))
                for hh in range(2):
                    inv = peak[:, 16 + c + 2 * hh:18 + c + 2 * hh]
                    h = 2 * p + hh
                    last = dve.tensor_tensor(mixed[:, :, 64 * h:64 * h + 64],
                                             psum[:, slot(p) + hh, 384:512].rearrange("p (b d) -> p b d", b=2),
                                             inv.rearrange("p (b o) -> p b o", o=1).to_broadcast([P, 2, 64]),
                                             ALU.mult)
                last.then_inc(sem("fox_o_out"), 1)

            for p in range(3):
                fox_peak(p)
            for p in range(1, 8):
                fox_take(p - 1)
                if p + 2 < 8:
                    fox_peak(p + 2)
            fox_take(7)
            dve.wait_ge(sem("fox_o_out"), 8)
            dve.nop().then_inc(sem("mixed_ready"), 2)
            split_set(16)
            split_set(17)
            norm(4, ALPHA_2, projected(2))
            split_set(18)
            split_set(19)
            split_to(AT["UP"] + 3)

            def ff_pair(j, i=None):
                h = AT["UP"] + 2 * j

                def at(n, per):
                    return n if i is None else i * per + n

                if i is None:
                    split_to(h + 1 + AHEAD)
                else:
                    hh = h + 3
                    dve.wait_ge(half_used, at(hh - RING + 1, 4))
                    split_half(hh, at(hh + 1, 4))
                dve.wait_ge(sem("ff_mid"), at(j + 1, 2))
                for lag, tap in ((1, 1), (2, 0)):
                    for c in range(2):
                        k = 2 * j + c
                        w = conv[:, tap, k:k + 1] if i is None else conv[:, tap, bass.ds(i * 4 + k, 1)]
                        o = ff_t[:, j % 2, T * c + lag:T * c + T]
                        last = dve.scalar_tensor_tensor(o, psum[:, 2 * (j % 2), T * c:T * c + T - lag], w, o,
                                                        ALU.mult, ALU.add)
                        if lag == 1:
                            loop_own.did(last)
                    if lag == 1:
                        loop_own.settle()
                last.then_inc(sem("ff_conv"), 1)
                if i is None:
                    split_to(h + 2 + AHEAD)
                    dve.wait_ge(half_used, h + 2)
                else:
                    hh = h + 4
                    dve.wait_ge(half_used, at(hh - RING + 1, 4))
                    split_half(hh, at(hh + 1, 4))
                    dve.wait_ge(half_used, at(h + 2, 4))
                dve.wait_ge(sem("ff_gelu"), at(j + 1, 2))
                fa = ff_a[:, 2 * j:2 * j + 2, :] if i is None else ff_a[:, bass.ds(i * 4 + 2 * j, 2), :]
                dve.tensor_tensor(fa.rearrange("p k t -> p (k t)"), ff_g[:, j % 2, :], psum[:, 2 * (j % 2) + 1, :],
                                  ALU.mult).then_inc(sem("ff_free"), 1)

            loop_own = Tally(dve, sem("conv_own"))
            dve.nop().then_inc(sem("ff_free"), 2)
            with dve.Fori(0, FC // 4) as i:
                loop_own.enter(i, 4)
                for j in range(2):
                    ff_pair(j, i)
            loop_own.leave(FC // 4)
            done[0] += 20
            ff_pair(10)
            dve.wait_ge(sem("ff_free"), FC // 2 + 2)

            def row_rest(j):
                dve.wait_ge(sem("fa_hi"), j + 1)
                q = 2 * (j % 4)
                rest(mt_lo[:, q:q + 2, :].rearrange("p k t -> p (k t)"),
                     ff_a[:, 2 * j:2 * j + 2, :].rearrange("p k t -> p (k t)"),
                     mt_hi[:, q:q + 2, :].rearrange("p k t -> p (k t)")).then_inc(sem("fa_lo"), 1)

            for j in range(4):
                row_rest(j)
            for j in range(FC // 2):
                split_to(AT["DN"] + j + 4)
                if j + 4 < FC // 2:
                    row_rest(j + 4)
            split_set(20, n=2)
            split_to(AT["PP"] + 1)
            norm(5, ALPHA_2, summed(half_used, AT["DN"] + 11))
            for r in range(4):
                dve.wait_ge(sem("last_hi"), r + 1)
                rest(xt_lo[:, 2 * r:2 * r + 2, :].rearrange("p k t -> p (k t)"), psum[:, r % 2, :],
                     xt_hi[:, 2 * r:2 * r + 2, :].rearrange("p k t -> p (k t)")).then_inc(sem("last_lo"), 1)
            dve.wait_ge(gain_in, 32 * 6 + 16)
            for j in range(2):
                used(AT["PG"] + 2 * j + 1)
                for b in range(TB):
                    n = 2 * j + b
                    cs = slice(512 * j, 512 * j + 512)
                    dve.tensor_tensor(pl_s[:, n % 2, :], psum[:, 2 * j + b, :], gain[:, 0, cs], ALU.add)\
                        .then_inc(sem("pl_sum"), 1)
                for b in range(TB):
                    n = 2 * j + b
                    cs = slice(512 * j, 512 * j + 512)
                    dve.wait_ge(sem("pl_gate"), n + 1)
                    own.link(dve.tensor_tensor(pl_s[:, n % 2, :], pl_s[:, n % 2, :], psum[:, 4 + 2 * j + b, :], ALU.mult))
                    own.link(dve.tensor_tensor(x_res[:, b, cs], x_res[:, b, cs], pl_s[:, n % 2, :], ALU.add))
            dve.nop().then_inc(sem("result"), TB)


_FULL = ["x", "mem", "a_w_in", "a_gnorm", "b_w_in", "w_kv_shared", "w_mem_kv", "w_o", "ln_mix_g", "ln_mix_b",
         "ln_ffn_g", "ln_ffn_b", "w_gate", "w_up", "w_down", "p_2", "attn_w_in_2", "attn_b_f_2", "attn_w_out_2",
         "ln_mix_g_2", "ln_mix_b_2", "ffn_w_up_2", "ffn_w_down_2", "ln_ffn_g_2", "ln_ffn_b_2", "ple_w_proj_2",
         "ple_w_gate_2", "ple_b_gate_2"]


def kernel(**inputs):
    import numpy as np
    import concourse.bacc as bacc
    from concourse import mybir as mb
    from concourse.bass_utils import run_bass_kernel_spmd

    arrays = {n: np.ascontiguousarray(inputs[n]) for n in _FULL}

    def by_row(w):
        n = w.shape[-1]
        return np.ascontiguousarray(np.asarray(w).reshape(8, 128, n).transpose(1, 0, 2).reshape(128, 8 * n))

    router = [np.concatenate([np.asarray(inputs["w_group"][l]), np.asarray(inputs["w_router"][l])], axis=1)
              for l in range(2)]
    arrays["r_weights"] = np.ascontiguousarray(np.stack([by_row(r) for r in router], axis=1))
    arrays["r_bias"] = np.concatenate([np.asarray(inputs["b_group"]), np.asarray(inputs["b_router"])], axis=1)
    arrays["f_weights"] = by_row(np.asarray(inputs["attn_w_in_2"])[0][:, 3 * 1024:])
    taps = np.concatenate([np.asarray(inputs["ffn_conv_w_2"])[0], np.asarray(inputs["ffn_conv_b_2"])], axis=0)
    arrays["conv"] = np.ascontiguousarray(taps.reshape(4, 22, 128).transpose(2, 0, 1))

    nc = bacc.Bacc("TRN2", target_bir_lowering=False, num_devices=1, dynamic_dma_scratch_size=1024)
    a, named = {}, {}
    for name, v in arrays.items():
        named[f"in_{name}"] = v
        a[name] = nc.dram_tensor(f"in_{name}", v.shape, mb.dt.from_np(v.dtype), kind="ExternalInput").ap()
    out = nc.dram_tensor("out_0", (1, 256, 1024), mb.dt.from_np(np.dtype("float32")), kind="ExternalOutput").ap()
    build(nc, a, out)
    r = run_bass_kernel_spmd(nc, [named], core_ids=[0])
    return r.results[0]["out_0"]
```
